# Optimizing a Trainium2 kernel written in Bass

```python
import jax, jax.numpy as jnp
from jax import lax
import numpy as np
import math

D_MODEL = 1024
BATCH = 1
SEQ = 512
DEPTH = 2

CHUNK = 64
N_META = 16
N_EVEN = (DEPTH + 1) // 2
N_ODD = DEPTH // 2
EPS = 1e-6
D_FF = 4 * D_MODEL

HG_HEADS = 4
HG_K = 128
HG_V = (D_MODEL // 2) // HG_HEADS
HG_KW = HG_HEADS * HG_K
HG_VW = HG_HEADS * HG_V

MLA_HEADS = 4
NOPE = 128
ROPE = 64
V_DIM = (D_MODEL // 2) // MLA_HEADS
QK_DIM = NOPE + ROPE
Q_RANK = 256
KV_RANK = 256
ROPE_THETA = 10000.0
Q_BLOCK = 128

IN_SPLITS = (HG_KW, 2 * HG_KW, 2 * HG_KW + HG_VW, 2 * HG_KW + 2 * HG_VW,
             2 * HG_KW + 2 * HG_VW + Q_RANK, 2 * HG_KW + 2 * HG_VW + Q_RANK + KV_RANK)
IN_COLS = 2 * HG_KW + 2 * HG_VW + Q_RANK + KV_RANK + ROPE

POOL_WINDOWS = (2, 4, 8, 16)
POOL_GROUPS = len(POOL_WINDOWS)
POOL_G = D_MODEL // POOL_GROUPS


def rmsnorm(x, g):
    xf = x.astype(jnp.float32)
    y = xf * lax.rsqrt(jnp.mean(xf * xf, axis=-1, keepdims=True) + EPS)
    return (y * g.astype(jnp.float32)).astype(x.dtype)

def chunk_ids(L):
    p = jnp.arange(L)
    return jnp.where(p < N_META, 0, 1 + (p - N_META) // CHUNK)

def rope_tables(L):
    half = ROPE // 2
    inv = ROPE_THETA ** (-jnp.arange(half, dtype=jnp.float32) / half)
    ang = jnp.arange(L, dtype=jnp.float32)[:, None] * inv[None, :]
    return jnp.cos(ang), jnp.sin(ang)

def rope_tail(x, cos, sin):
    xn, xr = x[..., :NOPE], x[..., NOPE:]
    x1, x2 = xr[..., :ROPE // 2], xr[..., ROPE // 2:]
    c = cos[None, :, None, :].astype(x.dtype)
    s = sin[None, :, None, :].astype(x.dtype)
    return jnp.concatenate([xn, x1 * c - x2 * s, x2 * c + x1 * s], axis=-1)

def hgrn2_chunk_scan(q, k, v, log_f):
    B, L, H, K = q.shape
    lead = CHUNK - N_META
    tail = (-(L + lead)) % CHUNK
    nc = (L + lead + tail) // CHUNK

    def to_chunks(a):
        a = jnp.pad(a.astype(jnp.float32), ((0, 0), (lead, tail), (0, 0), (0, 0)))
        return a.reshape(B, nc, CHUNK, H, a.shape[-1]).transpose(1, 0, 3, 2, 4)

    qc, kc, vc, gc = to_chunks(q), to_chunks(k), to_chunks(v), to_chunks(log_f)
    tri = jnp.tril(jnp.ones((CHUNK, CHUNK), dtype=bool))[:, :, None]

    def step(S, inp):
        qi, ki, vi, gi = inp
        b = jnp.cumsum(gi, axis=2)
        o_inter = jnp.einsum('bhtk,bhkv->bhtv', qi * jnp.exp(b), S)
        diff = b[:, :, :, None, :] - b[:, :, None, :, :]
        dec = jnp.exp(jnp.where(tri, diff, -jnp.inf))
        att = jnp.einsum('bhtk,bhtsk,bhsk->bhts', qi, dec, ki)
        o_intra = jnp.einsum('bhts,bhsv->bhtv', att, vi)
        b_last = b[:, :, -1:, :]
        S_new = jnp.exp(b_last[:, :, 0, :])[..., None] * S + jnp.einsum(
            'bhsk,bhsv->bhkv', ki * jnp.exp(b_last - b), vi)
        return S_new, o_inter + o_intra

    S0 = jnp.zeros((B, H, K, v.shape[-1]), jnp.float32)
    _, o = lax.scan(step, S0, (qc, kc, vc, gc))
    o = o.transpose(1, 0, 3, 2, 4).reshape(B, nc * CHUNK, H, -1)
    return o[:, lead:lead + L]

def hgrn2_mixer(hq, hf, hi, hg, lb, out_gain):
    B, L, _ = hq.shape
    lb = lb.astype(jnp.float32)
    log_f = jnp.logaddexp(jnp.log(lb), jnp.log1p(-lb) + jax.nn.log_sigmoid(hf.astype(jnp.float32)))
    k = -jnp.expm1(log_f)
    q = jax.nn.silu(hq.astype(jnp.float32))
    o = hgrn2_chunk_scan(q.reshape(B, L, HG_HEADS, HG_K), k.reshape(B, L, HG_HEADS, HG_K),
                         hi.reshape(B, L, HG_HEADS, HG_V), log_f.reshape(B, L, HG_HEADS, HG_K))
    o = rmsnorm(o, out_gain) * jax.nn.silu(hg.reshape(B, L, HG_HEADS, HG_V).astype(jnp.float32))
    return o.reshape(B, L, HG_VW).astype(hq.dtype)

def block_causal_attention(q, k, v, cid):
    B, L, H, Dq = q.shape
    nq = -(-L // Q_BLOCK)
    pad = nq * Q_BLOCK - L
    qp = jnp.pad(q, ((0, 0), (0, pad), (0, 0), (0, 0)))
    qb = qp.reshape(B, nq, Q_BLOCK, H, Dq).transpose(1, 0, 2, 3, 4)
    qcid = jnp.pad(cid, (0, pad), constant_values=L).reshape(nq, Q_BLOCK)
    scale = Dq ** -0.5

    def one_block(args):
        qblk, qc = args
        s = jnp.einsum('bqhd,bkhd->bhqk', qblk, k).astype(jnp.float32) * scale
        mask = cid[None, :] <= qc[:, None]
        p = jax.nn.softmax(jnp.where(mask, s, -jnp.inf), axis=-1).astype(v.dtype)
        return jnp.einsum('bhqk,bkhd->bqhd', p, v)

    out = lax.map(one_block, (qb, qcid))
    out = out.transpose(1, 0, 2, 3, 4).reshape(B, nq * Q_BLOCK, H, v.shape[-1])
    return out[:, :L]

def mla_mixer(cq, ckv, kr, qa_g, kva_g, w_q_up, w_kv_up, qn_g, kn_g, cos, sin, cid):
    B, L, _ = cq.shape
    q = jnp.einsum('blr,re->ble', rmsnorm(cq, qa_g), w_q_up).reshape(B, L, MLA_HEADS, QK_DIM)
    kv = jnp.einsum('blr,re->ble', rmsnorm(ckv, kva_g), w_kv_up).reshape(B, L, MLA_HEADS, NOPE + V_DIM)
    k_nope, v = kv[..., :NOPE], kv[..., NOPE:]
    k = jnp.concatenate([k_nope, jnp.broadcast_to(kr[:, :, None, :], (B, L, MLA_HEADS, ROPE))], axis=-1)
    q = rope_tail(rmsnorm(q, qn_g), cos, sin)
    k = rope_tail(rmsnorm(k, kn_g), cos, sin)
    o = block_causal_attention(q, k, v, cid)
    return o.reshape(B, L, MLA_HEADS * V_DIM)

def multiscale_pool(h, w_groups, scale):
    B, L, D = h.shape
    hf = h.astype(jnp.float32).reshape(B, L, POOL_GROUPS, POOL_G)
    t = jnp.arange(L, dtype=jnp.float32)
    diffs = []
    for gi, w in enumerate(POOL_WINDOWS):
        c = jnp.pad(jnp.cumsum(hf[:, :, gi], axis=1), ((0, 0), (w, 0), (0, 0)))
        win = c[:, w:] - c[:, :L]
        cnt = jnp.minimum(t + 1.0, float(w))[None, :, None]
        diffs.append(win / cnt - hf[:, :, gi])
    d = jnp.stack(diffs, axis=2).astype(h.dtype)
    y = jnp.einsum('blgc,gce->blge', d, w_groups).reshape(B, L, D)
    return y * scale

def squared_relu_mlp(h, w_up, w_down):
    a = jax.nn.relu(jnp.einsum('bld,df->blf', h, w_up))
    return jnp.einsum('blf,fd->bld', a * a, w_down)

def first_inputs(seed: int = 0) -> dict:
    key = jax.random.key(seed)
    ks = jax.random.split(key, 20)
    n = jax.random.normal
    f32 = jnp.float32
    return {
        'x': n(ks[0], (BATCH, SEQ, D_MODEL), f32),
        'meta_tokens': n(ks[1], (N_META, D_MODEL), f32),
        'mix_norm': 1.0 + 0.02 * n(ks[2], (DEPTH, D_MODEL), f32),
        'mlp_norm': 1.0 + 0.02 * n(ks[3], (DEPTH, D_MODEL), f32),
        'w_mlp_up': n(ks[4], (DEPTH, D_MODEL, D_FF), f32) * D_MODEL ** -0.5,
        'w_mlp_down': n(ks[5], (DEPTH, D_FF, D_MODEL), f32) * (0.5 * D_FF ** -0.5),
        'w_in': n(ks[6], (N_EVEN, D_MODEL, IN_COLS), f32) * D_MODEL ** -0.5,
        'hgrn_lb': 0.5 * n(ks[7], (N_EVEN, HG_KW), f32),
        'hgrn_out_norm': 1.0 + 0.02 * n(ks[8], (N_EVEN, HG_V), f32),
        'mla_q_a_norm': 1.0 + 0.02 * n(ks[9], (N_EVEN, Q_RANK), f32),
        'mla_kv_a_norm': 1.0 + 0.02 * n(ks[10], (N_EVEN, KV_RANK), f32),
        'w_q_up': n(ks[11], (N_EVEN, Q_RANK, MLA_HEADS * QK_DIM), f32) * Q_RANK ** -0.5,
        'w_kv_up': n(ks[12], (N_EVEN, KV_RANK, MLA_HEADS * (NOPE + V_DIM)), f32) * KV_RANK ** -0.5,
        'q_norm': 1.0 + 0.02 * n(ks[13], (N_EVEN, QK_DIM), f32),
        'k_norm': 1.0 + 0.02 * n(ks[14], (N_EVEN, QK_DIM), f32),
        'w_out': n(ks[15], (N_EVEN, HG_VW + MLA_HEADS * V_DIM, D_MODEL), f32) * D_MODEL ** -0.5,
        'pool_w': n(ks[16], (N_ODD, POOL_GROUPS, POOL_G, POOL_G), f32) * POOL_G ** -0.5,
        'pool_scale': 1.0 + 0.1 * n(ks[17], (N_ODD, D_MODEL), f32),
    }

def first_block(x, meta_tokens, mix_norm, mlp_norm, w_mlp_up, w_mlp_down, w_in, hgrn_lb,
              hgrn_out_norm, mla_q_a_norm, mla_kv_a_norm, w_q_up, w_kv_up, q_norm, k_norm,
              w_out, pool_w, pool_scale):
    B = x.shape[0]
    meta = jnp.broadcast_to(meta_tokens[None].astype(x.dtype), (B, N_META, D_MODEL))
    h = jnp.concatenate([meta, x], axis=1)
    L = h.shape[1]
    cid = chunk_ids(L)
    cos, sin = rope_tables(L)
    lb_cum = jnp.cumsum(jax.nn.softmax(hgrn_lb.astype(jnp.float32), axis=0), axis=0)
    lower_bounds = lb_cum - lb_cum[0:1]

    for layer in range(DEPTH):
        u = rmsnorm(h, mix_norm[layer])
        if layer % 2 == 0:
            e = layer // 2
            z = jnp.einsum('bld,de->ble', u, w_in[e])
            hq, hf, hi, hg, cq, ckv, kr = jnp.split(z, IN_SPLITS, axis=-1)
            o_a = hgrn2_mixer(hq, hf, hi, hg, lower_bounds[e], hgrn_out_norm[e])
            o_b = mla_mixer(cq, ckv, kr, mla_q_a_norm[e], mla_kv_a_norm[e], w_q_up[e], w_kv_up[e],
                            q_norm[e], k_norm[e], cos, sin, cid)
            mix = jnp.einsum('ble,ed->bld', jnp.concatenate([o_a, o_b], axis=-1), w_out[e])
        else:
            o = layer // 2
            mix = multiscale_pool(u, pool_w[o], pool_scale[o])
        h = h + mix
        h = h + squared_relu_mlp(rmsnorm(h, mlp_norm[layer]), w_mlp_up[layer], w_mlp_down[layer])

    return h[:, N_META:]


DEPTH_2 = 1

N_MEM = 256
N_MIXERS = 3
MIXER_W = D_MODEL
GDN_DK = 128
GDN_DV = 128
GDN_HEADS = MIXER_W // GDN_DV
GDN_KW = GDN_HEADS * GDN_DK
GDN_VW = GDN_HEADS * GDN_DV
GDN_QKV = 2 * GDN_KW + GDN_VW
CONV_K = 4
ML_DQK = 64
ML_DV = 128
ML_HEADS = MIXER_W // ML_DV
ML_KW = ML_HEADS * ML_DQK
ML_VW = ML_HEADS * ML_DV
SB_DH = 64
SB_HEADS = MIXER_W // SB_DH
SB_W = SB_HEADS * SB_DH
SB_BLOCK = 128
MEM_HEADS = 4
MEM_DH = 128
MEM_W = MEM_HEADS * MEM_DH
MIX_W = MIXER_W + MEM_W
GDN_IN = GDN_QKV + GDN_VW + 2 * GDN_HEADS + MEM_W
ML_IN = 2 * ML_KW + 2 * ML_VW + 2 * ML_HEADS + MEM_W
SB_IN = 3 * SB_W + MEM_W
D_FF_2 = -(-8 * D_MODEL // (3 * 256)) * 256
N_GDN = (DEPTH_2 + 2) // N_MIXERS
N_ML = (DEPTH_2 + 1) // N_MIXERS
N_SB = DEPTH_2 // N_MIXERS


def rms_norm(x, g):
    xf = x.astype(jnp.float32)
    y = xf * lax.rsqrt(jnp.mean(xf * xf, axis=-1, keepdims=True) + EPS)
    return (y * g.astype(jnp.float32)).astype(x.dtype)

def l2norm(x):
    return x * lax.rsqrt(jnp.sum(x * x, axis=-1, keepdims=True) + EPS)

def split_heads(t, n):
    b, s, _ = t.shape
    return t.reshape(b, s, n, -1).transpose(0, 2, 1, 3)

def merge_heads(t):
    b, h, s, d = t.shape
    return t.transpose(0, 2, 1, 3).reshape(b, s, h * d)

def to_chunks(t):
    b, h, s = t.shape[:3]
    return t.reshape(b, h, s // CHUNK, CHUNK, *t.shape[3:])

def causal_dwconv(x, w):
    k, c = w.shape
    return lax.conv_general_dilated(x, w[:, None, :].astype(x.dtype), window_strides=(1,),
                                    padding=[(k - 1, 0)], dimension_numbers=("NWC", "WIO", "NWC"),
                                    feature_group_count=c)

def gated_delta_rule(q, k, v, a, b, a_log, dt_bias):
    f32 = jnp.float32
    q, k, v, a, b = (t.astype(f32) for t in (q, k, v, a, b))
    q = l2norm(q) * GDN_DK ** -0.5
    k = l2norm(k)
    beta = jax.nn.sigmoid(b)
    g = -jnp.exp(a_log.astype(f32))[None, :, None] * jax.nn.softplus(a + dt_bias.astype(f32)[None, :, None])
    qc, kc, vc, bc, gc = (to_chunks(t) for t in (q, k, v, beta, g))
    G = jnp.cumsum(gc, axis=-1)
    incl = jnp.tril(jnp.ones((CHUNK, CHUNK), dtype=bool))
    strict = jnp.tril(jnp.ones((CHUNK, CHUNK), dtype=bool), -1)
    diff = G[..., :, None] - G[..., None, :]
    decay = jnp.where(incl, jnp.exp(jnp.where(incl, diff, 0.0)), 0.0)
    kk = jnp.einsum("bhnid,bhnjd->bhnij", kc, kc)
    lower = jnp.where(strict, bc[..., :, None] * kk * decay, 0.0)
    rhs = jnp.concatenate([vc * bc[..., None], kc * (bc * jnp.exp(G))[..., None]], axis=-1)
    sol = lax.linalg.triangular_solve(lower + jnp.eye(CHUNK, dtype=f32), rhs, left_side=True,
                                      lower=True, unit_diagonal=True)
    u, w = sol[..., :GDN_DV], sol[..., GDN_DV:]
    p = jnp.einsum("bhnid,bhnjd->bhnij", qc, kc) * decay
    qg = qc * jnp.exp(G)[..., None]
    kg = kc * jnp.exp(G[..., -1:] - G)[..., None]
    gl = jnp.exp(G[..., -1])

    def step(state, xs):
        u_n, w_n, qg_n, kg_n, p_n, gl_n = xs
        v_new = u_n - jnp.einsum("bhcd,bhde->bhce", w_n, state)
        o_n = jnp.einsum("bhcd,bhde->bhce", qg_n, state) + jnp.einsum("bhij,bhje->bhie", p_n, v_new)
        state = state * gl_n[..., None, None] + jnp.einsum("bhcd,bhce->bhde", kg_n, v_new)
        return state, o_n

    bn, hn = q.shape[:2]
    s0 = jnp.zeros((bn, hn, GDN_DK, GDN_DV), f32)
    xs = tuple(jnp.moveaxis(t, 2, 0) for t in (u, w, qg, kg, p, gl))
    _, o = lax.scan(step, s0, xs)
    return jnp.moveaxis(o, 0, 2).reshape(bn, hn, -1, GDN_DV)

def mlstm_cell(q, k, v, i_pre, f_pre):
    f32 = jnp.float32
    q, k, v, i_pre, f_pre = (t.astype(f32) for t in (q, k, v, i_pre, f_pre))
    k = k * ML_DQK ** -0.5
    lf = jax.nn.log_sigmoid(f_pre)
    qc, kc, vc, lic, lfc = (to_chunks(t) for t in (q, k, v, i_pre, lf))
    bcum = jnp.cumsum(lfc, axis=-1)
    incl = jnp.tril(jnp.ones((CHUNK, CHUNK), dtype=bool))
    dmat = jnp.where(incl, bcum[..., :, None] - bcum[..., None, :] + lic[..., None, :], -jnp.inf)
    m_intra = jnp.max(dmat, axis=-1)
    sqk = jnp.einsum("bhnid,bhnjd->bhnij", qc, kc) * jnp.exp(dmat - m_intra[..., None])
    num_intra = jnp.einsum("bhnij,bhnje->bhnie", sqk, vc)
    den_intra = jnp.sum(sqk, axis=-1)
    bl = bcum[..., -1]
    wk = bl[..., None] - bcum + lic
    m_chunk = jnp.max(wk, axis=-1)
    e = jnp.exp(wk - m_chunk[..., None])
    kv_c = jnp.einsum("bhnc,bhncd,bhnce->bhnde", e, kc, vc)
    ks_c = jnp.einsum("bhnc,bhncd->bhnd", e, kc)

    def step(carry, xs):
        c_s, n_s, m_s = carry
        kv_n, ks_n, bl_n, mc_n = xs
        m_new = jnp.maximum(bl_n + m_s, mc_n)
        a = jnp.exp(bl_n + m_s - m_new)
        c = jnp.exp(mc_n - m_new)
        c_new = a[..., None, None] * c_s + c[..., None, None] * kv_n
        n_new = a[..., None] * n_s + c[..., None] * ks_n
        return (c_new, n_new, m_new), (c_s, n_s, m_s)

    bn, hn = q.shape[:2]
    init = (jnp.zeros((bn, hn, ML_DQK, ML_DV), f32), jnp.zeros((bn, hn, ML_DQK), f32),
            jnp.zeros((bn, hn), f32))
    xs = tuple(jnp.moveaxis(t, 2, 0) for t in (kv_c, ks_c, bl, m_chunk))
    _, (c_prev, n_prev, m_prev) = lax.scan(step, init, xs)
    c_prev = jnp.moveaxis(c_prev, 0, 2)
    n_prev = jnp.moveaxis(n_prev, 0, 2)
    m_prev = jnp.moveaxis(m_prev, 0, 2)
    a_inter = bcum + m_prev[..., None]
    m_t = jnp.maximum(a_inter, m_intra)
    s_inter = jnp.exp(a_inter - m_t)
    s_intra = jnp.exp(m_intra - m_t)
    num = s_inter[..., None] * jnp.einsum("bhncd,bhnde->bhnce", qc, c_prev) + s_intra[..., None] * num_intra
    den = s_inter * jnp.einsum("bhncd,bhnd->bhnc", qc, n_prev) + s_intra * den_intra
    h = num / jnp.maximum(jnp.abs(den), jnp.exp(-m_t))[..., None]
    return h.reshape(bn, hn, -1, ML_DV)

def stick_breaking(q, k, v):
    seq = q.shape[2]
    scale = SB_DH ** -0.5
    outs = []
    for blk in range(seq // SB_BLOCK):
        q0 = blk * SB_BLOCK
        kend = q0 + SB_BLOCK
        z = jnp.einsum("bhtd,bhsd->bhts", q[:, :, q0:kend], k[:, :, :kend]).astype(jnp.float32) * scale
        t_idx = q0 + jnp.arange(SB_BLOCK)[:, None]
        s_idx = jnp.arange(kend)[None, :]
        causal = s_idx < t_idx
        log_1mb = jnp.where(causal, jax.nn.log_sigmoid(-z), 0.0)
        tail = lax.cumsum(log_1mb, axis=3, reverse=True) - log_1mb
        att = jnp.where(causal, jnp.exp(jax.nn.log_sigmoid(z) + tail), 0.0)
        outs.append(jnp.einsum("bhts,bhsd->bhtd", att.astype(v.dtype), v[:, :, :kend]))
    return jnp.concatenate(outs, axis=2)

def memory_attention(q_mem, mem_k, mem_v):
    q = split_heads(q_mem, MEM_HEADS)
    k = split_heads(mem_k, MEM_HEADS)
    v = split_heads(mem_v, MEM_HEADS)
    s = jnp.einsum("bhtd,bhmd->bhtm", q, k).astype(jnp.float32) * MEM_DH ** -0.5
    p = jax.nn.softmax(s, axis=-1).astype(v.dtype)
    return merge_heads(jnp.einsum("bhtm,bhmd->bhtd", p, v))

def gdn_branch(proj, conv_w, a_log, dt_bias, out_norm):
    qkv, z, a, b, q_mem = jnp.split(proj, [GDN_QKV, GDN_QKV + GDN_VW, GDN_QKV + GDN_VW + GDN_HEADS,
                                           GDN_QKV + GDN_VW + 2 * GDN_HEADS], axis=-1)
    qkv = jax.nn.silu(causal_dwconv(qkv, conv_w))
    q, k, v = jnp.split(qkv, [GDN_KW, 2 * GDN_KW], axis=-1)
    o = gated_delta_rule(split_heads(q, GDN_HEADS), split_heads(k, GDN_HEADS), split_heads(v, GDN_HEADS),
                         a.transpose(0, 2, 1), b.transpose(0, 2, 1), a_log, dt_bias)
    o = rms_norm(o, out_norm) * jax.nn.silu(split_heads(z, GDN_HEADS).astype(jnp.float32))
    return merge_heads(o).astype(proj.dtype), q_mem

def mlstm_branch(proj, i_bias, f_bias, out_norm):
    q, k, v, o, i_pre, f_pre, q_mem = jnp.split(
        proj, [ML_KW, 2 * ML_KW, 2 * ML_KW + ML_VW, 2 * ML_KW + 2 * ML_VW,
               2 * ML_KW + 2 * ML_VW + ML_HEADS, 2 * ML_KW + 2 * ML_VW + 2 * ML_HEADS], axis=-1)
    i_pre = (i_pre + i_bias).transpose(0, 2, 1)
    f_pre = (f_pre + f_bias).transpose(0, 2, 1)
    h = mlstm_cell(split_heads(q, ML_HEADS), split_heads(k, ML_HEADS), split_heads(v, ML_HEADS), i_pre, f_pre)
    h = rms_norm(h, out_norm) * jax.nn.sigmoid(split_heads(o, ML_HEADS).astype(jnp.float32))
    return merge_heads(h).astype(proj.dtype), q_mem

def sb_branch(proj):
    q, k, v, q_mem = jnp.split(proj, [SB_W, 2 * SB_W, 3 * SB_W], axis=-1)
    o = stick_breaking(split_heads(q, SB_HEADS), split_heads(k, SB_HEADS), split_heads(v, SB_HEADS))
    return merge_heads(o), q_mem

def swiglu(x, w_in, w_out):
    g, u = jnp.split(x @ w_in, 2, axis=-1)
    return (jax.nn.silu(g) * u) @ w_out

def _w(key, shape, fan_in):
    return jax.random.normal(key, shape, jnp.float32) * fan_in ** -0.5

def _gain(key, shape):
    return 1.0 + 0.02 * jax.random.normal(key, shape, jnp.float32)

def second_inputs(seed: int = 0) -> dict:
    key = jax.random.key(seed)
    ks = jax.random.split(key, 24)
    dt = jnp.exp(jax.random.uniform(ks[14], (N_GDN, GDN_HEADS), jnp.float32,
                                    minval=math.log(1e-3), maxval=math.log(1e-1)))
    return {
        "x": jax.random.normal(ks[0], (BATCH, SEQ, D_MODEL), jnp.float32),
        "mem": jax.random.normal(ks[1], (BATCH, N_MEM, D_MODEL), jnp.float32),
        "mem_norm": _gain(ks[2], (D_MODEL,)),
        "norm_pre_mix": _gain(ks[3], (DEPTH_2, D_MODEL)),
        "norm_post_mix": _gain(ks[4], (DEPTH_2, D_MODEL)),
        "norm_pre_ffn": _gain(ks[5], (DEPTH_2, D_MODEL)),
        "norm_post_ffn": _gain(ks[6], (DEPTH_2, D_MODEL)),
        "w_mem_kv": _w(ks[7], (DEPTH_2, D_MODEL, 2 * MEM_W), D_MODEL),
        "w_out": _w(ks[8], (DEPTH_2, MIX_W, D_MODEL), MIX_W),
        "w_ffn_in": _w(ks[9], (DEPTH_2, D_MODEL, 2 * D_FF_2), D_MODEL),
        "w_ffn_out": _w(ks[10], (DEPTH_2, D_FF_2, D_MODEL), D_FF_2),
        "gdn_w_in": _w(ks[11], (N_GDN, D_MODEL, GDN_IN), D_MODEL),
        "gdn_conv": _w(ks[12], (N_GDN, CONV_K, GDN_QKV), CONV_K),
        "gdn_a_log": jnp.log(jax.random.uniform(ks[13], (N_GDN, GDN_HEADS), jnp.float32, minval=1.0, maxval=16.0)),
        "gdn_dt_bias": dt + jnp.log(-jnp.expm1(-dt)),
        "gdn_out_norm": _gain(ks[15], (N_GDN, GDN_DV)),
        "ml_w_in": _w(ks[16], (N_ML, D_MODEL, ML_IN), D_MODEL),
        "ml_i_bias": 0.1 * jax.random.normal(ks[17], (N_ML, ML_HEADS), jnp.float32),
        "ml_f_bias": jax.random.uniform(ks[18], (N_ML, ML_HEADS), jnp.float32, minval=3.0, maxval=6.0),
        "ml_out_norm": _gain(ks[19], (N_ML, ML_DV)),
        "sb_w_in": _w(ks[20], (N_SB, D_MODEL, SB_IN), D_MODEL),
    }

def second_block(x, mem, mem_norm, norm_pre_mix, norm_post_mix, norm_pre_ffn, norm_post_ffn, w_mem_kv,
              w_out, w_ffn_in, w_ffn_out, gdn_w_in, gdn_conv, gdn_a_log, gdn_dt_bias, gdn_out_norm,
              ml_w_in, ml_i_bias, ml_f_bias, ml_out_norm, sb_w_in):
    h = x
    mem_n = rms_norm(mem, mem_norm)
    for layer in range(DEPTH_2):
        kind = layer % N_MIXERS
        j = layer // N_MIXERS
        u = rms_norm(h, norm_pre_mix[layer])
        if kind == 0:
            y_mix, q_mem = gdn_branch(u @ gdn_w_in[j], gdn_conv[j], gdn_a_log[j], gdn_dt_bias[j], gdn_out_norm[j])
        elif kind == 1:
            y_mix, q_mem = mlstm_branch(u @ ml_w_in[j], ml_i_bias[j], ml_f_bias[j], ml_out_norm[j])
        else:
            y_mix, q_mem = sb_branch(u @ sb_w_in[j])
        mem_k, mem_v = jnp.split(mem_n @ w_mem_kv[layer], 2, axis=-1)
        y_mem = memory_attention(q_mem, mem_k, mem_v)
        y = jnp.concatenate([y_mix, y_mem], axis=-1) @ w_out[layer]
        h = h + rms_norm(y, norm_post_mix[layer])
        f = swiglu(rms_norm(h, norm_pre_ffn[layer]), w_ffn_in[layer], w_ffn_out[layer])
        h = h + rms_norm(f, norm_post_ffn[layer])
    return h


def setup_inputs(seed=0):
    out = dict(first_inputs(seed))
    for name, value in second_inputs(seed + 1).items():
        if name != "x":
            out[name + "_2"] = value
    return out


def reference(
    x, meta_tokens, mix_norm, mlp_norm, w_mlp_up, w_mlp_down, w_in, hgrn_lb, hgrn_out_norm,
    mla_q_a_norm, mla_kv_a_norm, w_q_up, w_kv_up, q_norm, k_norm, w_out, pool_w, pool_scale,
    mem_2, mem_norm_2, norm_pre_mix_2, norm_post_mix_2, norm_pre_ffn_2, norm_post_ffn_2,
    w_mem_kv_2, w_out_2, w_ffn_in_2, w_ffn_out_2, gdn_w_in_2, gdn_conv_2, gdn_a_log_2,
    gdn_dt_bias_2, gdn_out_norm_2, ml_w_in_2, ml_i_bias_2, ml_f_bias_2, ml_out_norm_2,
    sb_w_in_2,
):
    x = first_block(
        x, meta_tokens, mix_norm, mlp_norm, w_mlp_up, w_mlp_down, w_in, hgrn_lb, hgrn_out_norm,
        mla_q_a_norm, mla_kv_a_norm, w_q_up, w_kv_up, q_norm, k_norm, w_out, pool_w, pool_scale,
    )
    return second_block(
        x, mem_2, mem_norm_2, norm_pre_mix_2, norm_post_mix_2, norm_pre_ffn_2, norm_post_ffn_2,
        w_mem_kv_2, w_out_2, w_ffn_in_2, w_ffn_out_2, gdn_w_in_2, gdn_conv_2, gdn_a_log_2,
        gdn_dt_bias_2, gdn_out_norm_2, ml_w_in_2, ml_i_bias_2, ml_f_bias_2, ml_out_norm_2,
        sb_w_in_2,
    )


_drawn_inputs = setup_inputs


def setup_inputs(seed=0):
    import zlib

    import numpy as np

    out = dict(_drawn_inputs(seed))
    spreads = {}
    factors = {'mlp_norm': 2.962,
     'hgrn_out_norm': 21.592,
     'mla_q_a_norm': 8.0,
     'mla_kv_a_norm': 8.0,
     'q_norm': 8.0,
     'k_norm': 8.0,
     'mem_norm_2': 26.268,
     'norm_pre_mix_2': 2.854,
     'norm_post_mix_2': 27.687,
     'norm_pre_ffn_2': 17.197,
     'norm_post_ffn_2': 37.112,
     'gdn_out_norm_2': 54.472,
     'pool_scale': 3.38}
    for name, (base, spread) in spreads.items():
        noise = np.random.default_rng([zlib.crc32(name.encode()), seed]).standard_normal(out[name].shape)
        drawn = base * np.exp(spread * noise) if base else spread * noise
        out[name] = __import__('jax').numpy.asarray(drawn.astype(out[name].dtype))
    for name, factor in factors.items():
        out[name] = (out[name] * factor).astype(out[name].dtype)
    return out
```

```python
import math
from contextlib import ExitStack

import concourse.bass as bass
import numpy as np
from concourse import mybir

F32 = mybir.dt.float32
LNEXP = "natural_log_exp_and_others"
FR = mybir.dt.float32r
U32 = mybir.dt.uint32
ALU = mybir.AluOpType
ACT = mybir.ActivationFunctionType
AXX = mybir.AxisListType.X

P = 128
D = 1024
KT = D // P
META = 16
SEQ = 512
L = META + SEQ
HALF = L // 2
EPS = 1e-6
FQ = 4
HEADS = 4
NOPE, ROPE, RANK = 128, 64, 256
QK = NOPE + ROPE
CH = 128
LEAD = CH - META
LP = LEAD + L
NCH = LP // CH
LEVELS = 7
NMEM = 256
GH = 8
FF2 = 2816 // P
CONV = 4
SLOT = 16
BIG = -1.0e30

VEC = {}
_at = 0
for _n, _w in (("mix0", 8), ("mlp0", 8), ("mix1", 8), ("mlp1", 8), ("hg_out", 1), ("cq", 2), ("ckv", 2),
               ("qn", 1), ("qr", 1), ("kn", 1), ("kr", 1), ("pool", 8), ("mem", 8), ("pre_mix", 8), ("post_mix", 8),
               ("pre_ffn", 8), ("post_ffn", 8), ("gdn_out", 1), ("alog", 8), ("dtb", 8), ("conv", 24 * CONV)):
    VEC[_n] = _at
    _at += _w
NVEC = _at

STAGES = (("win", 160, 20), ("kr", 4, 1), ("qup", 12, 8), ("kvup", 16, 8), ("wout", 64, 8), ("mlp0", 512, 64),
          ("memkv", 64, 8), ("pool", 16, 8), ("mlp1", 512, 64), ("gin", 288, 36), ("ab", 16, 0), ("wout2", 96, 8),
          ("ffn", 528, 60))
BLOCK0, TILE0 = {}, {}
_b = _t = 0
for _n, _w, _k in STAGES:
    BLOCK0[_n], TILE0[_n] = _b, _t
    _b += _w
    _t += _k
NBLOCKS = _b
NSLOTS = _b // SLOT
assert NSLOTS * SLOT == _b


def tok(ap, n):
    if n == L:
        return ap.rearrange("p (h t) -> p h t", h=2)
    return ap[:, META:L] if n == SEQ else ap[:, 0:n]


def build(nc, xT, memT, W, vecs_d, masks_d, rope_d, out):
    ctx = ExitStack()
    with ctx:
        arena = ctx.enter_context(nc.sbuf_tensor("arena", [P, 212000 // 4], F32))
        base = [16512]
        del arena

        def at(name, shape, dt, offset):
            n = int(np.prod(shape[1:])) * 4
            assert offset % 32 == 0 and offset + n <= 16512 + 212000, (name, offset + n)
            return nc.alloc_sbuf_tensor_at(name, shape, dt, offset=offset), offset + n

        def place(name, shape, dt):
            t, end = at(name, shape, dt, base[0])
            base[0] = (end + 31) // 32 * 32
            return t

        def region(start, *items):
            got, off = [], start
            for name, shape, dt in items:
                t, end = at(name, shape, dt, off)
                off = (end + 31) // 32 * 32
                got.append(t)
            return got

        raw = [place(f"raw{c}", [P, SLOT, P], F32) for c in range(2)]
        whi = [place(f"whi{c}", [P, SLOT, P], FR) for c in range(2)]
        wlo = [place(f"wlo{c}", [P, SLOT, P], FR) for c in range(2)]
        H = place("H", [P, KT, L], F32)
        u_at = base[0]
        UH = place("UH", [P, KT, L], FR)
        UL = place("UL", [P, KT, L], FR)
        R = [place(f"R{c}", [P, L], F32) for c in range(2)]
        SQ = [place(f"SQ{c}", [P, L], F32) for c in range(2)]
        R2 = place("R2", [P, L], F32)
        vecs = place("vecs", [P, NVEC], F32)
        masks = place("masks", [P, LEVELS + 5, P], F32)
        zero = place("zero", [P, 1], F32)
        eps = place("eps", [P, 1], F32)
        S0 = base[0]
        level = masks[:, 0:LEVELS, :]
        ident = masks[:, LEVELS, :]
        upper = masks[:, LEVELS + 1, :]
        ones = masks[:, LEVELS + 2, :]
        turn = masks[0:ROPE, LEVELS + 3, 0:ROPE]
        early = masks[0:1, LEVELS + 4, :]

        Z, = region(S0, ("Z", [P, 20, L], F32))
        hw = S0 + 20 * L * 4
        (qp, kp, vp, lf, bb, qb, kd, XD0, XD1, XE0, XE1, am, kdT, vT, S, TA, TB, GL) = region(
            hw, ("qp", [P, LP], F32), ("kp", [P, LP], F32), ("vp", [P, LP], F32), ("lf", [P, LP], F32),
            ("bb", [P, LP], F32), ("qb", [P, LP], F32), ("kd", [P, LP], F32), ("XD0", [P, LP], F32),
            ("XD1", [P, LP], F32), ("XE0", [P, LP], F32), ("XE1", [P, LP], F32), ("am", [P, LP], F32),
            ("kdT", [P, 4, P], F32), ("vT", [P, NCH, P], F32), ("S", [P, 4, P], F32), ("TA", [P, L], F32),
            ("TB", [P, L], F32), ("GL", [P, 8], F32))
        XD, XE = [XD0, XD1], [XE0, XE1]
        KR, TAB = region((16512 + 212000 - 3 * 2112 - 96) // 32 * 32, ("KR", [ROPE, L], F32), ("TAB", [ROPE, 2, L], F32))
        mw = S0 + 4 * L * 4
        CHI, CLO, QN, KN, V, QR = region(
            mw, ("CHI", [P, 4, L], FR), ("CLO", [P, 4, L], FR), ("QN", [P, HEADS, L], F32),
            ("KN", [P, HEADS, L], F32), ("V", [P, HEADS, L], F32), ("QR", [ROPE, HEADS, L], F32))
        TD0, TD1 = region(S0 + 16 * L * 4 + 4 * L * 4, ("TD0", [P, L], F32), ("TD1", [P, L], F32))
        TD = [TD0, TD1]
        rq, rk, PP0, PP1, PT0, PT1, cr = region(
            mw, ("rq", [P, L], F32), ("rk", [P, L], F32), ("PP0", [P, L], F32), ("PP1", [P, L], F32),
            ("PT0", [P, 5, P], F32), ("PT1", [P, 5, P], F32), ("cr", [ROPE, L], F32))
        PP, PT = [PP0, PP1], [PT0, PT1]
        qs, ks, qrs, krs, tr, sr, vs, VT, stat = region(
            mw + 24 * L * 4, ("qs", [P, L], F32), ("ks", [P, L], F32), ("qrs", [ROPE, L], F32), ("krs", [ROPE, L], F32),
            ("tr", [ROPE, L], F32), ("sr", [ROPE, L], F32), ("vs", [P, L], F32), ("VT", [P, 5, P], F32),
            ("stat", [P, 16], F32))

        HH, HL, RL0, RL1, SB0, SB1 = region(
            S0, ("HH", [P, 8, L], FR), ("HL", [P, 8, L], FR), ("RL0", [P, L], F32), ("RL1", [P, L], F32),
            ("SB0", [P, L], F32), ("SB1", [P, L], F32))
        RL, SB = [RL0, RL1], [SB0, SB1]

        UX, W0, W1, DD0, DD1 = region(S0, ("UX", [P, KT, L], F32), ("W0", [P, 2, L], F32), ("W1", [P, 2, L], F32),
                                      ("DD0", [P, 2, L], F32), ("DD1", [P, 2, L], F32))
        DD = [DD0, DD1]
        END = (16512 + 212000) // 32 * 32
        KM, VMT = region(END - 8192, ("KM", [P, HEADS, NMEM], F32), ("VMT", [P, 2, 512], F32))
        MEM, MSQ, MH, ML, RM, VM = region(
            END - 8192 - 4 * 8192 - 1024 - 4096, ("MEM", [P, KT, NMEM], F32), ("MSQ", [P, KT, NMEM], F32),
            ("MH", [P, KT, NMEM], FR), ("ML", [P, KT, NMEM], FR), ("RM", [P, NMEM], F32), ("VM", [P, HEADS, NMEM], F32))
        QKV, ZQ, XP0, XP1, CA0, CA1, AB, SCAL, SC = region(
            S0, ("QKV", [P, 24, SEQ], F32), ("ZQ", [P, 12, SEQ], F32), ("XP0", [P, SEQ + 4], F32),
            ("XP1", [P, SEQ + 4], F32), ("CA0", [P, SEQ], F32), ("CA1", [P, SEQ], F32), ("AB", [P, 6, 32], F32),
            ("SCAL", [P, 6, 32], F32), ("SC", [P, 6, 8], F32))
        XP, CA = [XP0, XP1], [CA0, CA1]
        g2 = ("qn", "kn", "kg", "vt", "T", "LT", "PT", "LM")
        wk = region(u_at, *[("w_%s%d" % (n, g), [P, 4, P], F32) for n in g2 for g in range(2)])
        G2 = {n: wk[2 * a:2 * a + 2] for a, n in enumerate(g2)}
        wk = region(S0 + 36 * SEQ * 4, *[("w_%s%d" % (n, g), [P, 4, P], F32) for n in ("U", "A") for g in range(2)])
        G2["U"], G2["A"] = wk[0:2], wk[2:4]
        ST8, = region(END - 8192, ("ST8", [P, GH, P], F32))
        am_p, am_t, am_q, am_k, am_v, am_s = region(
            u_at, ("am_p", [P, 4, NMEM], F32), ("am_t", [P, 2, SEQ], F32), ("am_q", [P, SEQ], F32),
            ("am_k", [P, NMEM], F32), ("am_v", [P, 2, P], F32), ("am_s", [P, 16], F32))
        OMH, OML, GR0, GR1, GT0, GT1, Y = region(
            S0 + 8 * SEQ * 4, ("OMH", [P, HEADS, L], FR), ("OML", [P, HEADS, L], FR), ("GR0", [P, L], F32),
            ("GR1", [P, L], F32), ("GT0", [P, L], F32), ("GT1", [P, L], F32), ("Y", [P, KT, L], F32))
        GR, GT = [GR0, GR1], [GT0, GT1]
        FH, FL, FO, GA0, GA1, GS0, GS1, GC0, GC1 = region(
            S0, ("FH", [P, 11, L], FR), ("FL", [P, 11, L], FR), ("FO", [P, KT, L], F32), ("GA0", [P, L], F32),
            ("GA1", [P, L], F32), ("GS0", [P, L], F32), ("GS1", [P, L], F32), ("GC0", [P, L], F32), ("GC1", [P, L], F32))
        GA, GS, GC = [GA0, GA1], [GS0, GS1], [GC0, GC1]

        ps = ctx.enter_context(nc.psum_tensor("ps", [P, 8, 512], F32))
        flat = ps[:, :, :].rearrange("p b c -> p (b c)")

        def sem(name):
            return ctx.enter_context(nc.semaphore(name))

        raw_in = [sem(f"raw_in{c}") for c in range(2)]
        w_hi, w_lo, w_used = sem("w_hi"), sem("w_lo"), sem("w_used")
        tile_done = sem("tile_done")
        evac = [sem(f"evac{c}") for c in range(2)]
        consts_in, x_in, rope_in = sem("consts_in"), sem("x_in"), sem("rope_in")
        zero_set = sem("zero_set")
        h_final, sq_done, sq_summed, r_ready = sem("h_final"), sem("sq_done"), sem("sq_summed"), sem("r_ready")
        uh_done, u_done, r2_done = sem("uh_done"), sem("u_done"), sem("r2_done")
        relu_done, relu2_done, hh_done, hid_done = sem("relu_done"), sem("relu2_done"), sem("hh_done"), sem("hid_done")
        out_done = sem("out_done")
        passed = sem("passed")
        X = {n: sem("hg_" + n) for n in ("silu", "l", "lf", "d", "k", "v", "b", "eb", "qb", "dk", "ek", "kd", "vt", "vtc",
                                         "kt", "ktc", "st", "S", "D", "E", "EQ", "A", "am", "o", "osq", "on", "or", "og",
                                         "oh", "end")}

        M = {n: sem("mla_" + n) for n in ("sq", "sum", "chi", "r", "c", "q", "qsum", "rr", "vt", "vtc", "vs", "x", "turn",
                                          "s", "sc", "max", "exp", "p", "t", "tc", "pv", "oh", "end")}

        N = {n: sem(n) for n in ("mem_in", "mem_sq", "mem_sum", "mem_r", "mem_hi", "mem_lo", "mem_vt", "mem_vtc", "dd",
                                 "conv", "conv_silu", "gate_silu", "rt", "ab", "ab_x", "ab_ln", "ab_g", "ab_cum", "ab_exp",
                                 "ab_all", "ma_in", "ma_s", "ma_max", "ma_exp", "ma_p", "ma_t", "ma_tc", "ma_o",
                                 "ma_end", "om_hi", "om_lo", "g_sum", "g_r", "g_t", "y_sq", "f_silu", "f_hh",
                                 "f_hid", "y_out")}
        G = {n: sem("gd_" + n) for n in ("sq", "sum", "rs", "nrm", "gb", "d", "eg", "dec", "kk", "tr", "lt", "kg", "lm",
                                         "a", "ac", "p", "u", "ks", "r", "vn", "vnc", "o", "oc", "s")}

        def psum(t, n, m=P):
            b = 2 * (t % 2)
            return ps[0:m, b:b + 2, 0:HALF] if n == L else ps[0:m, b, 0:n]

        def evacuated(t):
            return evac[t % 2], t // 2 + 1

        block = ctx.enter_context(nc.Block())

        @block.sync
        def _(sp):
            sp.dma_start(H[:, :, :], xT).then_inc(x_in, 16)
            sp.dma_start(vecs[:, :], vecs_d).then_inc(consts_in, 16)
            sp.dma_start(masks[:, :, :], masks_d).then_inc(consts_in, 16)
            sp.dma_start(TAB[:, :, :], rope_d).then_inc(rope_in, 16)
            for c in range(2):
                sp.dma_start(raw[c][:, :, :], W[c]).then_inc(raw_in[c], 16)
            with sp.Fori(1, NSLOTS // 2) as i:
                for c in range(2):
                    sp.wait_ge(w_lo, 2 * i + c - 1)
                    sp.dma_start(raw[c][:, :, :], W[bass.ds(2 * i + c, 1), :, :, :].rearrange("a p s e -> p (a s) e")
                                 ).then_inc(raw_in[c], 16)
            for s in range(NSLOTS // 2 * 2, NSLOTS):
                sp.wait_ge(w_lo, s - 1)
                sp.dma_start(raw[s % 2][:, :, :], W[s]).then_inc(raw_in[s % 2], 16)
            for k in range(KT):
                sp.wait_ge(N["y_out"], k + 1)
                sp.dma_start(out[:, k, :], H[:, k, META:L]).then_inc(out_done, 16)
            sp.wait_ge(out_done, 16 * KT)

        @block.gpsimd
        def _(pool):
            pool.memset(zero[:, :], 0.0).then_inc(zero_set, 1)
            pool.memset(eps[:, :], EPS).then_inc(zero_set, 1)
            pool.wait_ge(zero_set, 2)

            def split(c, g, first):
                src = raw[c][:, :, :].rearrange("p s e -> p (s e)")
                hi = whi[c][:, :, :].rearrange("p s e -> p (s e)")
                lo = wlo[c][:, :, :].rearrange("p s e -> p (s e)")
                pool.wait_ge(raw_in[c], 16 * g + 16)
                if not first:
                    pool.wait_ge(w_used, 2 * g + c)
                pool.tensor_tensor(hi, src, zero[:, 0:1].to_broadcast([P, SLOT * P]), ALU.add).then_inc(w_hi, 1)
                pool.wait_ge(w_hi, 2 * g + c + 1)
                pool.tensor_tensor(lo, src, hi.bitcast(F32), ALU.subtract).then_inc(w_lo, 1)

            for c in range(2):
                split(c, 0, True)
            with pool.Fori(1, NSLOTS // 2) as i:
                for c in range(2):
                    split(c, i, False)
            for s in range(NSLOTS // 2 * 2, NSLOTS):
                split(s % 2, s // 2, False)

        @block.tensor
        def _(pe):
            class Stream:
                pos, tile, slots, tiles = 0, 0, 0, 0

            st = Stream()

            def take():
                s, b = st.pos // SLOT, st.pos % SLOT
                if b == 0:
                    pe.wait_ge(w_lo, s + 1 + st.slots)
                release = b == 0
                st.pos += 1
                return whi[s % 2][:, b, :], wlo[s % 2][:, b, :], release

            def passes(dst, wh, wl, xh, xl, start, stop_, release):
                for n, (a, b) in enumerate(((wh, xh), (wh, xl), (wl, xh))):
                    mm = pe.matmul(dst, a, b, start=start and n == 0, stop=stop_ and n == 2)
                    if release and n == 0:
                        mm.then_inc(w_used, 1)
                return mm

            def loop(n, blocks, tiles, body):
                assert blocks % (2 * SLOT) == 0 and tiles % 2 == 0
                pos, tile = st.pos, st.tile
                with pe.Fori(0, n) as i:
                    st.slots, st.tiles = i * (blocks // SLOT), i * tiles
                    body(i)
                    assert st.pos == pos + blocks and st.tile == tile + tiles
                st.slots = st.tiles = 0
                st.pos, st.tile = pos + n * blocks, tile + n * tiles

            def tile(ks, n, xh, xl, m=P, cols=None, before=None):
                t = st.tile
                pe.wait_ge(evac[t % 2], t // 2 + st.tiles // 2)
                dst = psum(t, n, m)
                for k in range(ks):
                    if before:
                        before(k)
                    wh, wl, rel = take()
                    if n == L:
                        a, b = tok(xh(k), n), tok(xl(k), n)
                        for h in range(2):
                            mm = passes(dst[:, h, :], wh[:, 0:m], wl[:, 0:m], a[:, h, :], b[:, h, :], k == 0,
                                        k == ks - 1, rel and h == 0)
                    else:
                        mm = passes(dst, wh[:, 0:m], wl[:, 0:m], tok(xh(k), n), tok(xl(k), n), k == 0, k == ks - 1, rel)
                mm.then_inc(tile_done, 1)
                st.tile += 1

            def norm_sum(m, k, n=L):
                x = 8 * m + k
                pe.wait_ge(sq_done, x + 1)
                if k == 0 and m > 0:
                    pe.wait_ge(r_ready, m)
                if m >= 3:
                    mm = pe.matmul(ps[:, 4, :], ones, SQ[x % 2][:, META:L], start=k == 0, stop=k == KT - 1)
                else:
                    for h in range(2):
                        mm = pe.matmul(ps[:, 4 + h, 0:HALF], ones, SQ[x % 2][:, h * HALF:(h + 1) * HALF],
                                       start=k == 0, stop=k == KT - 1)
                mm.then_inc(sq_summed, 1)

            def u(k):
                return UH[:, k, :]

            def ul(k):
                return UL[:, k, :]

            def mlp(m, n, layer):
                def quarter(q, last):
                    for j in range(8):
                        tile(KT, n, u, ul)
                    for e in range(8):
                        def hid_wait(f):
                            if e == 0:
                                pe.wait_ge(hid_done, 32 * layer + 8 * q + f + 1)
                        tile(8, n, lambda f: HH[:, f, :], lambda f: HL[:, f, :], before=hid_wait)
                        if last and e >= 2:
                            norm_sum(m, e - 2)
                loop(FQ - 1, 128, 16, lambda i: quarter(i, False))
                quarter(FQ - 1, True)
                for k in (6, 7):
                    norm_sum(m, k)

            def hgrn(h):
                def w(name, per, c):
                    pe.wait_ge(X[name], h * per + c)
                w("v", 1, 1)
                for c in range(NCH):
                    mm = pe.transpose(flat[:, 3072 + c * P:3072 + (c + 1) * P], vp[:, c * P:(c + 1) * P], ident)
                mm.then_inc(X["vt"], 1)
                w("k", 1, 1)
                w("b", 1, 1)
                w("am", 8, 0)
                for c in range(NCH):
                    mm = pe.matmul(flat[:, c * P:(c + 1) * P], kp[:, c * P:(c + 1) * P], qp[:, c * P:(c + 1) * P],
                                   start=True, stop=True)
                mm.then_inc(X["A"], 1)
                w("kd", 1, 1)
                w("or", 1, 0)
                for c in range(4):
                    mm = pe.transpose(ps[:, 4, c * P:(c + 1) * P], kd[:, c * P:(c + 1) * P], ident)
                mm.then_inc(X["kt"], 1)
                w("ktc", 1, 1)
                w("vtc", 1, 1)
                w("S", 1, 0)
                for c in range(4):
                    mm = pe.matmul(ps[:, 5, c * P:(c + 1) * P], kdT[:, c, :], vT[:, c, :], start=True, stop=True)
                mm.then_inc(X["st"], 1)
                for l in range(1, LEVELS + 1):
                    w("EQ", LEVELS, l)
                    if l >= 2:
                        w("am", 8, l - 1)
                    o = 1024 * (l % 2)
                    e = XE[l % 2]
                    for c in range(NCH):
                        mm = pe.matmul(flat[:, o + c * P:o + (c + 1) * P], e[:, c * P:(c + 1) * P],
                                       e[:, c * P:(c + 1) * P], start=True, stop=True)
                    mm.then_inc(X["A"], 1)
                w("am", 8, 8)
                w("S", 1, 1)
                w("qb", 1, 1)
                for c in range(NCH):
                    dst = flat[:, 3072 + c * P:3072 + (c + 1) * P]
                    mm = pe.matmul(dst, vT[:, c, :], am[:, c * P:(c + 1) * P], start=True, stop=c == 0)
                    if c:
                        mm = pe.matmul(dst, S[:, c - 1, :], qb[:, c * P:(c + 1) * P], start=False, stop=True)
                mm.then_inc(X["o"], 1)
                w("osq", 1, 1)
                for g in range(2):
                    mm = pe.matmul(ps[:, 4 + g, 0:HALF], ones, TA[:, g * HALF:(g + 1) * HALF], start=True, stop=True)
                mm.then_inc(X["on"], 1)

            pe.wait_ge(consts_in, 32)
            for k in range(KT):
                norm_sum(0, k)
            pe.wait_ge(u_done, 8)
            loop(5, 32, 4, lambda i: [tile(KT, L, u, ul) for _ in range(4)])
            t = st.tile
            pe.wait_ge(evac[t % 2], t // 2)
            for k in range(KT):
                if k % 2 == 0:
                    wh, wl, rel = take()
                c = ROPE * (k % 2)
                for h in range(2):
                    mm = passes(psum(t, L, ROPE)[:, h, :], wh[:, c:c + ROPE], wl[:, c:c + ROPE],
                                tok(u(k), L)[:, h, :], tok(ul(k), L)[:, h, :], k == 0, k == KT - 1, rel and h == 0)
                rel = False
            mm.then_inc(tile_done, 1)
            st.tile += 1
            with pe.Fori(0, HEADS) as h:
                hgrn(h)
            for x in range(4):
                pe.wait_ge(M["sq"], x + 1)
                for g in range(2):
                    mm = pe.matmul(ps[:, 4 + 2 * (x // 2) + g, 0:HALF], ones, SQ[x % 2][:, g * HALF:(g + 1) * HALF],
                                   start=x % 2 == 0, stop=x % 2 == 1)
                mm.then_inc(M["sum"], 1)
            pe.wait_ge(M["c"], 4)
            for h in range(HEADS):
                tile(2, L, lambda k: CHI[:, k, :], lambda k: CLO[:, k, :])
                t = st.tile
                pe.wait_ge(evac[t % 2], t // 2)
                wh, wl, rel = take()
                for k in range(2):
                    c = ROPE * k
                    for g in range(2):
                        mm = passes(psum(t, L, ROPE)[:, g, :], wh[:, c:c + ROPE], wl[:, c:c + ROPE],
                                    tok(CHI[:, k, :], L)[:, g, :], tok(CLO[:, k, :], L)[:, g, :], k == 0, k == 1,
                                    rel and k == g == 0)
                mm.then_inc(tile_done, 1)
                st.tile += 1
            for j in range(2 * HEADS):
                tile(2, L, lambda k: CHI[:, 2 + k, :], lambda k: CLO[:, 2 + k, :])

            def attend(h):
                def w(name, per, c):
                    pe.wait_ge(M[name], h * per + c)
                w("vs", 1, 1)
                for c in range(5):
                    a, n = (0, META) if c == 0 else (META + (c - 1) * P, P)
                    mm = pe.transpose(flat[0:n, 3072 + c * P:3072 + (c + 1) * P], vs[:, a:a + n], ident)
                mm.then_inc(M["vt"], 1)
                for x in range(2):
                    w("q", 2, x + 1)
                    if x:
                        w("rr", 2, 1)
                    for g in range(2):
                        a = slice(g * HALF, (g + 1) * HALF)
                        pe.matmul(ps[:, 4 + g, 0:HALF], ones, SQ[0][:, a], start=True, stop=False)
                        mm = pe.matmul(ps[:, 4 + g, 0:HALF], ones[0:ROPE, :], SQ[1][0:ROPE, a], start=False, stop=True)
                    mm.then_inc(M["qsum"], 1)
                for x in range(2):
                    w("x", 2, x + 1)
                    pe.sem_inc(passed, 1)
                    for g in range(2):
                        mm = pe.matmul(ps[0:ROPE, 2 * x + g, 0:HALF], turn, tr[:, g * HALF:(g + 1) * HALF], start=True,
                                       stop=True)
                    mm.then_inc(M["turn"], 1)
                w("s", 2, 2)
                w("vtc", 1, 1)

                def span(j):
                    return (0, META, META) if j == 0 else (META + (j - 1) * P, P, META + j * P)

                def score(j):
                    q0, n, nk = span(j)
                    if j >= 2:
                        w("exp", 5, j - 1)
                    o = 1024 * (j % 2)
                    for a, b in ((0, min(nk, 512)), (512, nk)):
                        if a >= b:
                            continue
                        pe.matmul(flat[0:n, o + a:o + b], qs[:, q0:q0 + n], ks[:, a:b], start=True, stop=False,
                                  skip_group_check=True)
                        mm = pe.matmul(flat[0:n, o + a:o + b], qrs[:, q0:q0 + n], krs[:, a:b], start=False,
                                       stop=True, skip_group_check=True)
                        c = max(a, nk - 64)
                        if j and c < b:
                            mm = pe.matmul(flat[0:n, o + c:o + b], early, ones[0:1, 0:b - c], start=False, stop=True,
                                           skip_group_check=True)
                    mm.then_inc(M["sc"], 1)

                def turned(j):
                    q0, n, nk = span(j)
                    if j:
                        w("tc", 5, j)
                    w("p", 5, j + 1)
                    pe.sem_inc(passed, 1)
                    for c in range(j + 1):
                        a, m = (0, META) if c == 0 else (META + (c - 1) * P, P)
                        mm = pe.transpose(flat[0:m, 2048 + c * P:2048 + c * P + n], PP[j % 2][0:n, a:a + m],
                                          ident[0:n, 0:n])
                    mm.then_inc(M["t"], 1)

                def values(j):
                    q0, n, nk = span(j)
                    w("tc", 5, j + 1)
                    dst = flat[:, 3584:3584 + META] if j == 0 else flat[:, 3072 + (j - 1) * P:3072 + j * P]
                    for c in range(j + 1):
                        m = META if c == 0 else P
                        mm = pe.matmul(dst, VT[0:m, c, :], PT[j % 2][0:m, c, 0:n], start=c == 0, stop=c == j)
                    mm.then_inc(M["pv"], 1)
                score(0)
                for j in range(5):
                    if j + 1 < 5:
                        score(j + 1)
                    turned(j)
                    if j:
                        values(j - 1)
                values(4)

            with pe.Fori(0, HEADS) as h:
                attend(h)
            pe.wait_ge(M["end"], HEADS)
            for e in range(KT):
                tile(KT, L, u, ul)
                if e >= 2:
                    norm_sum(1, e - 2)
            for k in (6, 7):
                norm_sum(1, k)
            pe.wait_ge(u_done, 16)
            mlp(2, L, 0)
            pe.wait_ge(N["mem_sq"], 1)
            for k in range(KT):
                mm = pe.matmul(ps[:, 6, 0:NMEM], ones, MSQ[:, k, :], start=k == 0, stop=k == KT - 1)
            mm.then_inc(N["mem_sum"], 1)
            pe.wait_ge(N["mem_lo"], KT)
            for j in range(2 * HEADS):
                tile(KT, NMEM, lambda k: MH[:, k, :], lambda k: ML[:, k, :])
            for e in range(KT):
                g = 2 * (e // 2)
                pe.wait_ge(u_done, 16 + g + 2)
                tile(2, SEQ, lambda k: UH[:, g + k, :], lambda k: UL[:, g + k, :])
                if e >= 2:
                    norm_sum(3, e - 2)
            for k in (6, 7):
                norm_sum(3, k)
            pe.wait_ge(*evacuated(TILE0["memkv"] + 6))
            pe.wait_ge(*evacuated(TILE0["memkv"] + 7))
            for x in range(2):
                for h in range(HEADS):
                    mm = pe.transpose(ps[:, 6 + x, h * P:(h + 1) * P], VM[:, h, x * P:(x + 1) * P], ident)
            mm.then_inc(N["mem_vt"], 1)
            pe.wait_ge(u_done, 32)
            mlp(4, SEQ, 1)
            pe.wait_ge(u_done, 40)
            loop(6, 32, 4, lambda i: [tile(KT, SEQ, u, ul) for _ in range(4)])
            loop(3, 32, 4, lambda i: [tile(KT, SEQ, u, ul) for _ in range(4)])
            t = st.tile
            for x in (t - 2, t - 1):
                pe.wait_ge(*evacuated(x))
            wh, wl, rel = take()
            for c in range(4):
                for k in range(KT):
                    a = slice(META + c * P, META + (c + 1) * P)
                    for n, (p1, p2) in enumerate(((UH, wh), (UL, wh), (UH, wl))):
                        mm = pe.matmul(ps[:, 7, 16 * c:16 * c + 16], p1[:, k, a], p2[:, 16 * k:16 * k + 16],
                                       start=k == 0 and n == 0, stop=k == KT - 1 and n == 2)
                        if rel:
                            mm.then_inc(w_used, 1)
                            rel = False
            for c in range(4):
                mm = pe.matmul(ps[:, 7, 64 + c:65 + c], R[0][0:1, META + c * P:META + (c + 1) * P], ones[0:1, 0:1],
                               start=True, stop=True)
            mm.then_inc(N["rt"], 1)
            st.pos += SLOT - 1
            pe.wait_ge(N["ab_g"], 1)
            pe.matmul(ps[:, 7, 128:160], upper, AB[:, 0, :], start=True, stop=True)
            pe.matmul(ps[:, 7, 160:192], ones, AB[:, 0, :], start=True, stop=True).then_inc(N["ab_cum"], 1)

            def recall(h):
                def w(name, c):
                    pe.wait_ge(N[name], h + c)
                w("ma_in", 1)
                w("ma_p", 0)
                for c in range(4):
                    mm = pe.matmul(ps[:, c // 2, NMEM * (c % 2):NMEM * (c % 2 + 1)], am_q[:, c * P:(c + 1) * P],
                                   am_k[:, :], start=True, stop=True)
                mm.then_inc(N["ma_s"], 1)
                w("ma_p", 1)
                for x in range(2):
                    for c in range(4):
                        mm = pe.transpose(ps[:, 2 + x, c * P:(c + 1) * P], am_p[:, c, x * P:(x + 1) * P], ident)
                mm.then_inc(N["ma_t"], 1)
                w("ma_tc", 1)
                w("ma_end", 0)
                for x in range(2):
                    mm = pe.matmul(ps[:, 4, :], am_v[:, x, :], am_t[:, x, :], start=x == 0, stop=x == 1)
                mm.then_inc(N["ma_o"], 1)
            with pe.Fori(0, HEADS) as h:
                recall(h)

            def chunk(c):
                def w(name, k, per=1):
                    pe.wait_ge(G[name], c * 2 * per + k)

                def four(bank, a, b, g):
                    for x in range(4):
                        mm = pe.matmul(ps[:, 4 * g + bank, x * P:(x + 1) * P], a(x), b(x), start=True, stop=True)
                    return mm

                def turned(bank, a, g):
                    for x in range(4):
                        mm = pe.transpose(ps[:, 4 * g + bank, x * P:(x + 1) * P], a[:, x, :], ident)
                    return mm
                for g in range(2):
                    w("sq", g + 1)
                    pe.matmul(ps[:, 4 * g, :], ones, G2["LM"][g][:, :, :].rearrange("p x t -> p (x t)"), start=True,
                              stop=True)
                    pe.matmul(ps[:, 4 * g + 1, :], ones, G2["A"][g][:, :, :].rearrange("p x t -> p (x t)"), start=True,
                              stop=True).then_inc(G["sum"], 1)
                for g in range(2):
                    w("nrm", g + 1)
                    w("oc", 0)
                    four(2, lambda x: SC[:, 0, 4 * g + x:4 * g + x + 1].to_broadcast([P, P]), lambda x: upper, g
                         ).then_inc(G["gb"], 1)
                    w("s", 0)
                    kn, qn = G2["kn"][g], G2["qn"][g]
                    four(0, lambda x: kn[:, x, :], lambda x: kn[:, x, :], g)
                    four(1, lambda x: kn[:, x, :], lambda x: qn[:, x, :], g).then_inc(G["kk"], 1)
                    turned(3, kn, g)
                    w("d", g + 1)
                    w("eg", g + 1)
                    turned(2, G2["PT"][g], g).then_inc(G["tr"], 1)
                for g in range(2):
                    w("lm", g + 1, LEVELS)
                    turned(0, G2["LM"][g], g).then_inc(G["a"], 1)
                for l in range(1, LEVELS):
                    for g in range(2):
                        w("u", 2 * (l - 1) + g + 1, LEVELS)
                        w("lm", 2 * l + g + 1, LEVELS)
                        four(0, lambda x: G2["LM"][g][:, x, :], lambda x: G2["T"][g][:, x, :], g).then_inc(G["a"], 1)
                    for g in range(2):
                        w("ac", 2 * (l - 1) + g + 1, LEVELS - 1)
                        a, uu = G2["A"][g], G2["U"][g]
                        if l < LEVELS - 1:
                            four(1, lambda x: uu[:, x, :], lambda x: a[:, x, :], g)
                        if l == 1:
                            w("kg", g + 1)
                        four(2, lambda x: a[:, x, :], lambda x: uu[:, x, :], g).then_inc(G["p"], 1)
                for g in range(2):
                    four(0, lambda x: G2["kn"][g][:, x, :], lambda x: ST8[:, 4 * g + x, :], g).then_inc(G["ks"], 1)
                for g in range(2):
                    w("u", 2 * (LEVELS - 1) + g + 1, LEVELS)
                    w("r", g + 1)
                    four(1, lambda x: G2["U"][g][:, x, :], lambda x: G2["LM"][g][:, x, :], g).then_inc(G["vn"], 1)
                for g in range(2):
                    w("vnc", g + 1)
                    vn = G2["A"][g]
                    for x in range(4):
                        dst = ps[:, 4 * g + 2, x * P:(x + 1) * P]
                        pe.matmul(dst, ST8[:, 4 * g + x, :], G2["qn"][g][:, x, :], start=True, stop=False)
                        pe.matmul(dst, vn[:, x, :], G2["PT"][g][:, x, :], start=False, stop=True)
                    four(3, lambda x: G2["kg"][g][:, x, :], lambda x: vn[:, x, :], g).then_inc(G["o"], 1)
            with pe.Fori(0, 4) as c:
                chunk(c)
            for h in range(GH):
                pe.wait_ge(N["y_sq"], h + 1)
                if h >= 2:
                    pe.wait_ge(N["g_r"], h - 1)
                pe.matmul(ps[:, 4 + h % 2, :], ones, SQ[h % 2][:, META:L], start=True, stop=True).then_inc(N["g_sum"], 1)
            pe.wait_ge(u_done, 48)
            pe.wait_ge(N["om_lo"], HEADS)
            for e in range(KT):
                tile(12, SEQ, lambda k: UH[:, k, :] if k < 8 else OMH[:, k - 8, :],
                     lambda k: UL[:, k, :] if k < 8 else OML[:, k - 8, :])
                if e >= 2:
                    norm_sum(5, e - 2)
            for k in (6, 7):
                norm_sum(5, k)
            for k in range(KT):
                norm_sum(6, k)
            pe.wait_ge(u_done, 56)
            for a in range(2):
                for j in range(22):
                    tile(KT, SEQ, u, ul)
                for e in range(KT):
                    def hid_wait(f):
                        if e == 0:
                            pe.wait_ge(N["f_hid"], 11 * a + f + 1)
                    tile(11, SEQ, lambda f: FH[:, f, :], lambda f: FL[:, f, :], before=hid_wait)
                    if a and e >= 2:
                        norm_sum(7, e - 2)
            for k in (6, 7):
                norm_sum(7, k)

        @block.scalar
        def _(act):
            def square(m, k, src, ready=None):
                x = 8 * m + k
                if ready:
                    act.wait_ge(*ready)
                if x >= 2:
                    act.wait_ge(sq_summed, x - 1)
                c = META if m >= 3 else 0
                act.activation(SQ[x % 2][:, c:L], src[:, c:L], ACT.Square).then_inc(sq_done, 1)

            def rstd(m, n=D):
                act.wait_ge(sq_summed, 8 * m + 8)
                r = R[m % 2]
                if m >= 3:
                    r = r[:, META:L]
                    act.activation(r, ps[:, 4, :], ACT.Ln, bias=eps[:, 0:1], scale=1.0 / n)
                else:
                    r = r[:, :]
                    act.activation(tok(r, L), ps[:, 4:6, 0:HALF], ACT.Ln, bias=eps[:, 0:1], scale=1.0 / n)
                act.drain()
                act.activation(r, r, ACT.Exp, scale=-0.5).then_inc(r_ready, 1)

            def hi(m, k, vec):
                g = vecs[:, VEC[vec] + k:VEC[vec] + k + 1]
                c = META if m >= 3 else 0
                act.activation(UH[:, k, c:L], H[:, k, c:L], ACT.Copy, scale=g).then_inc(uh_done, 1)

            act.preload_act_table_set(LNEXP)
            act.wait_ge(x_in, 16)
            act.wait_ge(consts_in, 32)
            act.wait_ge(zero_set, 2)
            for k in range(KT):
                square(0, k, H[:, k, :])
                hi(0, k, "mix0")
            rstd(0)

            for t in (7, 6, 19, 18):
                act.wait_ge(*evacuated(t))
            for a in (4, 16):
                act.activation(Z[:, a:a + 4, :], Z[:, a:a + 4, :], ACT.Silu).then_inc(X["silu"], 1)
            act.preload_act_table_set(LNEXP)

            def hgrn(h):
                def w(name, per, c):
                    act.wait_ge(X[name], h * per + c)
                f = Z[:, bass.ds(8 + h, 1), :].rearrange("p a t -> p (a t)")
                w("end", 1, 0)
                act.activation(TA[:, :], f, ACT.Abs)
                act.drain()
                act.activation(TA[:, :], TA[:, :], ACT.Exp, scale=-1.0)
                act.drain()
                act.activation(TA[:, :], TA[:, :], ACT.Ln, bias=1.0).then_inc(X["l"], 1)
                w("d", 1, 1)
                act.activation(kp[:, LEAD:LP], TB[:, :], ACT.Exp).then_inc(X["k"], 1)
                w("b", 1, 1)
                act.activation(XE[0][:, :], bb[:, :], ACT.Exp)
                act.activation(GL[:, 0:NCH], bb[:, CH - 1:LP:CH], ACT.Exp).then_inc(X["eb"], 1)
                w("vt", 1, 1)
                act.activation(vT[:, :, :].rearrange("p c v -> p (c v)"), flat[:, 3072:3072 + LP], ACT.Copy
                               ).then_inc(X["vtc"], 1)
                w("dk", 1, 1)
                act.activation(XE[1][:, 0:4 * P], XD[1][:, 0:4 * P], ACT.Exp).then_inc(X["ek"], 1)
                w("kt", 1, 1)
                act.activation(kdT[:, :, :].rearrange("p c v -> p (c v)"), ps[:, 4, :], ACT.Copy).then_inc(X["ktc"], 1)
                for l in range(1, LEVELS + 1):
                    w("D", LEVELS, l)
                    if l >= 3:
                        w("A", 8, l - 1)
                    act.activation(XE[l % 2][:, :], XD[l % 2][:, :], ACT.Exp).then_inc(X["E"], 1)
                w("o", 1, 1)
                o = flat[:, 3072 + LEAD:3072 + LP]
                act.activation(TA[:, :], o, ACT.Square).then_inc(X["osq"], 1)
                w("on", 1, 1)
                act.activation(tok(TB[:, :], L), ps[:, 4:6, 0:HALF], ACT.Ln, bias=eps[:, 0:1], scale=1.0 / P)
                act.drain()
                act.activation(TB[:, :], TB[:, :], ACT.Exp, scale=-0.5).then_inc(X["or"], 1)
                w("og", 1, 1)
                act.activation(UH[:, bass.ds(h, 1), :].rearrange("p a t -> p (a t)"), TB[:, :], ACT.Copy
                               ).then_inc(X["oh"], 1)

            with act.Fori(0, HEADS) as h:
                hgrn(h)
            act.wait_ge(X["end"], HEADS)
            for x in range(4):
                if x >= 2:
                    act.wait_ge(M["sum"], x - 1)
                act.activation(SQ[x % 2][:, :], Z[:, x, :], ACT.Square).then_inc(M["sq"], 1)
                g = VEC["cq"] + x
                act.activation(CHI[:, x, :], Z[:, x, :], ACT.Copy, scale=vecs[:, g:g + 1]).then_inc(M["chi"], 1)
            for x, r in enumerate((R2, R[1])):
                act.wait_ge(M["sum"], 2 * x + 2)
                act.activation(tok(r[:, :], L), ps[:, 4 + 2 * x:6 + 2 * x, 0:HALF], ACT.Ln, bias=eps[:, 0:1],
                               scale=1.0 / RANK)
                act.drain()
                act.activation(r[:, :], r[:, :], ACT.Exp, scale=-0.5).then_inc(M["r"], 1)

            def attend(h):
                def w(name, per, c):
                    act.wait_ge(M[name], h * per + c)
                for x in range(2):
                    if x == 0:
                        w("end", 1, 0)
                    else:
                        w("qsum", 2, 1)
                    a, b = (QN, QR[:, bass.ds(h, 1), :]) if x == 0 else (KN, KR[:, :])
                    act.activation(SQ[0][:, :], a[:, bass.ds(h, 1), :].rearrange("p a t -> p (a t)"), ACT.Square)
                    b = b.rearrange("p a t -> p (a t)") if x == 0 else b
                    act.activation(SQ[1][0:ROPE, :], b, ACT.Square).then_inc(M["q"], 1)
                    w("qsum", 2, x + 1)
                    r = (rq, rk)[x]
                    act.activation(tok(r[:, :], L), ps[:, 4:6, 0:HALF], ACT.Ln, bias=eps[:, 0:1], scale=1.0 / QK)
                    act.drain()
                    act.activation(r[:, :], r[:, :], ACT.Exp, scale=-0.5).then_inc(M["rr"], 1)
                w("vt", 1, 1)
                act.activation(VT[0:META, 0, :], flat[0:META, 3072:3072 + P], ACT.Copy)
                act.activation(VT[:, 1:5, :], flat[:, 3072 + P:3072 + 5 * P].rearrange("p (c v) -> p c v", c=4),
                               ACT.Copy).then_inc(M["vtc"], 1)

                def exps(j):
                    n, nk = (META, META) if j == 0 else (P, META + j * P)
                    w("max", 5, j + 1)
                    if j >= 2:
                        w("t", 5, j - 1)
                    o = 1024 * (j % 2)
                    act.activation(PP[j % 2][0:n, 0:nk], flat[0:n, o:o + nk], ACT.Exp, bias=stat[0:n, j:j + 1],
                                   scale=QK ** -0.5, accum_out=stat[0:n, 8 + j:9 + j]).then_inc(M["exp"], 1)

                def copies(j):
                    n = META if j == 0 else P
                    w("t", 5, j + 1)
                    if j >= 2:
                        w("pv", 5, j - 1)
                    last = act.activation(PT[j % 2][0:META, 0, 0:n], flat[0:META, 2048:2048 + n], ACT.Copy)
                    if j:
                        last = act.activation(PT[j % 2][:, 1:j + 1, :],
                                              flat[:, 2048 + P:2048 + (j + 1) * P].rearrange("p (c v) -> p c v", c=j),
                                              ACT.Copy)
                    last.then_inc(M["tc"], 1)
                exps(0)
                for j in range(5):
                    if j + 1 < 5:
                        exps(j + 1)
                    copies(j)
                w("pv", 5, 5)
                o = UH[:, bass.ds(4 + h, 1), :].rearrange("p a t -> p (a t)")
                act.activation(o[:, 0:META], flat[:, 3584:3584 + META], ACT.Copy)
                act.activation(o[:, META:L], flat[:, 3072:3584], ACT.Copy).then_inc(M["oh"], 1)

            for t in range(TILE0["wout"] - 2, TILE0["wout"]):
                act.wait_ge(*evacuated(t))
            with act.Fori(0, HEADS) as h:
                attend(h)
            act.wait_ge(M["end"], HEADS)
            act.dma_start(MEM[:, :, :], memT).then_inc(N["mem_in"], 16)
            for e in range(KT):
                square(1, e, H[:, e, :], evacuated(TILE0["wout"] + e))
            rstd(1)
            for e in range(KT):
                hi(1, e, "mlp0")

            def mlp(layer, n, m):
                odd = TILE0["mlp%d" % layer] % 2

                def quarter(q, base, last, first=False):
                    def relu(j):
                        t, x = base + j, 8 * q + j
                        act.wait_ge(tile_done, t + 1)
                        if not (first and j < 2):
                            act.wait_ge(relu2_done, x - 1)
                        act.activation(tok(RL[j % 2][:, :], n), psum(odd + j, n), ACT.Relu
                                       ).then_inc(evac[(odd + j) % 2], 1)

                    def part(j):
                        act.wait_ge(relu2_done, 8 * q + j + 1)
                        act.activation(tok(HH[:, j, :], n), tok(SB[j % 2][:, :], n), ACT.Copy).then_inc(hh_done, 1)
                    relu(0)
                    for j in range(8):
                        if j + 1 < 8:
                            relu(j + 1)
                        part(j)
                    if last:
                        for e in range(8):
                            square(m, e, H[:, e, :], (h_final, 8 * layer + e + 1))
                            if m != 2:
                                hi(m, e, {4: "pre_mix"}[m])
                b = TILE0["mlp%d" % layer]
                quarter(FQ * layer, b, False, layer == 0)
                with act.Fori(1, FQ - 1) as i:
                    quarter(i + FQ * layer, i * 16 + b, False)
                quarter(FQ * layer + FQ - 1, b + 16 * (FQ - 1), True)
                rstd(m)
            mlp(0, L, 2)
            act.wait_ge(N["mem_in"], 16)
            act.activation(MSQ[:, :, :], MEM[:, :, :], ACT.Square).then_inc(N["mem_sq"], 1)
            for k in range(KT):
                g = VEC["mem"] + k
                act.activation(MH[:, k, :], MEM[:, k, :], ACT.Copy, scale=vecs[:, g:g + 1]).then_inc(N["mem_hi"], 1)
            act.wait_ge(N["mem_sum"], 1)
            act.activation(RM[:, :], ps[:, 6, 0:NMEM], ACT.Ln, bias=eps[:, 0:1], scale=1.0 / D)
            act.drain()
            act.activation(RM[:, :], RM[:, :], ACT.Exp, scale=-0.5).then_inc(N["mem_r"], 1)
            for g in range(4):
                act.wait_ge(N["dd"], g + 1)
                for c in range(2):
                    act.activation(UH[:, 2 * g + c, META:L], DD[g % 2][:, c, META:L], ACT.Copy).then_inc(uh_done, 1)
            for e in range(KT):
                t = TILE0["pool"] + e
                square(3, e, H[:, e, :], evacuated(t))
                if e % 2:
                    for x in (e - 1, e):
                        hi(3, x, "mlp1")
            rstd(3)
            act.wait_ge(N["mem_vt"], 1)
            act.activation(VMT[:, :, :], ps[:, 6:8, :], ACT.Copy).then_inc(N["mem_vtc"], 1)
            mlp(1, SEQ, 4)
            act.preload_act_table(ACT.Silu)
            with act.Fori(0, 6) as i:
                for j in range(4):
                    act.wait_ge(N["conv"], 4 * i + j + 1)
                    act.sem_inc(passed, 1)
                    act.activation(QKV[:, bass.ds(4 * i + j, 1), :].rearrange("p a t -> p (a t)"), CA[j % 2][:, :],
                                   ACT.Silu).then_inc(N["conv_silu"], 1)
            for t in (TILE0["ab"] - 1, TILE0["ab"] - 2):
                act.wait_ge(*evacuated(t))
            act.activation(ZQ[:, 0:8, :], ZQ[:, 0:8, :], ACT.Silu).then_inc(N["gate_silu"], 1)
            act.preload_act_table_set(LNEXP)
            act.wait_ge(N["ab_x"], 1)
            x3 = AB[:, 1:3, :]
            act.activation(AB[:, 3:5, :], x3, ACT.Abs)
            act.drain()
            act.activation(AB[:, 3:5, :], AB[:, 3:5, :], ACT.Exp, scale=-1.0)
            act.drain()
            act.activation(AB[:, 5, 0:8], vecs[:, VEC["alog"]:VEC["alog"] + 8], ACT.Exp)
            act.activation(AB[:, 3:5, :], AB[:, 3:5, :], ACT.Ln, bias=1.0).then_inc(N["ab_ln"], 1)
            act.wait_ge(N["ab_cum"], 1)
            act.activation(SCAL[:, 2, :], ps[:, 7, 128:160], ACT.Exp)
            act.activation(SCAL[:, 5, :], ps[:, 7, 160:192], ACT.Exp).then_inc(N["ab_exp"], 1)
            act.wait_ge(N["ab_x"], 2)
            act.activation(SCAL[:, 1, :], SCAL[:, 1, :], ACT.Exp)
            act.activation(SCAL[:, 4, :], SCAL[:, 4, :], ACT.Exp).then_inc(N["ab_all"], 1)

            def recall(h):
                def w(name, c):
                    act.wait_ge(N[name], h + c)
                w("ma_end", 0)
                act.sem_inc(passed, 1)
                act.activation(am_q[:, :], ZQ[:, bass.ds(8 + h, 1), :].rearrange("p a t -> p (a t)"), ACT.Copy)
                act.activation(am_k[:, :], KM[:, bass.ds(h, 1), :].rearrange("p a t -> p (a t)"), ACT.Copy)
                act.activation(am_v[:, :, :], VMT[:, :, bass.ds(h * P, P)], ACT.Copy).then_inc(N["ma_in"], 1)
                w("ma_max", 1)
                for c in range(4):
                    last = act.activation(am_p[:, c, :], ps[:, c // 2, NMEM * (c % 2):NMEM * (c % 2 + 1)], ACT.Exp,
                                          bias=am_s[:, c:c + 1], scale=P ** -0.5, accum_out=am_s[:, 4 + c:5 + c])
                last.then_inc(N["ma_exp"], 1)
                w("ma_t", 1)
                act.activation(am_t[:, :, :], ps[:, 2:4, :], ACT.Copy).then_inc(N["ma_tc"], 1)
                w("ma_o", 1)
                act.sem_inc(passed, 1)
                act.activation(ZQ[:, bass.ds(8 + h, 1), :].rearrange("p a t -> p (a t)"), ps[:, 4, :], ACT.Copy
                               ).then_inc(N["ma_end"], 1)
            with act.Fori(0, HEADS) as h:
                recall(h)

            def chunk(c):
                def w(name, k, per=1):
                    act.wait_ge(G[name], c * 2 * per + k)

                def bank(g, b):
                    return ps[:, 4 * g + b, :].rearrange("p (x t) -> p x t", x=4)
                cols = bass.ds(c * P, P)
                for g in range(2):
                    w("r", 0)
                    w("o", 0)
                    act.sem_inc(passed, 1)
                    act.activation(G2["LM"][g][:, :, :], QKV[:, 4 * g:4 * g + 4, cols], ACT.Square)
                    act.activation(G2["A"][g][:, :, :], QKV[:, 8 + 4 * g:12 + 4 * g, cols], ACT.Square
                                   ).then_inc(G["sq"], 1)
                for g in range(2):
                    w("sum", g + 1)
                    for b, d in ((0, G2["U"][g]), (1, G2["LT"][g])):
                        act.activation(d[:, :, :], bank(g, b), ACT.Ln, bias=eps[:, 0:1])
                    act.drain()
                    act.activation(G2["U"][g][:, :, :], G2["U"][g][:, :, :], ACT.Exp, scale=-0.5)
                    act.activation(G2["LT"][g][:, :, :], G2["LT"][g][:, :, :], ACT.Exp, scale=-0.5
                                   ).then_inc(G["rs"], 1)
                for g in range(2):
                    w("gb", g + 1)
                    act.activation(G2["U"][g][:, :, :], bank(g, 2), ACT.Exp).then_inc(G["eg"], 1)
                    w("d", g + 1)
                    act.activation(G2["T"][g][:, :, :], G2["T"][g][:, :, :], ACT.Exp).then_inc(G["dec"], 1)
                for g in range(2):
                    w("tr", g + 1)
                    for x in range(4):
                        act.activation(G2["kg"][g][:, x, :], ps[:, 4 * g + 3, x * P:(x + 1) * P], ACT.Copy,
                                       scale=SC[:, 4, 4 * g + x:4 * g + x + 1])
                    act.activation(G2["vt"][g][:, :, :], bank(g, 2), ACT.Copy).then_inc(G["kg"], 1)
                for l in range(1, LEVELS):
                    for g in range(2):
                        w("a", 2 * l + g + 1, LEVELS)
                        act.activation(G2["A"][g][:, :, :], bank(g, 0), ACT.Copy).then_inc(G["ac"], 1)
                for g in range(2):
                    w("vn", g + 1)
                    for x in range(4):
                        last = act.activation(G2["A"][g][:, x, :], ps[:, 4 * g + 1, x * P:(x + 1) * P], ACT.Copy,
                                              scale=SC[:, 1, 4 * g + x:4 * g + x + 1])
                    last.then_inc(G["vnc"], 1)
                for g in range(2):
                    w("o", g + 1)
                    act.sem_inc(passed, 1)
                    act.activation(QKV[:, 4 * g:4 * g + 4, cols], bank(g, 2), ACT.Copy).then_inc(G["oc"], 1)
            with act.Fori(0, 4) as c:
                chunk(c)
            act.drain()
            for h in range(HEADS):
                act.activation(OMH[:, h, META:L], ZQ[:, 8 + h, :], ACT.Copy).then_inc(N["om_hi"], 1)

            def head_hi(h):
                act.wait_ge(N["g_t"], h + 1)
                act.activation(UH[:, h, META:L], GT[h % 2][:, META:L], ACT.Copy).then_inc(uh_done, 1)
            for h in range(GH):
                if h >= 2:
                    act.wait_ge(N["g_sum"], h - 1)
                act.activation(SQ[h % 2][:, META:L], QKV[:, h, :], ACT.Square).then_inc(N["y_sq"], 1)
                act.wait_ge(N["g_sum"], h + 1)
                if h >= 2:
                    act.wait_ge(N["g_t"], h - 1)
                a = GR[h % 2][:, META:L]
                act.activation(a, ps[:, 4 + h % 2, :], ACT.Ln, bias=eps[:, 0:1], scale=1.0 / P)
                act.drain()
                act.activation(a, a, ACT.Exp, scale=-0.5).then_inc(N["g_r"], 1)
                if h:
                    head_hi(h - 1)
            head_hi(GH - 1)
            act.drain()
            for e in range(KT):
                t = TILE0["wout2"] + e
                act.wait_ge(tile_done, t + 1)
                act.activation(tok(Y[:, e, :], SEQ), psum(t, SEQ), ACT.Copy).then_inc(evac[t % 2], 1)
                act.drain()
                square(5, e, Y[:, e, :])
            rstd(5)
            for e in range(KT):
                square(6, e, H[:, e, :], (h_final, 16 + e + 1))
                hi(6, e, "pre_ffn")
            rstd(6)
            act.preload_act_table(ACT.Silu)

            def f_hi(a, j):
                act.wait_ge(evac[(TILE0["ffn"] + 30 * a + 2 * j + 1) % 2], (TILE0["ffn"] + 30 * a + 2 * j + 1) // 2 + 1)
                act.activation(FH[:, j, META:L], GC[j % 2][:, META:L], ACT.Copy).then_inc(N["f_hh"], 1)
            for a in range(2):
                for j in range(11):
                    act.wait_ge(*evacuated(TILE0["ffn"] + 30 * a + 2 * j))
                    act.activation(GS[j % 2][:, META:L], GA[j % 2][:, META:L], ACT.Silu).then_inc(N["f_silu"], 1)
                    if j:
                        f_hi(a, j - 1)
                f_hi(a, 10)
            for e in range(KT):
                square(7, e, FO[:, e, :], (h_final, 24 + e + 1))
            act.preload_act_table_set(LNEXP)
            rstd(7)

        @block.vector
        def _(dve):
            def lo(m, k, vec):
                g = vecs[:, VEC[vec] + k:VEC[vec] + k + 1]
                dve.wait_ge(uh_done, 8 * m + k + 1)
                c = META if m >= 3 else 0
                dve.scalar_tensor_tensor(UL[:, k, c:L], H[:, k, c:L], g, UH[:, k, c:L].bitcast(F32), ALU.mult,
                                         ALU.subtract).then_inc(u_done, 1)

            def scaled(t, n, dst, r, extra=0, m=P):
                dve.wait_ge(tile_done, t + 1 + extra)
                dve.tensor_tensor(dst, psum(t, n, m), tok(r[0:m, :], n), ALU.mult).then_inc(evac[t % 2], 1)

            dve.wait_ge(x_in, 16)
            dve.wait_ge(consts_in, 32)
            for pad in (qp, kp, vp, lf):
                dve.memset(pad[:, 0:LEAD], 0.0)
            for k in range(KT):
                lo(0, k, "mix0")
            dve.wait_ge(r_ready, 1)
            with dve.Fori(0, 5) as i:
                for j in range(4):
                    dst = Z[:, bass.ds(4 * i + j, 1), :].rearrange("p a (h t) -> p (a h) t", h=2)
                    scaled(j, L, dst, R[0], extra=4 * i)
            scaled(20, L, tok(KR[:, :], L), R[0], m=ROPE)

            def hgrn(h):
                def w(name, per, c):
                    dve.wait_ge(X[name], h * per + c)

                def z(a):
                    return Z[:, bass.ds(a + h, 1), :].rearrange("p a t -> p (a t)")
                dve.tensor_copy(vp[:, LEAD:LP], z(12)).then_inc(X["v"], 1)
                w("l", 1, 1)
                dve.scalar_tensor_tensor(lf[:, LEAD:LP], z(8), 0.0, TA[:, :], ALU.min, ALU.subtract)
                dve.drain()
                dve.tensor_tensor(TB[:, :], lf[:, LEAD:LP], z(8), ALU.subtract).then_inc(X["d"], 1)
                dve.tensor_copy(qp[:, LEAD:LP], z(4))
                for c in range(NCH):
                    last = dve.tensor_tensor_scan(bb[:, c * P:(c + 1) * P], ones, lf[:, c * P:(c + 1) * P], 0.0,
                                                  ALU.mult, ALU.add)
                last.then_inc(X["b"], 1)
                dve.drain()
                b3 = bb[:, 0:4 * P].rearrange("p (c t) -> p c t", c=4)
                d3 = XD[1][:, 0:4 * P].rearrange("p (c t) -> p c t", c=4)
                dve.tensor_tensor(d3, b3[:, :, P - 1:P].to_broadcast([P, 4, P]), b3, ALU.subtract
                                  ).then_inc(X["dk"], 1)
                w("eb", 1, 1)
                dve.tensor_tensor(qb[:, :], qp[:, :], XE[0][:, :], ALU.mult).then_inc(X["qb"], 1)
                w("k", 1, 1)
                w("ek", 1, 1)
                dve.tensor_tensor(kd[:, 0:4 * P], kp[:, 0:4 * P], XE[1][:, 0:4 * P], ALU.mult).then_inc(X["kd"], 1)
                w("A", 8, 1)
                am3 = am[:, :].rearrange("p (c t) -> p c t", c=NCH)
                dve.tensor_tensor(am3, flat[:, 0:LP].rearrange("p (c t) -> p c t", c=NCH),
                                  ident.rearrange("p (a t) -> p a t", a=1).to_broadcast([P, NCH, P]), ALU.mult
                                  ).then_inc(X["am"], 1)

                def halves(ap, m):
                    v = ap[:, :].rearrange("p (b s m) -> p b s m", s=2, m=m)
                    return v[:, :, 0, :], v[:, :, 1, :]

                def diff(l):
                    m = CH >> l
                    left, right = halves(bb, m)
                    ref = left[:, :, m - 1:m].to_broadcast([P, LP // (2 * m), m])
                    dl, dr = halves(XD[l % 2], m)
                    if l >= 3:
                        w("E", LEVELS, l - 2)
                    dve.tensor_tensor(dl, ref, left, ALU.subtract)
                    dve.tensor_tensor(dr, right, ref, ALU.subtract).then_inc(X["D"], 1)

                def weigh(l):
                    m = CH >> l
                    w("E", LEVELS, l)
                    for a, b in zip(halves(XE[l % 2], m), (halves(kp, m)[0], halves(qp, m)[1])):
                        last = dve.tensor_tensor(a, a, b, ALU.mult)
                    last.then_inc(X["EQ"], 1)

                def keep(l):
                    dve.drain()
                    w("A", 8, l + 1)
                    dve.sem_inc(passed, 1)
                    o = 1024 * (l % 2)
                    msk = level[:, l - 1, :].rearrange("p (a t) -> p a t", a=1).to_broadcast([P, NCH, P]).bitcast(U32)
                    dve.copy_predicated(am3, msk, flat[:, o:o + LP].rearrange("p (c t) -> p c t", c=NCH)
                                        ).then_inc(X["am"], 1)
                dve.drain()
                diff(1)
                for l in range(1, LEVELS + 1):
                    if l < LEVELS:
                        diff(l + 1)
                    weigh(l)
                    if l >= 2:
                        keep(l - 1)
                keep(LEVELS)
                w("st", 1, 1)
                dve.tensor_copy(S[:, 0, :], ps[:, 5, 0:P])
                for c in range(1, 4):
                    dve.drain()
                    last = dve.scalar_tensor_tensor(S[:, c, :], S[:, c - 1, :], GL[:, c:c + 1],
                                                    ps[:, 5, c * P:(c + 1) * P], ALU.mult, ALU.add)
                last.then_inc(X["S"], 1)
                w("or", 1, 1)
                g = vecs[:, VEC["hg_out"]:VEC["hg_out"] + 1]
                o = flat[:, 3072 + LEAD:3072 + LP]
                dve.scalar_tensor_tensor(TB[:, :], o, g, TB[:, :], ALU.mult, ALU.mult)
                dve.drain()
                dve.tensor_tensor(TB[:, :], TB[:, :], z(16), ALU.mult).then_inc(X["og"], 1)
                w("oh", 1, 1)
                u1 = UH[:, bass.ds(h, 1), :].rearrange("p a t -> p (a t)").bitcast(F32)
                dve.tensor_tensor(UL[:, bass.ds(h, 1), :].rearrange("p a t -> p (a t)"), TB[:, :], u1,
                                  ALU.subtract).then_inc(X["end"], 1)

            dve.wait_ge(X["silu"], 2)
            with dve.Fori(0, HEADS) as h:
                hgrn(h)
            for x in range(4):
                g = VEC["cq"] + x
                dve.wait_ge(M["chi"], x + 1)
                dve.scalar_tensor_tensor(CLO[:, x, :], Z[:, x, :], vecs[:, g:g + 1], CHI[:, x, :].bitcast(F32),
                                         ALU.mult, ALU.subtract).then_inc(M["c"], 1)
            t = TILE0["qup"]
            dve.wait_ge(M["r"], 1)
            for h in range(HEADS):
                scaled(t, L, tok(QN[:, h, :], L), R2)
                scaled(t + 1, L, tok(QR[:, h, :], L), R2, m=ROPE)
                t += 2
            dve.wait_ge(M["r"], 2)
            for h in range(HEADS):
                scaled(t, L, tok(KN[:, h, :], L), R[1])
                scaled(t + 1, L, tok(V[:, h, :], L), R[1])
                t += 2
            dve.drain()
            dve.wait_ge(rope_in, 16)

            def attend(h):
                def w(name, per, c):
                    dve.wait_ge(M[name], h * per + c)

                def row(a):
                    return a[:, bass.ds(h, 1), :].rearrange("p a t -> p (a t)")

                def gain(n):
                    return vecs[:, VEC[n]:VEC[n] + 1]
                dve.tensor_copy(vs[:, :], row(V)).then_inc(M["vs"], 1)
                for x, (a, b, r, gn, gr, d, dr) in enumerate(((row(QN), row(QR), rq, "qn", "qr", qs, qrs),
                                                              (row(KN), KR[:, :], rk, "kn", "kr", ks, krs))):
                    if x:
                        dve.drain()
                    w("rr", 2, x + 1)
                    dve.scalar_tensor_tensor(tr[:, :], b, gain(gr)[0:ROPE], r[0:ROPE, :], ALU.mult, ALU.mult
                                             ).then_inc(M["x"], 1)
                    dve.scalar_tensor_tensor(d[:, :], a, gain(gn), r[:, :], ALU.mult, ALU.mult)
                    dve.drain()
                    dve.tensor_tensor(cr[:, :], tr[:, :], TAB[:, 0, :], ALU.mult)
                    w("turn", 2, x + 1)
                    dve.tensor_tensor(tok(sr[:, :], L), ps[0:ROPE, 2 * x:2 * x + 2, 0:HALF], tok(TAB[:, 1, :], L),
                                      ALU.mult)
                    dve.drain()
                    dve.tensor_tensor(dr[:, :], cr[:, :], sr[:, :], ALU.add).then_inc(M["s"], 1)

                def top(j):
                    n, nk = (META, META) if j == 0 else (P, META + j * P)
                    w("sc", 5, j + 1)
                    o = 1024 * (j % 2)
                    dve.tensor_reduce(stat[0:n, j:j + 1], flat[0:n, o:o + nk], AXX, ALU.max)
                    dve.drain()
                    dve.tensor_scalar(stat[0:n, j:j + 1], stat[0:n, j:j + 1], -QK ** -0.5, None, ALU.mult
                                      ).then_inc(M["max"], 1)

                def share(j):
                    n, nk = (META, META) if j == 0 else (P, META + j * P)
                    w("exp", 5, j + 1)
                    dve.reciprocal(stat[0:n, 8 + j:9 + j], stat[0:n, 8 + j:9 + j])
                    dve.drain()
                    dve.tensor_scalar(PP[j % 2][0:n, 0:nk], PP[j % 2][0:n, 0:nk], stat[0:n, 8 + j:9 + j], None,
                                      ALU.mult).then_inc(M["p"], 1)
                top(0)
                for j in range(5):
                    if j + 1 < 5:
                        top(j + 1)
                    share(j)
                w("oh", 1, 1)
                uh = UH[:, bass.ds(4 + h, 1), :].rearrange("p a t -> p (a t)").bitcast(F32)
                ul = UL[:, bass.ds(4 + h, 1), :].rearrange("p a t -> p (a t)")
                dve.tensor_tensor(ul[:, 0:META], flat[:, 3584:3584 + META], uh[:, 0:META], ALU.subtract)
                dve.tensor_tensor(ul[:, META:L], flat[:, 3072:3584], uh[:, META:L], ALU.subtract).then_inc(M["end"], 1)

            with dve.Fori(0, HEADS) as h:
                attend(h)
            for e in range(KT):
                t = TILE0["wout"] + e
                dve.wait_ge(tile_done, t + 1)
                dve.tensor_tensor(tok(H[:, e, :], L), psum(t, L), tok(H[:, e, :], L), ALU.add).then_inc(evac[t % 2], 1)
            for e in range(KT):
                lo(1, e, "mlp0")

            def mlp(layer, n, m, split):
                r = R[(m - 1) % 2][:, :]
                dve.wait_ge(r_ready, m)
                dve.tensor_tensor(tok(R2[:, :], n), tok(r, n), tok(r, n), ALU.mult)
                dve.drain()

                def quarter(q, base, last):
                    def square(j):
                        dve.drain()
                        dve.wait_ge(evac[(b + j) % 2], 8 * (q - FQ * layer) + (b + j) // 2 + 1)
                        a = tok(RL[j % 2][:, :], n)
                        dve.tensor_tensor(tok(SB[j % 2][:, :], n), a, a, ALU.mult).then_inc(relu2_done, 1)

                    def part(j):
                        dve.wait_ge(hh_done, 8 * q + j + 1)
                        dve.tensor_tensor(tok(HL[:, j, :], n), tok(SB[j % 2][:, :], n), tok(HH[:, j, :], n).bitcast(F32),
                                          ALU.subtract).then_inc(hid_done, 1)
                    square(0)
                    for j in range(8):
                        if j + 1 < 8:
                            square(j + 1)
                        part(j)
                    for e in range(8):
                        dve.wait_ge(tile_done, base + 8 + e + 1)
                        a, he = tok(TD[e % 2][:, :], n), tok(H[:, e, :], n)
                        dve.tensor_tensor(a, psum(b + e, n), tok(R2[:, :], n), ALU.mult
                                          ).then_inc(evac[(b + e) % 2], 1)
                        dve.drain()
                        x = dve.tensor_tensor(he, he, a, ALU.add)
                        if last:
                            x.then_inc(h_final, 1)
                            if split and e:
                                lo(*split(e - 1))
                b = TILE0["mlp%d" % layer]
                with dve.Fori(0, FQ - 1) as i:
                    quarter(i + FQ * layer, i * 16 + b, False)
                quarter(FQ * layer + FQ - 1, b + 16 * (FQ - 1), True)
                if split:
                    lo(*split(7))
            mlp(0, L, 2, None)
            for k in range(KT):
                g = VEC["mem"] + k
                dve.wait_ge(N["mem_hi"], k + 1)
                dve.scalar_tensor_tensor(ML[:, k, :], MEM[:, k, :], vecs[:, g:g + 1], MH[:, k, :].bitcast(F32), ALU.mult,
                                         ALU.subtract).then_inc(N["mem_lo"], 1)
            dve.wait_ge(r_ready, 3)
            for k in range(KT):
                g = VEC["mix1"] + k
                dve.scalar_tensor_tensor(UX[:, k, :], H[:, k, :], vecs[:, g:g + 1], R[0][:, :], ALU.mult, ALU.mult)
            dve.wait_ge(N["mem_r"], 1)

            def pool_lo(g):
                for c in range(2):
                    k = 2 * g + c
                    dve.wait_ge(uh_done, 16 + k + 1)
                    dve.tensor_tensor(UL[:, k, META:L], DD[g % 2][:, c, META:L], UH[:, k, META:L].bitcast(F32),
                                      ALU.subtract).then_inc(u_done, 1)
            for g in range(4):
                cur, a, s_ = UX[:, 2 * g:2 * g + 2, :], 0, 1
                for x in range(g + 1):
                    nxt = (W0, W1)[x % 2]
                    a += s_
                    dve.drain()
                    dve.tensor_tensor(nxt[:, :, a:L], cur[:, :, a:L], cur[:, :, a - s_:L - s_], ALU.add)
                    cur, s_ = nxt, 2 * s_
                dve.drain()
                dve.scalar_tensor_tensor(DD[g % 2][:, :, META:L], cur[:, :, META:L], 1.0 / s_,
                                         UX[:, 2 * g:2 * g + 2, META:L], ALU.mult, ALU.subtract).then_inc(N["dd"], 1)
                for x in (2 * g, 2 * g + 1):
                    t = TILE0["memkv"] + x
                    d = KM[:, x, :] if x < HEADS else VM[:, x - HEADS, :]
                    dve.wait_ge(tile_done, t + 1)
                    dve.tensor_tensor(d, psum(t, NMEM), RM[:, :], ALU.mult).then_inc(evac[t % 2], 1)
                if g:
                    pool_lo(g - 1)
            pool_lo(3)
            for e in range(KT):
                t, g = TILE0["pool"] + e, VEC["pool"] + e
                dve.wait_ge(tile_done, t + 1)
                he = tok(H[:, e, :], SEQ)
                dve.scalar_tensor_tensor(he, psum(t, SEQ), vecs[:, g:g + 1], he, ALU.mult, ALU.add
                                         ).then_inc(evac[t % 2], 1)
                if e % 2:
                    for x in (e - 1, e):
                        lo(3, x, "mlp1")
            mlp(1, SEQ, 4, lambda e: (4, e, "pre_mix"))
            for x in range(2):
                dve.memset(XP[x][:, 0:CONV - 1], 0.0)
            dve.wait_ge(r_ready, 5)
            dve.drain()
            with dve.Fori(0, 6) as i:
                for j in range(4):
                    t = TILE0["gin"] + j
                    dve.wait_ge(tile_done, 4 * i + t + 1)
                    xp, ca = XP[j % 2], CA[j % 2]
                    dve.tensor_tensor(xp[:, 3:3 + SEQ], psum(t, SEQ), R[0][:, META:L], ALU.mult).then_inc(evac[t % 2], 1)
                    dve.drain()
                    if j >= 2:
                        dve.wait_ge(N["conv_silu"], 4 * i + j - 1)
                    else:
                        dve.wait_ge(N["conv_silu"], 4 * i)
                    for n in range(CONV - 1, -1, -1):
                        tap = vecs[:, bass.ds(VEC["conv"] + CONV * (4 * i + j) + n, 1)]
                        if n < CONV - 1:
                            dve.drain()
                        if n == CONV - 1:
                            dve.tensor_scalar(ca[:, :], xp[:, n:n + SEQ], tap, None, ALU.mult)
                        else:
                            last = dve.scalar_tensor_tensor(ca[:, :], xp[:, n:n + SEQ], tap, ca[:, :], ALU.mult, ALU.add)
                    last.then_inc(N["conv"], 1)
            with dve.Fori(0, 3) as i:
                for j in range(4):
                    t = TILE0["gin"] + 24 + j
                    dve.wait_ge(tile_done, 4 * i + t + 1)
                    dve.tensor_tensor(ZQ[:, bass.ds(4 * i + j, 1), :].rearrange("p a t -> p (a t)"), psum(t, SEQ),
                                      R[0][:, META:L], ALU.mult).then_inc(evac[t % 2], 1)
            dve.wait_ge(N["rt"], 1)
            dve.tensor_copy(SC[:, 0, 0:4], ps[:, 7, 64:68])
            dve.drain()
            for c in range(4):
                dve.tensor_scalar(AB[:, 1:3, 8 * c:8 * c + 8], ps[:, 7, 16 * c:16 * c + 16].rearrange("p (a h) -> p a h", a=2),
                                  SC[:, 0, c:c + 1], None, ALU.mult)
            dve.drain()

            def by_chunk(ap):
                return ap.rearrange("p (c h) -> p c h", c=4)

            def each_chunk(ap):
                return ap.rearrange("p (c h) -> p c h", c=1).to_broadcast([P, 4, 8])
            dve.tensor_tensor(by_chunk(AB[:, 1, :]), by_chunk(AB[:, 1, :]),
                              each_chunk(vecs[:, VEC["dtb"]:VEC["dtb"] + 8]), ALU.add).then_inc(N["ab_x"], 1)
            dve.wait_ge(N["ab_ln"], 1)
            dve.drain()
            dve.scalar_tensor_tensor(AB[:, 3, :], AB[:, 1, :], 0.0, AB[:, 3, :], ALU.max, ALU.add)
            dve.scalar_tensor_tensor(SCAL[:, 1, :], AB[:, 2, :], 0.0, AB[:, 4, :], ALU.min, ALU.subtract)
            dve.drain()
            dve.scalar_tensor_tensor(by_chunk(AB[:, 0, :]), by_chunk(AB[:, 3, :]), -1.0, each_chunk(AB[:, 5, 0:8]),
                                     ALU.mult, ALU.mult).then_inc(N["ab_g"], 1)
            dve.drain()
            dve.tensor_copy(SCAL[:, 0, :], AB[:, 0, :])
            dve.wait_ge(N["ab_exp"], 1)
            dve.tensor_scalar(SCAL[:, 2, :], SCAL[:, 2, :], -1.0, None, ALU.mult)
            dve.tensor_copy(SCAL[:, 3, :], ps[:, 7, 128:160])
            dve.drain()
            dve.tensor_tensor(SCAL[:, 4, :], ps[:, 7, 160:192], SCAL[:, 3, :], ALU.subtract).then_inc(N["ab_x"], 1)

            def recall(h):
                def w(name, c):
                    dve.wait_ge(N[name], h + c)
                w("ma_s", 1)
                dve.tensor_reduce(am_s[:, 8:12], ps[:, 0:2, :].rearrange("p b (c k) -> p (b c) k", c=2), AXX, ALU.max)
                dve.drain()
                dve.tensor_scalar(am_s[:, 0:4], am_s[:, 8:12], -P ** -0.5, None, ALU.mult).then_inc(N["ma_max"], 1)
                w("ma_exp", 1)
                dve.reciprocal(am_s[:, 12:16], am_s[:, 4:8])
                dve.drain()
                dve.tensor_tensor(am_p[:, :, :], am_p[:, :, :],
                                  am_s[:, 12:16].rearrange("p (c k) -> p c k", k=1).to_broadcast([P, 4, NMEM]), ALU.mult
                                  ).then_inc(N["ma_p"], 1)
            with dve.Fori(0, HEADS) as h:
                recall(h)
            dve.wait_ge(N["ab_all"], 1)
            dve.wait_ge(N["ma_end"], HEADS)
            dve.wait_ge(N["mem_vtc"], 1)
            dve.memset(ST8[:, :, :], 0.0)

            def chunk(c):
                def w(name, k, per=1):
                    dve.wait_ge(G[name], c * 2 * per + k)

                def bank(g, b):
                    return ps[:, 4 * g + b, :].rearrange("p (x t) -> p x t", x=4)

                def four(m):
                    return m.rearrange("p (a t) -> p a t", a=1).to_broadcast([P, 4, P])

                def sc(row, g, x):
                    return SC[:, row, 4 * g + x:4 * g + x + 1]
                cols = bass.ds(c * P, P)
                dve.drain()
                dve.tensor_copy(SC[:, :, :], SCAL[:, :, bass.ds(8 * c, 8)])
                dve.drain()
                for g in range(2):
                    w("rs", g + 1)
                    dve.tensor_copy(G2["PT"][g][:, :, :], QKV[:, 16 + 4 * g:20 + 4 * g, cols])
                    dve.scalar_tensor_tensor(G2["qn"][g][:, :, :], QKV[:, 4 * g:4 * g + 4, cols], P ** -0.5,
                                             G2["U"][g][:, :, :], ALU.mult, ALU.mult)
                    dve.tensor_tensor(G2["kn"][g][:, :, :], QKV[:, 8 + 4 * g:12 + 4 * g, cols], G2["LT"][g][:, :, :],
                                      ALU.mult).then_inc(G["nrm"], 1)
                for g in range(2):
                    w("eg", g + 1)
                    for x in range(4):
                        last = dve.tensor_scalar(G2["T"][g][:, x, :], ps[:, 4 * g + 2, x * P:(x + 1) * P], sc(3, g, x), 0.0,
                                                 ALU.subtract, ALU.min)
                    last.then_inc(G["d"], 1)
                for g in range(2):
                    w("dec", g + 1)
                    dve.tensor_tensor(G2["T"][g][:, :, :], G2["T"][g][:, :, :], four(upper), ALU.mult)
                    dve.drain()
                    w("kk", g + 1)
                    for x in range(4):
                        dve.scalar_tensor_tensor(G2["LT"][g][:, x, :], ps[:, 4 * g, x * P:(x + 1) * P], sc(1, g, x),
                                                 G2["T"][g][:, x, :], ALU.mult, ALU.mult)
                    dve.tensor_tensor(G2["qn"][g][:, :, :], G2["qn"][g][:, :, :], G2["U"][g][:, :, :], ALU.mult)
                    w("tr", g + 1)
                    dve.tensor_tensor(G2["PT"][g][:, :, :], bank(g, 1), G2["T"][g][:, :, :], ALU.mult
                                      ).then_inc(G["lt"], 1)
                    dve.drain()
                    dve.tensor_tensor(G2["LM"][g][:, :, :], G2["LT"][g][:, :, :], four(level[:, LEVELS - 1, :]), ALU.mult
                                      ).then_inc(G["lm"], 1)
                    dve.drain()
                    dve.tensor_tensor(G2["U"][g][:, :, :], four(ident), G2["LM"][g][:, :, :], ALU.subtract)
                for g in range(2):
                    w("a", g + 1, LEVELS)
                    dve.tensor_tensor(G2["T"][g][:, :, :], four(ident), bank(g, 0), ALU.subtract).then_inc(G["u"], 1)
                    dve.drain()
                    dve.tensor_tensor(G2["LM"][g][:, :, :], G2["LT"][g][:, :, :], four(level[:, LEVELS - 2, :]), ALU.mult
                                      ).then_inc(G["lm"], 1)
                for l in range(1, LEVELS):
                    for g in range(2):
                        if l < LEVELS - 1:
                            dve.drain()
                            w("a", 2 * l + g + 1, LEVELS)
                            dve.tensor_tensor(G2["LM"][g][:, :, :], G2["LT"][g][:, :, :],
                                              four(level[:, LEVELS - 2 - l, :]), ALU.mult).then_inc(G["lm"], 1)
                        dve.drain()
                        w("p", 2 * (l - 1) + g + 1, LEVELS - 1)
                        if l < LEVELS - 1:
                            dve.tensor_tensor(G2["T"][g][:, :, :], G2["T"][g][:, :, :], bank(g, 1), ALU.subtract)
                        dve.tensor_tensor(G2["U"][g][:, :, :], G2["U"][g][:, :, :], bank(g, 2), ALU.subtract
                                          ).then_inc(G["u"], 1)
                for g in range(2):
                    dve.drain()
                    w("ks", g + 1)
                    for x in range(4):
                        last = dve.scalar_tensor_tensor(G2["LM"][g][:, x, :], ps[:, 4 * g, x * P:(x + 1) * P], sc(2, g, x),
                                                        G2["vt"][g][:, x, :], ALU.mult, ALU.add)
                    last.then_inc(G["r"], 1)
                for g in range(2):
                    dve.drain()
                    w("o", g + 1)
                    for x in range(4):
                        last = dve.scalar_tensor_tensor(ST8[:, 4 * g + x, :], ST8[:, 4 * g + x, :], sc(5, g, x),
                                                        ps[:, 4 * g + 3, x * P:(x + 1) * P], ALU.mult, ALU.add)
                    last.then_inc(G["s"], 1)
            with dve.Fori(0, 4) as c:
                chunk(c)
            for h in range(HEADS):
                dve.wait_ge(N["om_hi"], h + 1)
                dve.tensor_tensor(OML[:, h, META:L], ZQ[:, 8 + h, :], OMH[:, h, META:L].bitcast(F32), ALU.subtract
                                  ).then_inc(N["om_lo"], 1)

            def head_lo(h):
                dve.wait_ge(uh_done, 40 + h + 1)
                dve.tensor_tensor(UL[:, h, META:L], GT[h % 2][:, META:L], UH[:, h, META:L].bitcast(F32), ALU.subtract
                                  ).then_inc(u_done, 1)
            for h in range(GH):
                dve.wait_ge(N["g_r"], h + 1)
                dve.drain()
                a = GT[h % 2][:, META:L]
                dve.scalar_tensor_tensor(a, QKV[:, h, :], vecs[:, VEC["gdn_out"]:VEC["gdn_out"] + 1],
                                         GR[h % 2][:, META:L], ALU.mult, ALU.mult)
                dve.drain()
                dve.tensor_tensor(a, a, ZQ[:, h, :], ALU.mult).then_inc(N["g_t"], 1)
                if h:
                    head_lo(h - 1)
            head_lo(GH - 1)
            dve.wait_ge(r_ready, 6)
            for e in range(KT):
                g = VEC["post_mix"] + e
                he, a = H[:, e, META:L], SB[e % 2][:, META:L]
                dve.drain()
                dve.scalar_tensor_tensor(a, Y[:, e, META:L], vecs[:, g:g + 1], R[1][:, META:L], ALU.mult, ALU.mult)
                dve.drain()
                dve.tensor_tensor(he, he, a, ALU.add).then_inc(h_final, 1)
                if e:
                    lo(6, e - 1, "pre_ffn")
            lo(6, 7, "pre_ffn")
            dve.wait_ge(r_ready, 7)

            def f_lo(a, j):
                dve.wait_ge(N["f_hh"], 11 * a + j + 1)
                dve.tensor_tensor(FL[:, j, META:L], GC[j % 2][:, META:L], FH[:, j, META:L].bitcast(F32), ALU.subtract
                                  ).then_inc(N["f_hid"], 1)
            for a in range(2):
                b = TILE0["ffn"] + 30 * a
                for j in range(11):
                    if j >= 2:
                        dve.wait_ge(N["f_silu"], 11 * a + j - 1)
                    dve.wait_ge(tile_done, b + 2 * j + 1)
                    dve.tensor_tensor(GA[j % 2][:, META:L], psum(b, SEQ), R[0][:, META:L], ALU.mult
                                      ).then_inc(evac[b % 2], 1)
                    if j:
                        f_lo(a, j - 1)
                    dve.wait_ge(tile_done, b + 2 * j + 2)
                    dve.wait_ge(N["f_silu"], 11 * a + j + 1)
                    dve.drain()
                    dve.tensor_tensor(GC[j % 2][:, META:L], psum(b + 1, SEQ), GS[j % 2][:, META:L], ALU.mult
                                      ).then_inc(evac[(b + 1) % 2], 1)
                f_lo(a, 10)
                for e in range(KT):
                    t = b + 22 + e
                    dve.wait_ge(tile_done, t + 1)
                    if a == 0:
                        dve.tensor_tensor(FO[:, e, META:L], psum(t, SEQ), R[0][:, META:L], ALU.mult
                                          ).then_inc(evac[t % 2], 1)
                    else:
                        x = GA[e % 2][:, META:L]
                        dve.drain()
                        dve.tensor_tensor(x, psum(t, SEQ), R[0][:, META:L], ALU.mult).then_inc(evac[t % 2], 1)
                        dve.drain()
                        dve.tensor_tensor(FO[:, e, META:L], FO[:, e, META:L], x, ALU.add).then_inc(h_final, 1)
            dve.wait_ge(r_ready, 8)
            for e in range(KT):
                g = VEC["post_ffn"] + e
                x, he = GA[e % 2][:, META:L], H[:, e, META:L]
                dve.drain()
                dve.scalar_tensor_tensor(x, FO[:, e, META:L], vecs[:, g:g + 1], R[1][:, META:L], ALU.mult, ALU.mult)
                dve.drain()
                dve.tensor_tensor(he, he, x, ALU.add).then_inc(N["y_out"], 1)


def constants():
    s = np.arange(P)[:, None]
    t = np.arange(P)[None, :]
    masks = []
    for l in range(1, LEVELS + 1):
        m = CH >> l
        masks.append((s // (2 * m) == t // (2 * m)) & (s % (2 * m) < m) & (t % (2 * m) >= m))
    half = ROPE // 2
    turn = np.where(t == s - half, -1.0, 0.0) * (s < ROPE) + np.where(t == s + half, 1.0, 0.0) * (t < ROPE)
    early = np.where(t < 64, BIG, 0.0)
    masks += [s == t, s <= t, s >= 0, turn, early]
    return np.ascontiguousarray(np.stack([np.broadcast_to(x, (P, P)) for x in masks], 1).astype(np.float32))


def rope_table():
    half = ROPE // 2
    inv = (np.float32(10000.0) ** (-np.arange(half, dtype=np.float32) / np.float32(half))).astype(np.float32)
    ang = np.arange(L, dtype=np.float32)[None, :] * inv[:, None]
    c, s = np.cos(ang), np.sin(ang)
    return np.ascontiguousarray(np.stack([np.concatenate([c, c]), np.concatenate([s, s])], 1).astype(np.float32))


def pack(i):
    blocks = []

    def put(w, cols, kt=None):
        w = np.asarray(w)
        for c in cols:
            for k in range(w.shape[0] // P) if kt is None else kt:
                b = np.zeros((P, P), np.float32)
                part = w[k * P:(k + 1) * P, c:c + P]
                b[:, 0:part.shape[1]] = part
                blocks.append(b)

    def halves(w, c, width):
        w = np.asarray(w)
        n = P // width
        for k in range(0, w.shape[0] // P, n):
            b = np.zeros((P, P), np.float32)
            for j in range(min(n, w.shape[0] // P - k)):
                b[:, j * width:(j + 1) * width] = w[(k + j) * P:(k + j + 1) * P, c:c + width]
            blocks.append(b)

    win = i["w_in"][0]
    put(win, [2048 + P * j for j in range(4)] + [P * j for j in range(16)])
    halves(win, 2560, ROPE)
    for h in range(HEADS):
        put(i["w_q_up"][0], [h * QK])
        halves(i["w_q_up"][0], h * QK + NOPE, ROPE)
    put(i["w_kv_up"][0], [P * j for j in range(8)])
    put(i["w_out"][0], [P * j for j in range(8)])

    def mlp(layer):
        for q in range(FQ):
            put(i["w_mlp_up"][layer], [P * (8 * q + j) for j in range(8)])
            put(i["w_mlp_down"][layer], [P * e for e in range(8)], range(8 * q, 8 * q + 8))
    mlp(0)
    put(i["w_mem_kv_2"][0], [P * j for j in range(8)])
    for g in range(4):
        put(i["pool_w"][0][g], [0, P])
    mlp(1)
    gin = i["gdn_w_in_2"][0]
    put(gin, [P * j for j in range(32)] + [4112 + P * j for j in range(4)])
    halves(gin, 4096, 16)
    blocks.extend([np.zeros((P, P), np.float32)] * 15)
    put(i["w_out_2"][0], [P * j for j in range(8)])
    for a in range(2):
        for j in range(11):
            put(i["w_ffn_in_2"][0], [P * (11 * a + j), P * (FF2 + 11 * a + j)])
        put(i["w_ffn_out_2"][0], [P * e for e in range(8)], range(11 * a, 11 * a + 11))
    assert len(blocks) == NBLOCKS, (len(blocks), NBLOCKS)
    w = np.stack(blocks).reshape(NSLOTS, SLOT, P, P).transpose(0, 2, 1, 3)
    return np.ascontiguousarray(w)


def vectors(i):
    v = np.zeros((P, NVEC), np.float32)

    def put(name, a):
        a = np.asarray(a)
        a = a.reshape(-1, P).T
        v[:, VEC[name]:VEC[name] + a.shape[1]] = a
    put("mix0", i["mix_norm"][0]); put("mix1", i["mix_norm"][1])
    put("mlp0", i["mlp_norm"][0]); put("mlp1", i["mlp_norm"][1])
    put("hg_out", i["hgrn_out_norm"][0]); put("cq", i["mla_q_a_norm"][0]); put("ckv", i["mla_kv_a_norm"][0])
    put("qn", i["q_norm"][0][:NOPE]); put("kn", i["k_norm"][0][:NOPE])
    v[:ROPE, VEC["qr"]] = i["q_norm"][0][NOPE:]
    v[:ROPE, VEC["kr"]] = i["k_norm"][0][NOPE:]
    put("pool", i["pool_scale"][0]); put("mem", i["mem_norm_2"]); put("pre_mix", i["norm_pre_mix_2"][0])
    put("post_mix", i["norm_post_mix_2"][0]); put("pre_ffn", i["norm_pre_ffn_2"][0])
    put("post_ffn", i["norm_post_ffn_2"][0]); put("gdn_out", i["gdn_out_norm_2"][0])
    v[:, VEC["alog"]:VEC["alog"] + 8] = i["gdn_a_log_2"][0][None]
    v[:, VEC["dtb"]:VEC["dtb"] + 8] = i["gdn_dt_bias_2"][0][None]
    c = np.asarray(i["gdn_conv_2"][0]).reshape(CONV, 24, P).transpose(2, 1, 0)
    v[:, VEC["conv"]:VEC["conv"] + 24 * CONV] = c.reshape(P, -1)
    return v


def kernel(**inputs):
    import concourse.bacc as bacc
    import concourse.bass_utils as bass_utils

    i = {n: np.asarray(a) for n, a in inputs.items()}
    x = np.concatenate([i["meta_tokens"], i["x"][0]], 0)
    arrays = {
        "xT": np.ascontiguousarray(x.T.reshape(KT, P, L).transpose(1, 0, 2)),
        "memT": np.ascontiguousarray(i["mem_2"][0].T.reshape(KT, P, NMEM).transpose(1, 0, 2)),
        "W": pack(i), "vecs": vectors(i), "masks": constants(), "rope": rope_table(),
    }
    nc = bacc.Bacc("TRN2", target_bir_lowering=False, num_devices=1)
    args = [nc.dram_tensor(n, a.shape, F32, kind="ExternalInput").ap() for n, a in arrays.items()]
    out = nc.dram_tensor("out", (P, KT, SEQ), F32, kind="ExternalOutput").ap()
    build(nc, *args, out)
    r = bass_utils.run_bass_kernel_spmd(nc, [arrays], core_ids=[0])
    y = np.asarray(r.results[0]["out"])
    return np.ascontiguousarray(y.transpose(1, 0, 2).reshape(D, SEQ).T)[None]
```

```python
import math
from contextlib import ExitStack

import concourse.bass as bass
import numpy as np
from concourse import mybir

F32 = mybir.dt.float32
LNEXP = "natural_log_exp_and_others"
FR = mybir.dt.float32r
U32 = mybir.dt.uint32
ALU = mybir.AluOpType
ACT = mybir.ActivationFunctionType
AXX = mybir.AxisListType.X

P = 128
D = 1024
KT = D // P
META = 16
SEQ = 512
L = META + SEQ
HALF = L // 2
EPS = 1e-6
FQ = 4
HEADS = 4
NOPE, ROPE, RANK = 128, 64, 256
QK = NOPE + ROPE
CH = 128
LEAD = CH - META
LP = LEAD + L
NCH = LP // CH
LEVELS = 7
NMEM = 256
GH = 8
FF2 = 2816 // P
CONV = 4
FREE = 1
SLOT = 16
BIG = -1.0e30

VEC = {}
_at = 0
for _n, _w in (("mix0", 8), ("mlp0", 8), ("mix1", 8), ("mlp1", 8), ("hg_out", 1), ("cq", 2), ("ckv", 2),
               ("qn", 1), ("qr", 1), ("kn", 1), ("kr", 1), ("pool", 8), ("mem", 8), ("pre_mix", 8), ("post_mix", 8),
               ("pre_ffn", 8), ("post_ffn", 8), ("gdn_out", 1), ("alog", 8), ("dtb", 8), ("conv", 24 * CONV)):
    VEC[_n] = _at
    _at += _w
NVEC = _at

STAGES = (("win", 160, 20), ("kr", 4, 1), ("qup", 12, 8), ("kvup", 16, 8), ("wout", 64, 8), ("mlp0", 512, 64),
          ("memkv", 64, 8), ("pool", 16, 8), ("mlp1", 512, 64), ("gin", 288, 36), ("wout2", 96, 8),
          ("ffn", 528, 60))
BLOCK0, TILE0 = {}, {}
_b = _t = 0
for _n, _w, _k in STAGES:
    BLOCK0[_n], TILE0[_n] = _b, _t
    _b += _w
    _t += _k
NBLOCKS = _b
NSLOTS = _b // SLOT
assert NSLOTS * SLOT == _b


def tok(ap, n):
    if n == L:
        return ap.rearrange("p (h t) -> p h t", h=2)
    return ap[:, META:L] if n == SEQ else ap[:, 0:n]


def build(nc, xT, memT, W, vecs_d, masks_d, rope_d, gates_d, out):
    ctx = ExitStack()
    with ctx:
        arena = ctx.enter_context(nc.sbuf_tensor("arena", [P, 212000 // 4], F32))
        base = [16512]
        del arena

        def at(name, shape, dt, offset):
            n = int(np.prod(shape[1:])) * 4
            assert offset % 32 == 0 and offset + n <= 16512 + 212000, (name, offset + n)
            return nc.alloc_sbuf_tensor_at(name, shape, dt, offset=offset), offset + n

        def place(name, shape, dt):
            t, end = at(name, shape, dt, base[0])
            base[0] = (end + 31) // 32 * 32
            return t

        def region(start, *items):
            got, off = [], start
            for name, shape, dt in items:
                t, end = at(name, shape, dt, off)
                off = (end + 31) // 32 * 32
                got.append(t)
            return got

        raw = [place(f"raw{c}", [P, SLOT, P], F32) for c in range(2)]
        whi = [place(f"whi{c}", [P, SLOT, P], FR) for c in range(2)]
        wlo = [place(f"wlo{c}", [P, SLOT, P], FR) for c in range(2)]
        H = place("H", [P, KT, L], F32)
        u_at = base[0]
        UH = place("UH", [P, KT, L], FR)
        UL = place("UL", [P, KT, L], FR)
        R = [place(f"R{c}", [P, L], F32) for c in range(2)]
        SQ = [place(f"SQ{c}", [P, L], F32) for c in range(2)]
        R2 = place("R2", [P, L], F32)
        L2R = [R[1], R2]
        vecs = place("vecs", [P, NVEC], F32)
        masks = place("masks", [P, LEVELS + 5, P], F32)
        zero = place("zero", [P, 1], F32)
        eps = place("eps", [P, 1], F32)
        S0 = base[0]
        level = masks[:, 0:LEVELS, :]
        ident = masks[:, LEVELS, :]
        upper = masks[:, LEVELS + 1, :]
        ones = masks[:, LEVELS + 2, :]
        turn = masks[0:ROPE, LEVELS + 3, 0:ROPE]
        early = masks[0:1, LEVELS + 4, :]

        Z, = region(S0, ("Z", [P, 20, L], F32))
        hw = S0 + 20 * L * 4
        (qp, kp, vp, lf, bb, qb, kd, XD0, XD1, XE0, XE1, am, kdT, vT, S, TA, TB, GL) = region(
            hw, ("qp", [P, LP], F32), ("kp", [P, LP], F32), ("vp", [P, LP], F32), ("lf", [P, LP], F32),
            ("bb", [P, LP], F32), ("qb", [P, LP], F32), ("kd", [P, LP], F32), ("XD0", [P, LP], F32),
            ("XD1", [P, LP], F32), ("XE0", [P, LP], F32), ("XE1", [P, LP], F32), ("am", [P, LP], F32),
            ("kdT", [P, 4, P], F32), ("vT", [P, NCH, P], F32), ("S", [P, 4, P], F32), ("TA", [P, L], F32),
            ("TB", [P, L], F32), ("GL", [P, 8], F32))
        XD, XE = [XD0, XD1], [XE0, XE1]
        KR, TAB = region((16512 + 212000 - 3 * 2112 - 96) // 32 * 32, ("KR", [ROPE, L], F32), ("TAB", [ROPE, 2, L], F32))
        mw = S0 + 4 * L * 4
        CHI, CLO, QN, KN, V, QR = region(
            mw, ("CHI", [P, 4, L], FR), ("CLO", [P, 4, L], FR), ("QN", [P, HEADS, L], F32),
            ("KN", [P, HEADS, L], F32), ("V", [P, HEADS, L], F32), ("QR", [ROPE, HEADS, L], F32))
        TD0, TD1 = region(S0 + 16 * L * 4 + 4 * L * 4, ("TD0", [P, L], F32), ("TD1", [P, L], F32))
        TD = [TD0, TD1]
        PP0, PP1, PT0, PT1 = region(
            mw, ("PP0", [P, L], F32), ("PP1", [P, L], F32), ("PT0", [P, 5, P], F32), ("PT1", [P, 5, P], F32))
        PP, PT = [PP0, PP1], [PT0, PT1]
        RB0, RB1, SR0, SR1, KSQ, KRP, SN, VT, stat, KRS = region(
            mw + 24 * L * 4, ("RB0", [P, L], F32), ("RB1", [P, L], F32), ("SR0", [ROPE, L], F32),
            ("SR1", [ROPE, L], F32), ("KSQ", [ROPE, L], F32), ("KRP", [ROPE, L], F32), ("SN", [ROPE, L], F32),
            ("VT", [P, 5, P], F32), ("stat", [P, 16], F32), ("KRS", [ROPE, HEADS, L], F32))
        RB, SR = [RB0, RB1], [SR0, SR1]

        HH, HL, RL0, RL1, SB0, SB1 = region(
            S0, ("HH", [P, 8, L], FR), ("HL", [P, 8, L], FR), ("RL0", [P, L], F32), ("RL1", [P, L], F32),
            ("SB0", [P, L], F32), ("SB1", [P, L], F32))
        RL, SB = [RL0, RL1], [SB0, SB1]

        UX, W0, W1, DD0, DD1 = region(S0, ("UX", [P, KT, L], F32), ("W0", [P, 2, L], F32), ("W1", [P, 2, L], F32),
                                      ("DD0", [P, 2, L], F32), ("DD1", [P, 2, L], F32))
        DD = [DD0, DD1]
        END = (16512 + 212000) // 32 * 32
        KM, VMT = region(END - 8192, ("KM", [P, HEADS, NMEM], F32), ("VMT", [P, 2, 512], F32))
        ABW, ABH, ABL = region(END - 8192 - 1536, ("ABW", [P, KT, 16], F32), ("ABH", [P, KT, 16], FR),
                               ("ABL", [P, KT, 16], FR))
        MEM, MSQ, MH, ML, RM, VM = region(
            END - 8192 - 1536 - 4 * 8192 - 1024 - 4096, ("MEM", [P, KT, NMEM], F32), ("MSQ", [P, KT, NMEM], F32),
            ("MH", [P, KT, NMEM], FR), ("ML", [P, KT, NMEM], FR), ("RM", [P, NMEM], F32), ("VM", [P, HEADS, NMEM], F32))
        QKV, ZQ, XP0, XP1, CA0, CA1, AB, SCAL, SC, GN = region(
            S0, ("QKV", [P, 24, SEQ], F32), ("ZQ", [P, 12, SEQ], F32), ("XP0", [P, SEQ + 4], F32),
            ("XP1", [P, SEQ + 4], F32), ("CA0", [P, SEQ], F32), ("CA1", [P, SEQ], F32), ("AB", [P, 6, 32], F32),
            ("SCAL", [P, 6, 32], F32), ("SC", [P, 6, 8], F32), ("GN", [P, 8], F32))
        XP, CA = [XP0, XP1], [CA0, CA1]
        g2 = ("qn", "kn", "kg", "vt", "T", "LT", "PT", "LM")
        wk = region(u_at, *[("w_%s%d" % (n, g), [P, 4, P], F32) for n in g2 for g in range(2)])
        G2 = {n: wk[2 * a:2 * a + 2] for a, n in enumerate(g2)}
        wk = region(S0 + 36 * SEQ * 4, *[("w_%s%d" % (n, g), [P, 4, P], F32) for n in ("U", "A") for g in range(2)])
        G2["U"], G2["A"] = wk[0:2], wk[2:4]
        ST8, = region(END - 8192, ("ST8", [P, GH, P], F32))
        am_p0, am_p1, am_t, am_s0, am_s1 = region(
            u_at, ("am_p0", [P, 4, NMEM], F32), ("am_p1", [P, 4, NMEM], F32), ("am_t", [P, 2, SEQ], F32),
            ("am_s0", [P, 16], F32), ("am_s1", [P, 16], F32))
        am_p, am_s = [am_p0, am_p1], [am_s0, am_s1]
        OMH, OML, GR0, GR1, GT0, GT1, Y = region(
            S0 + 8 * SEQ * 4, ("OMH", [P, HEADS, L], FR), ("OML", [P, HEADS, L], FR), ("GR0", [P, L], F32),
            ("GR1", [P, L], F32), ("GT0", [P, L], F32), ("GT1", [P, L], F32), ("Y", [P, KT, L], F32))
        GR, GT = [GR0, GR1], [GT0, GT1]
        FH, FL, FO, GA0, GA1, GS0, GS1, GC0, GC1 = region(
            S0, ("FH", [P, 11, L], FR), ("FL", [P, 11, L], FR), ("FO", [P, KT, L], F32), ("GA0", [P, L], F32),
            ("GA1", [P, L], F32), ("GS0", [P, L], F32), ("GS1", [P, L], F32), ("GC0", [P, L], F32), ("GC1", [P, L], F32))
        GA, GS, GC = [GA0, GA1], [GS0, GS1], [GC0, GC1]

        ps = ctx.enter_context(nc.psum_tensor("ps", [P, 8, 512], F32))
        flat = ps[:, :, :].rearrange("p b c -> p (b c)")

        def sem(name):
            return ctx.enter_context(nc.semaphore(name))

        raw_in = [sem(f"raw_in{c}") for c in range(2)]
        w_hi, w_lo, w_used = sem("w_hi"), sem("w_lo"), sem("w_used")
        tile_done = sem("tile_done")
        evac = [sem(f"evac{c}") for c in range(2)]
        consts_in, x_in, rope_in = sem("consts_in"), sem("x_in"), sem("rope_in")
        zero_set = sem("zero_set")
        h_final, sq_done, sq_summed, r_ready = sem("h_final"), sem("sq_done"), sem("sq_summed"), sem("r_ready")
        uh_done, u_done, r2_done = sem("uh_done"), sem("u_done"), sem("r2_done")
        relu_done, relu2_done, hh_done, hid_done = sem("relu_done"), sem("relu2_done"), sem("hh_done"), sem("hid_done")
        out_done = sem("out_done")
        passed = sem("passed")
        X = {n: sem("hg_" + n) for n in ("pad", "qp", "silu", "l", "d", "k", "v", "b", "eb", "qb", "dk", "ek", "kd", "vt", "vtc",
                                         "kt", "ktc", "st", "S", "D", "E", "EQ", "A", "am", "o", "osq", "on", "or", "og",
                                         "oh", "end")}

        M = {n: sem("mla_" + n) for n in ("qa", "kx", "kturn", "ks", "rope", "sq", "sum", "chi", "r", "c", "q", "qsum", "rr", "vt", "vtc", "x", "turn",
                                          "s", "sc", "max", "exp", "p", "t", "tc", "pv", "oh", "end")}

        N = {n: sem(n) for n in ("mem_in", "mem_sq", "mem_sum", "mem_r", "mem_hi", "mem_lo", "mem_vt", "mem_vtc", "dd",
                                 "conv", "conv_silu", "ab", "ab_row", "ab_turn", "ab_in", "ab_hi", "ab_lo", "ab_x", "ab_ln", "ab_g", "ab_cum", "ab_exp",
                                 "ab_all", "l2_sq", "l2_sum", "l2_r", "l2_done", "ma_s", "ma_max", "ma_exp", "ma_p", "ma_t", "ma_tc", "ma_o",
                                 "ma_end", "om_hi", "om_lo", "g_sum", "g_r", "g_t", "y_t", "y_sq", "f_silu", "f_hh",
                                 "f_hid", "y_out")}
        G = {n: sem("gd_" + n) for n in ("gn", "vin", "nrm", "gb", "pq", "pt", "ui", "un", "d", "eg", "dec", "kk", "tr", "kg", "lm",
                                         "a", "ac", "p", "u", "ks", "r", "vn", "vnc", "o", "oc", "s")}

        def psum(t, n, m=P):
            b = 2 * (t % 2)
            return ps[0:m, b:b + 2, 0:HALF] if n == L else ps[0:m, b, 0:n]

        def halves(ap, m):
            v = ap[:, :].rearrange("p (b s m) -> p b s m", s=2, m=m)
            return v[:, :, 0, :], v[:, :, 1, :]

        def evacuated(t):
            return evac[t % 2], t // 2 + 1 + FREE

        for group, name in ((X, ("am", "or", "S", "end")), (G, ("gb", "oc", "s", "o")), (N, ("conv_silu",))):
            group.setdefault("from_one", set()).update(name)
        M["from_one"] = set()
        from_one = [group[n] for group in (X, G, N) for n in sorted(group["from_one"])] + evac

        def count(group, name, value):
            return value + FREE if name in group["from_one"] else value

        block = ctx.enter_context(nc.Block())

        @block.sync
        def _(sp):
            sp.dma_start(raw[0][:, :, :], W[0]).then_inc(raw_in[0], 16)
            sp.dma_start(H[:, :, :], xT).then_inc(x_in, 16)
            sp.dma_start(vecs[:, :], vecs_d).then_inc(consts_in, 16)
            sp.dma_start(masks[:, :, :], masks_d).then_inc(consts_in, 16)
            sp.dma_start(raw[1][:, :, :], W[1]).then_inc(raw_in[1], 16)
            sp.dma_start(TAB[:, :, :], rope_d).then_inc(rope_in, 16)
            sp.dma_start(ABW[:, :, :], gates_d).then_inc(N["ab_in"], 16)
            with sp.Fori(1, NSLOTS // 2) as i:
                for c in range(2):
                    sp.wait_ge(w_lo, 2 * i + c - 1)
                    sp.dma_start(raw[c][:, :, :], W[bass.ds(2 * i + c, 1), :, :, :].rearrange("a p s e -> p (a s) e")
                                 ).then_inc(raw_in[c], 16)
            for s in range(NSLOTS // 2 * 2, NSLOTS):
                sp.wait_ge(w_lo, s - 1)
                sp.dma_start(raw[s % 2][:, :, :], W[s]).then_inc(raw_in[s % 2], 16)
            for k in range(KT):
                sp.wait_ge(N["y_out"], k + 1)
                sp.dma_start(out[:, k, :], H[:, k, META:L]).then_inc(out_done, 16)
            sp.wait_ge(out_done, 16 * KT)

        @block.gpsimd
        def _(pool):
            pool.memset(zero[:, :], 0.0).then_inc(zero_set, 1)
            pool.memset(eps[:, :], EPS).then_inc(zero_set, 1)
            pool.wait_ge(zero_set, 2)

            def split(c, g, first):
                src = raw[c][:, :, :].rearrange("p s e -> p (s e)")
                hi = whi[c][:, :, :].rearrange("p s e -> p (s e)")
                lo = wlo[c][:, :, :].rearrange("p s e -> p (s e)")
                pool.wait_ge(raw_in[c], 16 * g + 16)
                if not first:
                    pool.wait_ge(w_used, 2 * g + c)
                pool.tensor_tensor(hi, src, zero[:, 0:1].to_broadcast([P, SLOT * P]), ALU.add).then_inc(w_hi, 1)
                pool.wait_ge(w_hi, 2 * g + c + 1)
                pool.tensor_tensor(lo, src, hi.bitcast(F32), ALU.subtract).then_inc(w_lo, 1)

            for c in range(2):
                split(c, 0, True)
            pool.wait_ge(N["ab_in"], 16)
            pool.tensor_tensor(ABH[:, :, :], ABW[:, :, :], zero[:, 0:1].rearrange("p (a b) -> p a b", a=1
                               ).to_broadcast([P, KT, 16]), ALU.add).then_inc(N["ab_hi"], 1)
            pool.wait_ge(N["ab_hi"], 1)
            pool.tensor_tensor(ABL[:, :, :], ABW[:, :, :], ABH[:, :, :].bitcast(F32), ALU.subtract
                               ).then_inc(N["ab_lo"], 1)

            def chunk(c):
                def w(name, k, per=1):
                    pool.wait_ge(G[name], count(G, name, c * 2 * per + k))
                w("gb", 0)
                pool.tensor_copy(GN[:, :], SCAL[:, 0, bass.ds(8 * c, 8)]).then_inc(G["gn"], 1)
                w("o", 0)
                for g in range(2):
                    pool.tensor_copy(G2["PT"][g][:, :, :], QKV[:, 16 + 4 * g:20 + 4 * g, bass.ds(c * P, P)]
                                     ).then_inc(G["vin"], 1)
                for g in range(2):
                    w("eg", g + 1)
                    w("kk", g + 1)
                    qn, uu = G2["qn"][g][:, :, :], G2["U"][g][:, :, :]
                    pool.tensor_tensor(qn, qn, uu, ALU.mult)
                    pool.drain()
                    w("lm", g + 1, LEVELS)
                    pool.tensor_tensor(uu, ident.rearrange("p (a t) -> p a t", a=1).to_broadcast([P, 4, P]),
                                       G2["LM"][g][:, :, :], ALU.subtract).then_inc(G["un"], 1)
                for g in range(2):
                    w("pq", g + 1)
                    pt = G2["PT"][g][:, :, :]
                    pool.tensor_tensor(pt, pt, upper.rearrange("p (a t) -> p a t", a=1).to_broadcast([P, 4, P]),
                                       ALU.mult).then_inc(G["pt"], 1)
            def hgrn(h, more):
                def w(name, per, c, h=h):
                    pool.wait_ge(X[name], count(X, name, h * per + c))

                def z(a, h=h):
                    return Z[:, bass.ds(a + h, 1), :].rearrange("p a t -> p (a t)")

                def diff(l):
                    m = CH >> l
                    left, right = halves(bb, m)
                    ref = left[:, :, m - 1:m].to_broadcast([P, LP // (2 * m), m])
                    dl, dr = halves(XD[l % 2], m)
                    if l >= 3:
                        w("E", LEVELS, l - 2)
                    pool.tensor_tensor(dl, ref, left, ALU.subtract)
                    pool.tensor_tensor(dr, right, ref, ALU.subtract).then_inc(X["D"], 1)
                w("k", 1, 1)
                w("b", 1, 1)
                for l in range(1, LEVELS + 1):
                    diff(l)
                    if l == 4:
                        pool.drain()
                        w("eb", 1, 1)
                        pool.tensor_tensor(qb[:, P:LP], qp[:, P:LP], TB[:, 0:4 * P], ALU.mult).then_inc(X["qb"], 1)
                    if l == 5:
                        w("ek", 1, 1)
                        pool.tensor_tensor(kd[:, 0:4 * P], kp[:, 0:4 * P], kd[:, 0:4 * P], ALU.mult
                                           ).then_inc(X["kd"], 1)
                if more:
                    w("vtc", 1, 1)
                    hgrn_copies(h + 1, 0)
                    w("EQ", LEVELS, LEVELS)
                    hgrn_copies(h + 1, 1)

            def hgrn_copies(h, x):
                to, tile0, name = ((vp, 12, "v"), (qp, 4, "qp"))[x]
                pool.tensor_copy(to[:, LEAD:LP], Z[:, bass.ds(tile0 + h, 1), :].rearrange("p a t -> p (a t)")
                                 ).then_inc(X[name], 1)
            pairs = (BLOCK0["qup"] // SLOT + 2) // 2
            with pool.Fori(1, pairs) as i:
                for c in range(2):
                    split(c, i, False)
            pool.wait_ge(X["silu"], 2)
            hgrn_copies(0, 0)
            hgrn_copies(0, 1)
            with pool.Fori(0, HEADS - 1) as h:
                hgrn(h, True)
            hgrn(HEADS - 1, False)
            for y in range(2 * HEADS):
                pool.wait_ge(M["q"], y + 1)
                a = SQ[y % 2][0:ROPE, :]
                pool.tensor_tensor(a, a, (SR[y % 2] if y < HEADS else KSQ)[:, :], ALU.add).then_inc(M["qa"], 1)
            done, pairs = pairs, (BLOCK0["wout2"] // SLOT + 1) // 2
            with pool.Fori(done, pairs) as i:
                for c in range(2):
                    split(c, i, False)
            pool.wait_ge(N["ab_all"], 1)
            with pool.Fori(0, 4) as c:
                chunk(c)
            pool.wait_ge(G["oc"], count(G, "oc", 2 * 4))
            for h in range(HEADS):
                pool.tensor_tensor(OMH[:, h, META:L], ZQ[:, 8 + h, :], zero[:, 0:1].to_broadcast([P, SEQ]), ALU.add
                                   ).then_inc(N["om_hi"], 1)
                pool.wait_ge(N["om_hi"], h + 1)
                pool.tensor_tensor(OML[:, h, META:L], ZQ[:, 8 + h, :], OMH[:, h, META:L].bitcast(F32), ALU.subtract
                                   ).then_inc(N["om_lo"], 1)
            done, pairs = pairs, (BLOCK0["ffn"] // SLOT + 1) // 2
            with pool.Fori(done, pairs) as i:
                for c in range(2):
                    split(c, i, False)
            for e in range(KT):
                pool.wait_ge(N["y_t"], e + 1)
                he = H[:, e, META:L]
                pool.tensor_tensor(he, he, GT[e % 2][:, META:L], ALU.add).then_inc(h_final, 1)
            with pool.Fori(pairs, NSLOTS // 2) as i:
                for c in range(2):
                    split(c, i, False)

        @block.tensor
        def _(pe):
            class Stream:
                pos, tile, slots, tiles = 0, 0, 0, 0

            st = Stream()

            def take():
                s, b = st.pos // SLOT, st.pos % SLOT
                if b == 0:
                    pe.wait_ge(w_lo, s + 1 + st.slots)
                release = b == 0
                st.pos += 1
                return whi[s % 2][:, b, :], wlo[s % 2][:, b, :], release

            def passes(dst, wh, wl, xh, xl, start, stop_, release):
                for n, (a, b) in enumerate(((wh, xh), (wh, xl), (wl, xh))):
                    mm = pe.matmul(dst, a, b, start=start and n == 0, stop=stop_ and n == 2)
                    if release and n == 0:
                        mm.then_inc(w_used, 1)
                return mm

            def loop(n, blocks, tiles, body):
                assert blocks % (2 * SLOT) == 0 and tiles % 2 == 0
                pos, tile = st.pos, st.tile
                with pe.Fori(0, n) as i:
                    st.slots, st.tiles = i * (blocks // SLOT), i * tiles
                    body(i)
                    assert st.pos == pos + blocks and st.tile == tile + tiles
                st.slots = st.tiles = 0
                st.pos, st.tile = pos + n * blocks, tile + n * tiles

            def tile(ks, n, xh, xl, m=P, cols=None, before=None):
                t = st.tile
                pe.wait_ge(evac[t % 2], t // 2 + FREE + st.tiles // 2)
                dst = psum(t, n, m)
                for k in range(ks):
                    if before:
                        before(k)
                    wh, wl, rel = take()
                    if n == L:
                        a, b = tok(xh(k), n), tok(xl(k), n)
                        for h in range(2):
                            mm = passes(dst[:, h, :], wh[:, 0:m], wl[:, 0:m], a[:, h, :], b[:, h, :], k == 0,
                                        k == ks - 1, rel and h == 0)
                    else:
                        mm = passes(dst, wh[:, 0:m], wl[:, 0:m], tok(xh(k), n), tok(xl(k), n), k == 0, k == ks - 1, rel)
                mm.then_inc(tile_done, 1)
                st.tile += 1

            def split_input(m):
                return lambda k: pe.wait_ge(u_done, 8 * m + k + 1)

            def norm_sum(m, k, n=L):
                x = 8 * m + k
                pe.wait_ge(sq_done, x + 1)
                if k == 0 and m > 0:
                    pe.wait_ge(r_ready, m)
                if m >= 3:
                    mm = pe.matmul(ps[:, 4, :], ones, SQ[x % 2][:, META:L], start=k == 0, stop=k == KT - 1)
                else:
                    for h in range(2):
                        mm = pe.matmul(ps[:, 4 + h, 0:HALF], ones, SQ[x % 2][:, h * HALF:(h + 1) * HALF],
                                       start=k == 0, stop=k == KT - 1)
                mm.then_inc(sq_summed, 1)

            def u(k):
                return UH[:, k, :]

            def ul(k):
                return UL[:, k, :]

            def mlp(m, n, layer):
                def quarter(q, last):
                    for j in range(8):
                        tile(KT, n, u, ul, before=split_input(m - 1) if j == 0 else None)
                    for e in range(8):
                        def hid_wait(f):
                            if e == 0:
                                pe.wait_ge(hid_done, 32 * layer + 8 * q + f + 1)
                        tile(8, n, lambda f: HH[:, f, :], lambda f: HL[:, f, :], before=hid_wait)
                        if last and e >= 2:
                            norm_sum(m, e - 2)
                loop(FQ - 1, 128, 16, lambda i: quarter(i, False))
                quarter(FQ - 1, True)
                for k in (6, 7):
                    norm_sum(m, k)

            def hgrn(h):
                def w(name, per, c):
                    pe.wait_ge(X[name], count(X, name, h * per + c))
                w("k", 1, 1)
                w("b", 1, 1)
                w("qp", 1, 1)
                w("am", 8, 0)
                for c in range(NCH):
                    mm = pe.matmul(flat[:, c * P:(c + 1) * P], kp[:, c * P:(c + 1) * P], qp[:, c * P:(c + 1) * P],
                                   start=True, stop=True)
                mm.then_inc(X["A"], 1)
                for l in range(1, LEVELS + 1):
                    if l == 2:
                        w("v", 1, 1)
                        w("end", 1, 0)
                        for c in range(NCH):
                            mm = pe.transpose(flat[:, 3072 + c * P:3072 + (c + 1) * P], vp[:, c * P:(c + 1) * P], ident)
                        mm.then_inc(X["vt"], 1)
                    if l == 6:
                        w("kd", 1, 1)
                        w("or", 1, 0)
                        for c in range(4):
                            mm = pe.transpose(ps[:, 4, c * P:(c + 1) * P], kd[:, c * P:(c + 1) * P], ident)
                        mm.then_inc(X["kt"], 1)
                    if l == 7:
                        w("ktc", 1, 1)
                        w("vtc", 1, 1)
                        w("S", 1, 0)
                        for c in range(4):
                            mm = pe.matmul(ps[:, 5, c * P:(c + 1) * P], kdT[:, c, :], vT[:, c, :], start=True, stop=True)
                        mm.then_inc(X["st"], 1)
                    w("EQ", LEVELS, l)
                    if l >= 2:
                        w("am", 8, l - 1)
                    o = 1024 * (l % 2)
                    e = XE[l % 2]
                    for c in range(NCH):
                        mm = pe.matmul(flat[:, o + c * P:o + (c + 1) * P], e[:, c * P:(c + 1) * P],
                                       e[:, c * P:(c + 1) * P], start=True, stop=True)
                    mm.then_inc(X["A"], 1)
                w("am", 8, 8)
                w("S", 1, 1)
                w("qb", 1, 1)
                for c in range(NCH):
                    dst = flat[:, 3072 + c * P:3072 + (c + 1) * P]
                    mm = pe.matmul(dst, vT[:, c, :], am[:, c * P:(c + 1) * P], start=True, stop=c == 0)
                    if c:
                        mm = pe.matmul(dst, S[:, c - 1, :], qb[:, c * P:(c + 1) * P], start=False, stop=True)
                mm.then_inc(X["o"], 1)
                w("osq", 1, 1)
                for g in range(2):
                    mm = pe.matmul(ps[:, 4 + g, 0:HALF], ones, TA[:, g * HALF:(g + 1) * HALF], start=True, stop=True)
                mm.then_inc(X["on"], 1)

            pe.wait_ge(consts_in, 32)
            for k in range(KT):
                norm_sum(0, k)
            loop(5, 32, 4, lambda i: [tile(KT, L, u, ul, before=split_input(0) if j == 0 else None)
                                      for j in range(4)])
            t = st.tile
            pe.wait_ge(evac[t % 2], t // 2 + FREE)
            for k in range(KT):
                if k % 2 == 0:
                    wh, wl, rel = take()
                c = ROPE * (k % 2)
                for h in range(2):
                    mm = passes(psum(t, L, ROPE)[:, h, :], wh[:, c:c + ROPE], wl[:, c:c + ROPE],
                                tok(u(k), L)[:, h, :], tok(ul(k), L)[:, h, :], k == 0, k == KT - 1, rel and h == 0)
                rel = False
            mm.then_inc(tile_done, 1)
            st.tile += 1
            pe.wait_ge(X["pad"], 1)
            with pe.Fori(0, HEADS) as h:
                hgrn(h)
            for x in range(4):
                pe.wait_ge(M["sq"], x + 1)
                for g in range(2):
                    mm = pe.matmul(ps[:, 4 + 2 * (x // 2) + g, 0:HALF], ones, SQ[x % 2][:, g * HALF:(g + 1) * HALF],
                                   start=x % 2 == 0, stop=x % 2 == 1)
                mm.then_inc(M["sum"], 1)
            pe.wait_ge(M["c"], 4)
            for h in range(HEADS):
                tile(2, L, lambda k: CHI[:, k, :], lambda k: CLO[:, k, :])
                t = st.tile
                pe.wait_ge(evac[t % 2], t // 2 + FREE)
                wh, wl, rel = take()
                for k in range(2):
                    c = ROPE * k
                    for g in range(2):
                        mm = passes(psum(t, L, ROPE)[:, g, :], wh[:, c:c + ROPE], wl[:, c:c + ROPE],
                                    tok(CHI[:, k, :], L)[:, g, :], tok(CLO[:, k, :], L)[:, g, :], k == 0, k == 1,
                                    rel and k == g == 0)
                mm.then_inc(tile_done, 1)
                st.tile += 1

            def head_sum(y):
                pe.wait_ge(M["qa"], y + 1)
                if 2 <= y < HEADS + 2:
                    pe.wait_ge(M["s"], y - 1)
                for g in range(2):
                    mm = pe.matmul(ps[:, 4 + 2 * (y % 2) + g, 0:HALF], ones, SQ[y % 2][:, g * HALF:(g + 1) * HALF],
                                   start=True, stop=True)
                mm.then_inc(M["qsum"], 1)

            def rotate(x, b, done):
                for g in range(2):
                    mm = pe.matmul(ps[0:ROPE, b + g, 0:HALF], turn, x[:, g * HALF:(g + 1) * HALF], start=True, stop=True)
                mm.then_inc(done, 1)
            for y in range(HEADS):
                for _ in range(2):
                    tile(2, L, lambda k: CHI[:, 2 + k, :], lambda k: CLO[:, 2 + k, :])
                if y == 0:
                    pe.wait_ge(M["kx"], 1)
                    pe.wait_ge(M["r"], 2)
                    rotate(KRP, 6, M["kturn"])
                if y == 1:
                    pe.wait_ge(M["ks"], 1)
                head_sum(y)
                if y:
                    pe.wait_ge(M["x"], y)
                    rotate(QR[:, y - 1, :], 4 + 2 * ((y - 1) % 2), M["turn"])
            head_sum(HEADS)
            pe.wait_ge(M["x"], HEADS)
            rotate(QR[:, HEADS - 1, :], 4 + 2 * ((HEADS - 1) % 2), M["turn"])
            for y in range(HEADS + 1, 2 * HEADS):
                head_sum(y)
            pe.wait_ge(M["x"], 2 * HEADS)
            pe.wait_ge(M["rope"], HEADS)

            def span(j):
                return (0, META, META) if j == 0 else (META + (j - 1) * P, P, META + j * P)

            def turn_values(h):
                if h:
                    pe.wait_ge(M["end"], h)
                for c in range(NCH):
                    a, n = (0, META) if c == 0 else (META + (c - 1) * P, P)
                    mm = pe.transpose(flat[0:n, 3072 + c * P:3072 + (c + 1) * P], V[:, h, a:a + n], ident)
                mm.then_inc(M["vt"], 1)

            def score(x):
                h, j = x // NCH, x % NCH
                q0, n, nk = span(j)
                if x >= 2:
                    pe.wait_ge(M["exp"], x - 1)
                o = 1024 * (x % 2)
                for a, b in ((0, min(nk, 512)), (512, nk)):
                    if a >= b:
                        continue
                    pe.matmul(flat[0:n, o + a:o + b], QN[:, h, q0:q0 + n], KN[:, h, a:b], start=True, stop=False,
                              skip_group_check=True)
                    mm = pe.matmul(flat[0:n, o + a:o + b], QR[:, h, q0:q0 + n], KRS[:, h, a:b], start=False,
                                   stop=True, skip_group_check=True)
                    c = max(a, nk - 64)
                    if j and c < b:
                        mm = pe.matmul(flat[0:n, o + c:o + b], early, ones[0:1, 0:b - c], start=False, stop=True,
                                       skip_group_check=True)
                mm.then_inc(M["sc"], 1)

            def turned(x):
                q0, n, nk = span(x % NCH)
                if x:
                    pe.wait_ge(M["tc"], x)
                pe.wait_ge(M["p"], x + 1)
                for c in range(x % NCH + 1):
                    a, m = (0, META) if c == 0 else (META + (c - 1) * P, P)
                    mm = pe.transpose(flat[0:m, 2048 + c * P:2048 + c * P + n], PP[x % 2][0:n, a:a + m],
                                      ident[0:n, 0:n])
                mm.then_inc(M["t"], 1)

            def values(x):
                j = x % NCH
                q0, n, nk = span(j)
                pe.wait_ge(M["vtc"], x // NCH + 1)
                pe.wait_ge(M["tc"], x + 1)
                dst = flat[:, 3584:3584 + META] if j == 0 else flat[:, 3072 + (j - 1) * P:3072 + j * P]
                for c in range(j + 1):
                    m = META if c == 0 else P
                    mm = pe.matmul(dst, VT[0:m, c, :], PT[x % 2][0:m, c, 0:n], start=c == 0, stop=c == j)
                mm.then_inc(M["pv"], 1)
            score(0)
            for x in range(HEADS * NCH):
                if x + 1 < HEADS * NCH:
                    score(x + 1)
                if x % NCH == 1:
                    turn_values(x // NCH)
                turned(x)
                if x:
                    values(x - 1)
            values(HEADS * NCH - 1)
            pe.wait_ge(M["end"], HEADS)
            for e in range(KT):
                tile(KT, L, u, ul)
                if e >= 2:
                    norm_sum(1, e - 2)
            for k in (6, 7):
                norm_sum(1, k)
            mlp(2, L, 0)
            pe.wait_ge(N["mem_sq"], 1)
            for k in range(KT):
                mm = pe.matmul(ps[:, 6, 0:NMEM], ones, MSQ[:, k, :], start=k == 0, stop=k == KT - 1)
            mm.then_inc(N["mem_sum"], 1)
            pe.wait_ge(N["mem_lo"], KT)
            for j in range(2 * HEADS):
                tile(KT, NMEM, lambda k: MH[:, k, :], lambda k: ML[:, k, :])
            for e in range(KT):
                g = 2 * (e // 2)
                pe.wait_ge(u_done, 16 + g + 2)
                tile(2, SEQ, lambda k: UH[:, g + k, :], lambda k: UL[:, g + k, :])
                if e >= 2:
                    norm_sum(3, e - 2)
            for k in (6, 7):
                norm_sum(3, k)
            pe.wait_ge(*evacuated(TILE0["memkv"] + 6))
            pe.wait_ge(*evacuated(TILE0["memkv"] + 7))
            for x in range(2):
                for h in range(HEADS):
                    mm = pe.transpose(ps[:, 6 + x, h * P:(h + 1) * P], VM[:, h, x * P:(x + 1) * P], ident)
            mm.then_inc(N["mem_vt"], 1)
            mlp(4, SEQ, 1)
            pe.wait_ge(N["mem_vtc"], 1)
            pe.wait_ge(N["ab_lo"], 1)
            for k in range(KT):
                split_input(4)(k)
                mm = passes(ps[0:16, 7, :], ABH[:, k, :], ABL[:, k, :], tok(u(k), SEQ), tok(ul(k), SEQ), k == 0,
                            k == KT - 1, False)
            mm.then_inc(N["ab"], 1)
            pe.wait_ge(N["ab_row"], 1)
            for c in range(4):
                mm = pe.matmul(ps[:, 6, 16 * c:16 * c + 16], R2[0:16, META + c * P:META + (c + 1) * P],
                               ident[0:16, 0:16], start=True, stop=True)
            mm.then_inc(N["ab_turn"], 1)

            loop(6, 32, 4, lambda i: [tile(KT, SEQ, u, ul) for _ in range(4)])
            pe.wait_ge(N["ab_g"], 1)
            pe.matmul(ps[:, 7, 128:160], upper, AB[:, 0, :], start=True, stop=True)
            pe.matmul(ps[:, 7, 160:192], ones, AB[:, 0, :], start=True, stop=True).then_inc(N["ab_cum"], 1)

            def gate_tiles(i):
                for j in range(4):
                    tile(KT, SEQ, u, ul)
                    for x in (2 * j, 2 * j + 1):
                        pe.wait_ge(N["l2_sq"], 8 * i + x + 1)
                        pe.matmul(ps[:, 4 + x % 2, :], ones, SQ[x % 2][:, META:L], start=True, stop=True
                                  ).then_inc(N["l2_sum"], 1)
            loop(2, 32, 4, gate_tiles)
            loop(1, 32, 4, lambda i: [tile(KT, SEQ, u, ul) for _ in range(4)])
            for t in range(st.tile - 4, st.tile):
                pe.wait_ge(*evacuated(t))
            pe.wait_ge(N["l2_done"], 16)

            def scores(h):
                for c in range(4):
                    mm = pe.matmul(ps[:, 2 * (h % 2) + c // 2, NMEM * (c % 2):NMEM * (c % 2 + 1)],
                                   ZQ[:, 8 + h, c * P:(c + 1) * P], KM[:, h, :], start=True, stop=True)
                mm.then_inc(N["ma_s"], 1)
            scores(0)
            scores(1)
            pe.wait_ge(N["ab_x"], 2)
            for h in range(HEADS):
                pe.wait_ge(N["ma_p"], h + 1)
                for x in range(2):
                    for c in range(4):
                        mm = pe.transpose(ps[:, 6 + x, c * P:(c + 1) * P], am_p[h % 2][:, c, x * P:(x + 1) * P], ident)
                mm.then_inc(N["ma_t"], 1)
                if h + 2 < HEADS:
                    scores(h + 2)
                pe.wait_ge(N["ma_tc"], h + 1)
                if h >= 2:
                    pe.wait_ge(N["ma_end"], h - 1)
                for x in range(2):
                    mm = pe.matmul(ps[:, 4 + h % 2, :], VMT[:, x, h * P:(h + 1) * P], am_t[:, x, :], start=x == 0,
                                   stop=x == 1)
                mm.then_inc(N["ma_o"], 1)

            def chunk(c):
                def w(name, k, per=1):
                    pe.wait_ge(G[name], count(G, name, c * 2 * per + k))

                def four(bank, a, b, g):
                    for x in range(4):
                        mm = pe.matmul(ps[:, 4 * g + bank, x * P:(x + 1) * P], a(x), b(x), start=True, stop=True)
                    return mm

                def turned(bank, a, g):
                    for x in range(4):
                        mm = pe.transpose(ps[:, 4 * g + bank, x * P:(x + 1) * P], a[:, x, :], ident)
                    return mm
                for g in range(2):
                    if g == 0:
                        pe.wait_ge(G["gn"], c + 1)
                    w("oc", 0)
                    four(2, lambda x: GN[:, 4 * g + x:4 * g + x + 1].to_broadcast([P, P]), lambda x: upper, g
                         ).then_inc(G["gb"], 1)
                for g in range(2):
                    w("nrm", g + 1)
                    w("s", 0)
                    kn, qn = G2["kn"][g], G2["qn"][g]
                    four(0, lambda x: kn[:, x, :], lambda x: kn[:, x, :], g)
                    four(1, lambda x: kn[:, x, :], lambda x: qn[:, x, :], g).then_inc(G["kk"], 1)
                    turned(3, kn, g)
                for g in range(2):
                    w("vin", g + 1)
                    w("d", g + 1)
                    w("eg", g + 1)
                    turned(2, G2["PT"][g], g).then_inc(G["tr"], 1)
                for g in range(2):
                    w("lm", g + 1, LEVELS)
                    turned(0, G2["LM"][g], g).then_inc(G["a"], 1)
                for l in range(1, LEVELS):
                    for g in range(2):
                        w("u", 2 * (l - 1) + g + 1, LEVELS - 1)
                        w("lm", 2 * l + g + 1, LEVELS)
                        four(0, lambda x: G2["LM"][g][:, x, :], lambda x: G2["T"][g][:, x, :], g).then_inc(G["a"], 1)
                    for g in range(2):
                        if l == 1:
                            w("un", g + 1)
                            w("kg", g + 1)
                            w("pq", g + 1)
                        else:
                            w("ui", 2 * (l - 2) + g + 1, LEVELS - 1)
                        w("ac", 2 * (l - 1) + g + 1, LEVELS - 1)
                        a, uu = G2["A"][g], G2["U"][g]
                        if l < LEVELS - 1:
                            four(1, lambda x: uu[:, x, :], lambda x: a[:, x, :], g)
                        four(2, lambda x: a[:, x, :], lambda x: uu[:, x, :], g).then_inc(G["p"], 1)
                for g in range(2):
                    four(0, lambda x: G2["kn"][g][:, x, :], lambda x: ST8[:, 4 * g + x, :], g).then_inc(G["ks"], 1)
                for g in range(2):
                    w("ui", 2 * (LEVELS - 2) + g + 1, LEVELS - 1)
                    w("r", g + 1)
                    four(1, lambda x: G2["U"][g][:, x, :], lambda x: G2["LM"][g][:, x, :], g).then_inc(G["vn"], 1)
                for g in range(2):
                    w("vnc", g + 1)
                    w("pt", g + 1)
                    vn = G2["A"][g]
                    for x in range(4):
                        dst = ps[:, 4 * g + 2, x * P:(x + 1) * P]
                        pe.matmul(dst, ST8[:, 4 * g + x, :], G2["qn"][g][:, x, :], start=True, stop=False)
                        pe.matmul(dst, vn[:, x, :], G2["PT"][g][:, x, :], start=False, stop=True)
                    four(3, lambda x: G2["kg"][g][:, x, :], lambda x: vn[:, x, :], g).then_inc(G["o"], 1)
            with pe.Fori(0, 4) as c:
                chunk(c)
            for h in range(GH):
                pe.wait_ge(N["y_sq"], h + 1)
                if h >= 2:
                    pe.wait_ge(N["g_r"], h - 1)
                pe.matmul(ps[:, 4 + h % 2, :], ones, SQ[h % 2][:, META:L], start=True, stop=True).then_inc(N["g_sum"], 1)
            pe.wait_ge(u_done, 48)
            pe.wait_ge(N["om_lo"], HEADS)
            for e in range(KT):
                tile(12, SEQ, lambda k: UH[:, k, :] if k < 8 else OMH[:, k - 8, :],
                     lambda k: UL[:, k, :] if k < 8 else OML[:, k - 8, :])
                if e >= 2:
                    norm_sum(5, e - 2)
            for k in (6, 7):
                norm_sum(5, k)

            def first_input(k):
                norm_sum(6, k)
                split_input(6)(k)
            for a in range(2):
                for j in range(22):
                    tile(KT, SEQ, u, ul, before=first_input if a == j == 0 else None)
                for e in range(KT):
                    def hid_wait(f):
                        if e == 0:
                            pe.wait_ge(N["f_hid"], 11 * a + f + 1)
                    tile(11, SEQ, lambda f: FH[:, f, :], lambda f: FL[:, f, :], before=hid_wait)
                    if a and e >= 2:
                        norm_sum(7, e - 2)
            for k in (6, 7):
                norm_sum(7, k)

        @block.scalar
        def _(act):
            def square(m, k, src, ready=None):
                x = 8 * m + k
                if ready:
                    act.wait_ge(*ready)
                if x >= 2:
                    act.wait_ge(sq_summed, x - 1)
                c = META if m >= 3 else 0
                act.activation(SQ[x % 2][:, c:L], src[:, c:L], ACT.Square).then_inc(sq_done, 1)

            def rstd(m, n=D):
                act.wait_ge(sq_summed, 8 * m + 8)
                r = R[m % 2]
                if m >= 3:
                    r = r[:, META:L]
                    act.activation(r, ps[:, 4, :], ACT.Ln, bias=eps[:, 0:1], scale=1.0 / n)
                else:
                    r = r[:, :]
                    act.activation(tok(r, L), ps[:, 4:6, 0:HALF], ACT.Ln, bias=eps[:, 0:1], scale=1.0 / n)
                act.drain()
                act.activation(r, r, ACT.Exp, scale=-0.5).then_inc(r_ready, 1)

            def hi(m, k, vec):
                g = vecs[:, VEC[vec] + k:VEC[vec] + k + 1]
                c = META if m >= 3 else 0
                act.activation(UH[:, k, c:L], H[:, k, c:L], ACT.Copy, scale=g).then_inc(uh_done, 1)

            act.preload_act_table_set(LNEXP)
            act.wait_ge(x_in, 16)
            act.wait_ge(consts_in, 32)
            act.wait_ge(zero_set, 2)
            for k in range(KT):
                square(0, k, H[:, k, :])
                hi(0, k, "mix0")
            rstd(0)

            for t in (7, 6, 19, 18):
                act.wait_ge(*evacuated(t))
            for a in (4, 16):
                act.activation(Z[:, a:a + 4, :], Z[:, a:a + 4, :], ACT.Silu).then_inc(X["silu"], 1)
            act.preload_act_table_set(LNEXP)

            def hgrn(h, more):
                def w(name, per, c, h=h):
                    act.wait_ge(X[name], count(X, name, h * per + c))
                for l in range(1, LEVELS + 1):
                    w("D", LEVELS, l)
                    if l >= 3:
                        w("A", 8, l - 1)
                    act.activation(XE[l % 2][:, :], XD[l % 2][:, :], ACT.Exp).then_inc(X["E"], 1)
                    if l == 1:
                        w("dk", 1, 1)
                        act.activation(kd[:, 0:4 * P], kd[:, 0:4 * P], ACT.Exp).then_inc(X["ek"], 1)
                    if l == 2:
                        act.drain()
                        w("end", 1, 0)
                        w("b", 1, 1)
                        act.activation(GL[:, 0:NCH], bb[:, CH - 1:LP:CH], ACT.Exp)
                        act.activation(TB[:, 0:4 * P], bb[:, P:LP], ACT.Exp).then_inc(X["eb"], 1)
                        w("vt", 1, 1)
                        act.activation(vT[:, :, :].rearrange("p c v -> p (c v)"), flat[:, 3072:3072 + LP], ACT.Copy
                                       ).then_inc(X["vtc"], 1)
                    if l == 6:
                        w("kt", 1, 1)
                        act.activation(kdT[:, :, :].rearrange("p c v -> p (c v)"), ps[:, 4, :], ACT.Copy
                                       ).then_inc(X["ktc"], 1)
                if more:
                    act.drain()
                    hgrn_keys(h + 1)
                w("o", 1, 1)
                o = flat[:, 3072 + LEAD:3072 + LP]
                act.activation(TA[:, :], o, ACT.Square).then_inc(X["osq"], 1)
                w("on", 1, 1)
                act.activation(tok(TB[:, :], L), ps[:, 4:6, 0:HALF], ACT.Ln, bias=eps[:, 0:1], scale=1.0 / P)
                act.drain()
                act.activation(TB[:, :], TB[:, :], ACT.Exp, scale=-0.5).then_inc(X["or"], 1)
                w("og", 1, 1)
                act.activation(UH[:, bass.ds(h, 1), :].rearrange("p a t -> p (a t)"), TB[:, :], ACT.Copy
                               ).then_inc(X["oh"], 1)

            def hgrn_keys(h):
                a, b = XD[0][:, 0:L], XD[1][:, 0:L]
                act.activation(a, Z[:, bass.ds(8 + h, 1), :].rearrange("p a t -> p (a t)"), ACT.Abs)
                act.drain()
                act.activation(a, a, ACT.Exp, scale=-1.0)
                act.drain()
                act.activation(a, a, ACT.Ln, bias=1.0).then_inc(X["l"], 1)
                act.wait_ge(X["d"], h + 1)
                act.activation(kp[:, LEAD:LP], b, ACT.Exp).then_inc(X["k"], 1)

            hgrn_keys(0)
            with act.Fori(0, HEADS - 1) as h:
                hgrn(h, True)
            hgrn(HEADS - 1, False)
            act.wait_ge(X["end"], HEADS + FREE)
            for x in range(4):
                if x >= 2:
                    act.wait_ge(M["sum"], x - 1)
                act.activation(SQ[x % 2][:, :], Z[:, x, :], ACT.Square).then_inc(M["sq"], 1)
                g = VEC["cq"] + x
                act.activation(CHI[:, x, :], Z[:, x, :], ACT.Copy, scale=vecs[:, g:g + 1]).then_inc(M["chi"], 1)
            for x, r in enumerate((R2, R[1])):
                act.wait_ge(M["sum"], 2 * x + 2)
                act.activation(tok(r[:, :], L), ps[:, 4 + 2 * x:6 + 2 * x, 0:HALF], ACT.Ln, bias=eps[:, 0:1],
                               scale=1.0 / RANK)
                act.drain()
                act.activation(r[:, :], r[:, :], ACT.Exp, scale=-0.5).then_inc(M["r"], 1)

            act.drain()
            act.activation(KSQ[:, :], KR[:, :], ACT.Square)

            def head_square(y):
                if y >= 2:
                    act.wait_ge(M["qsum"], y - 1)
                if y < HEADS:
                    act.wait_ge(*evacuated(TILE0["qup"] + 2 * y))
                    act.wait_ge(*evacuated(TILE0["qup"] + 2 * y + 1))
                    act.activation(SR[y % 2][:, :], QR[:, y, :], ACT.Square)
                else:
                    act.wait_ge(*evacuated(TILE0["kvup"] + 2 * (y - HEADS)))
                a = QN[:, y, :] if y < HEADS else KN[:, y - HEADS, :]
                act.activation(SQ[y % 2][:, :], a, ACT.Square).then_inc(M["q"], 1)
            head_square(0)
            head_square(1)
            for y in range(2 * HEADS):
                act.wait_ge(M["qsum"], y + 1)
                if y >= 2:
                    act.wait_ge(M["x"], y - 1)
                a = RB[y % 2][:, :]
                b = 4 + 2 * (y % 2)
                act.activation(tok(a, L), ps[:, b:b + 2, 0:HALF], ACT.Ln, bias=eps[:, 0:1], scale=1.0 / QK)
                act.drain()
                act.activation(a, a, ACT.Exp, scale=-0.5).then_inc(M["rr"], 1)
                if y + 2 < 2 * HEADS:
                    head_square(y + 2)

            def values_turned(h):
                act.wait_ge(M["vt"], h + 1)
                act.activation(VT[0:META, 0, :], flat[0:META, 3072:3072 + P], ACT.Copy)
                act.activation(VT[:, 1:5, :], flat[:, 3072 + P:3072 + 5 * P].rearrange("p (c v) -> p c v", c=4),
                               ACT.Copy).then_inc(M["vtc"], 1)

            def exps(x):
                j = x % NCH
                n, nk = (META, META) if j == 0 else (P, META + j * P)
                act.wait_ge(M["max"], x + 1)
                if x >= 2:
                    act.wait_ge(M["t"], x - 1)
                o = 1024 * (x % 2)
                act.activation(PP[x % 2][0:n, 0:nk], flat[0:n, o:o + nk], ACT.Exp, bias=stat[0:n, j:j + 1],
                               scale=QK ** -0.5, accum_out=stat[0:n, 8 + j:9 + j]).then_inc(M["exp"], 1)

            def copies(x):
                j = x % NCH
                n = META if j == 0 else P
                act.wait_ge(M["t"], x + 1)
                if x >= 2:
                    act.wait_ge(M["pv"], x - 1)
                last = act.activation(PT[x % 2][0:META, 0, 0:n], flat[0:META, 2048:2048 + n], ACT.Copy)
                if j:
                    last = act.activation(PT[x % 2][:, 1:j + 1, :],
                                          flat[:, 2048 + P:2048 + (j + 1) * P].rearrange("p (c v) -> p c v", c=j),
                                          ACT.Copy)
                last.then_inc(M["tc"], 1)

            def outputs(h):
                act.wait_ge(M["pv"], NCH * (h + 1))
                o = UH[:, 4 + h, :]
                act.activation(o[:, 0:META], flat[:, 3584:3584 + META], ACT.Copy)
                act.activation(o[:, META:L], flat[:, 3072:3584], ACT.Copy).then_inc(M["oh"], 1)
            for t in range(TILE0["wout"] - 2, TILE0["wout"]):
                act.wait_ge(*evacuated(t))
            exps(0)
            for x in range(HEADS * NCH):
                if x + 1 < HEADS * NCH:
                    exps(x + 1)
                if x % NCH == 1:
                    values_turned(x // NCH)
                copies(x)
                if x and x % NCH == 0:
                    outputs(x // NCH - 1)
            outputs(HEADS - 1)
            act.wait_ge(M["end"], HEADS)
            act.dma_start(MEM[:, :, :], memT).then_inc(N["mem_in"], 16)
            for e in range(KT):
                square(1, e, H[:, e, :], evacuated(TILE0["wout"] + e))
            for e in range(KT):
                hi(1, e, "mlp0")
            rstd(1)

            def mlp(layer, n, m):
                odd = TILE0["mlp%d" % layer] % 2

                def quarter(q, base, last, first=False):
                    def relu(j):
                        t, x = base + j, 8 * q + j
                        act.wait_ge(tile_done, t + 1)
                        if not (first and j < 2):
                            act.wait_ge(relu2_done, x - 1)
                        act.activation(tok(RL[j % 2][:, :], n), psum(odd + j, n), ACT.Relu
                                       ).then_inc(evac[(odd + j) % 2], 1)

                    def part(j):
                        act.wait_ge(relu2_done, 8 * q + j + 1)
                        act.activation(tok(HH[:, j, :], n), tok(SB[j % 2][:, :], n), ACT.Copy).then_inc(hh_done, 1)
                    relu(0)
                    for j in range(8):
                        if j + 1 < 8:
                            relu(j + 1)
                        part(j)
                    if last:
                        for e in range(8):
                            square(m, e, H[:, e, :], (h_final, 8 * layer + e + 1))
                            if m != 2:
                                hi(m, e, {4: "pre_mix"}[m])
                b = TILE0["mlp%d" % layer]
                quarter(FQ * layer, b, False, layer == 0)
                with act.Fori(1, FQ - 1) as i:
                    quarter(i + FQ * layer, i * 16 + b, False)
                quarter(FQ * layer + FQ - 1, b + 16 * (FQ - 1), True)
                rstd(m)
            mlp(0, L, 2)
            act.wait_ge(N["mem_in"], 16)
            act.activation(MSQ[:, :, :], MEM[:, :, :], ACT.Square).then_inc(N["mem_sq"], 1)
            for k in range(KT):
                g = VEC["mem"] + k
                act.activation(MH[:, k, :], MEM[:, k, :], ACT.Copy, scale=vecs[:, g:g + 1]).then_inc(N["mem_hi"], 1)
            act.wait_ge(N["mem_sum"], 1)
            act.activation(RM[:, :], ps[:, 6, 0:NMEM], ACT.Ln, bias=eps[:, 0:1], scale=1.0 / D)
            act.drain()
            act.activation(RM[:, :], RM[:, :], ACT.Exp, scale=-0.5).then_inc(N["mem_r"], 1)
            for g in range(4):
                act.wait_ge(N["dd"], g + 1)
                for c in range(2):
                    act.activation(UH[:, 2 * g + c, META:L], DD[g % 2][:, c, META:L], ACT.Copy).then_inc(uh_done, 1)
            for e in range(KT):
                t = TILE0["pool"] + e
                square(3, e, H[:, e, :], evacuated(t))
                if e % 2:
                    for x in (e - 1, e):
                        hi(3, x, "mlp1")
            rstd(3)
            act.wait_ge(N["mem_vt"], 1)
            act.activation(VMT[:, :, :], ps[:, 6:8, :], ACT.Copy).then_inc(N["mem_vtc"], 1)
            mlp(1, SEQ, 4)
            act.wait_ge(N["ab_x"], 1)
            act.activation(AB[:, 3:5, :], AB[:, 1:3, :], ACT.Abs)
            act.drain()
            act.activation(AB[:, 3:5, :], AB[:, 3:5, :], ACT.Exp, scale=-1.0)
            act.drain()
            act.activation(AB[:, 5, 0:8], vecs[:, VEC["alog"]:VEC["alog"] + 8], ACT.Exp)
            act.activation(AB[:, 3:5, :], AB[:, 3:5, :], ACT.Ln, bias=1.0).then_inc(N["ab_ln"], 1)
            act.preload_act_table(ACT.Silu)
            with act.Fori(0, 6) as i:
                for j in range(4):
                    act.wait_ge(N["conv"], 4 * i + j + 1)
                    act.sem_inc(passed, 1)
                    act.activation(QKV[:, bass.ds(4 * i + j, 1), :].rearrange("p a t -> p (a t)"), CA[j % 2][:, :],
                                   ACT.Silu).then_inc(N["conv_silu"], 1)
            act.preload_act_table_set(LNEXP)
            act.drain()

            def l2_square(x):
                if x >= 2:
                    act.wait_ge(N["l2_sum"], x - 1)
                act.activation(SQ[x % 2][:, META:L], QKV[:, x, :], ACT.Square).then_inc(N["l2_sq"], 1)
            l2_square(0)
            l2_square(1)
            for x in range(16):
                act.wait_ge(N["l2_sum"], x + 1)
                if x >= 2:
                    act.wait_ge(N["l2_done"], x - 1)
                a = L2R[x % 2][:, META:L]
                act.activation(a, ps[:, 4 + x % 2, :], ACT.Ln, bias=eps[:, 0:1])
                act.drain()
                act.activation(a, a, ACT.Exp, scale=-0.5).then_inc(N["l2_r"], 1)
                if x + 2 < 16:
                    l2_square(x + 2)
            act.preload_act_table(ACT.Silu)
            for t in (TILE0["gin"] + 30, TILE0["gin"] + 31):
                act.wait_ge(*evacuated(t))
            act.activation(ZQ[:, 0:8, :], ZQ[:, 0:8, :], ACT.Silu)
            act.preload_act_table_set(LNEXP)
            act.wait_ge(N["ab_cum"], 1)
            act.activation(SCAL[:, 2, :], ps[:, 7, 128:160], ACT.Exp)
            act.activation(SCAL[:, 5, :], ps[:, 7, 160:192], ACT.Exp).then_inc(N["ab_exp"], 1)
            act.wait_ge(N["ab_x"], 2)
            act.activation(SCAL[:, 1, :], SCAL[:, 1, :], ACT.Exp)
            act.activation(SCAL[:, 4, :], SCAL[:, 4, :], ACT.Exp).then_inc(N["ab_all"], 1)

            def exps(h):
                act.wait_ge(N["ma_max"], h + 1)
                if h >= 2:
                    act.wait_ge(N["ma_t"], h - 1)
                for c in range(4):
                    last = act.activation(am_p[h % 2][:, c, :],
                                          ps[:, 2 * (h % 2) + c // 2, NMEM * (c % 2):NMEM * (c % 2 + 1)], ACT.Exp,
                                          bias=am_s[h % 2][:, c:c + 1], scale=P ** -0.5,
                                          accum_out=am_s[h % 2][:, 4 + c:5 + c])
                last.then_inc(N["ma_exp"], 1)
            exps(0)
            for h in range(HEADS):
                if h + 1 < HEADS:
                    exps(h + 1)
                act.wait_ge(N["ma_t"], h + 1)
                act.activation(am_t[:, :, :], ps[:, 6:8, :], ACT.Copy).then_inc(N["ma_tc"], 1)
                act.wait_ge(N["ma_o"], h + 1)
                act.activation(ZQ[:, 8 + h, :], ps[:, 4 + h % 2, :], ACT.Copy).then_inc(N["ma_end"], 1)

            def chunk(c):
                def w(name, k, per=1):
                    act.wait_ge(G[name], count(G, name, c * 2 * per + k))

                def bank(g, b):
                    return ps[:, 4 * g + b, :].rearrange("p (x t) -> p x t", x=4)
                cols = bass.ds(c * P, P)
                w("o", 0)
                act.sem_inc(passed, 1)
                for g in range(2):
                    act.activation(G2["kn"][g][:, :, :], QKV[:, 8 + 4 * g:12 + 4 * g, cols], ACT.Copy)
                    act.activation(G2["qn"][g][:, :, :], QKV[:, 4 * g:4 * g + 4, cols], ACT.Copy
                                   ).then_inc(G["nrm"], 1)
                for g in range(2):
                    w("gb", g + 1)
                    act.activation(G2["U"][g][:, :, :], bank(g, 2), ACT.Exp).then_inc(G["eg"], 1)
                for g in range(2):
                    w("d", g + 1)
                    act.activation(G2["T"][g][:, :, :], G2["T"][g][:, :, :], ACT.Exp).then_inc(G["dec"], 1)
                for g in range(2):
                    w("tr", g + 1)
                    for x in range(4):
                        act.activation(G2["kg"][g][:, x, :], ps[:, 4 * g + 3, x * P:(x + 1) * P], ACT.Copy,
                                       scale=SC[:, 4, 4 * g + x:4 * g + x + 1])
                    act.activation(G2["vt"][g][:, :, :], bank(g, 2), ACT.Copy).then_inc(G["kg"], 1)
                for l in range(1, LEVELS):
                    for g in range(2):
                        w("a", 2 * l + g + 1, LEVELS)
                        act.activation(G2["A"][g][:, :, :], bank(g, 0), ACT.Copy).then_inc(G["ac"], 1)
                for g in range(2):
                    w("vn", g + 1)
                    for x in range(4):
                        last = act.activation(G2["A"][g][:, x, :], ps[:, 4 * g + 1, x * P:(x + 1) * P], ACT.Copy,
                                              scale=SC[:, 1, 4 * g + x:4 * g + x + 1])
                    last.then_inc(G["vnc"], 1)
                for g in range(2):
                    w("o", g + 1)
                    act.sem_inc(passed, 1)
                    act.activation(QKV[:, 4 * g:4 * g + 4, cols], bank(g, 2), ACT.Copy).then_inc(G["oc"], 1)
            with act.Fori(0, 4) as c:
                chunk(c)
            act.drain()

            def head_hi(h):
                act.wait_ge(N["g_t"], h + 1)
                act.activation(UH[:, h, META:L], GT[h % 2][:, META:L], ACT.Copy).then_inc(uh_done, 1)
            def head_square(h):
                if h >= 2:
                    act.wait_ge(N["g_sum"], h - 1)
                act.activation(SQ[h % 2][:, META:L], QKV[:, h, :], ACT.Square).then_inc(N["y_sq"], 1)
            head_square(0)
            head_square(1)
            for h in range(GH):
                act.wait_ge(N["g_sum"], h + 1)
                if h >= 2:
                    act.wait_ge(N["g_t"], h - 1)
                a = GR[h % 2][:, META:L]
                act.activation(a, ps[:, 4 + h % 2, :], ACT.Ln, bias=eps[:, 0:1], scale=1.0 / P)
                act.drain()
                act.activation(a, a, ACT.Exp, scale=-0.5).then_inc(N["g_r"], 1)
                if h + 2 < GH:
                    head_square(h + 2)
                if h:
                    head_hi(h - 1)
            head_hi(GH - 1)
            act.drain()
            for e in range(KT):
                t = TILE0["wout2"] + e
                act.wait_ge(tile_done, t + 1)
                act.activation(tok(Y[:, e, :], SEQ), psum(t, SEQ), ACT.Copy).then_inc(evac[t % 2], 1)
                act.drain()
                square(5, e, Y[:, e, :])
            rstd(5)
            for e in range(KT):
                square(6, e, H[:, e, :], (h_final, 16 + e + 1))
                hi(6, e, "pre_ffn")
            rstd(6)
            act.preload_act_table(ACT.Silu)

            def f_hi(a, j):
                act.wait_ge(*evacuated(TILE0["ffn"] + 30 * a + 2 * j + 1))
                act.activation(FH[:, j, META:L], GC[j % 2][:, META:L], ACT.Copy).then_inc(N["f_hh"], 1)
            for a in range(2):
                for j in range(11):
                    act.wait_ge(*evacuated(TILE0["ffn"] + 30 * a + 2 * j))
                    act.activation(GS[j % 2][:, META:L], GA[j % 2][:, META:L], ACT.Silu).then_inc(N["f_silu"], 1)
                    if j:
                        f_hi(a, j - 1)
                f_hi(a, 10)
            for e in range(KT):
                square(7, e, FO[:, e, :], (h_final, 24 + e + 1))
            act.preload_act_table_set(LNEXP)
            rstd(7)

        @block.vector
        def _(dve):
            for first in from_one:
                dve.sem_inc(first, FREE)
            def lo(m, k, vec):
                g = vecs[:, VEC[vec] + k:VEC[vec] + k + 1]
                dve.wait_ge(uh_done, 8 * m + k + 1)
                c = META if m >= 3 else 0
                dve.scalar_tensor_tensor(UL[:, k, c:L], H[:, k, c:L], g, UH[:, k, c:L].bitcast(F32), ALU.mult,
                                         ALU.subtract).then_inc(u_done, 1)

            def scaled(t, n, dst, r, extra=0, m=P):
                dve.wait_ge(tile_done, t + 1 + extra)
                dve.tensor_tensor(dst, psum(t, n, m), tok(r[0:m, :], n), ALU.mult).then_inc(evac[t % 2], 1)

            dve.wait_ge(x_in, 16)
            dve.wait_ge(consts_in, 32)
            for pad in (qp, kp, vp, lf):
                dve.memset(pad[:, 0:LEAD], 0.0)
            dve.drain()
            dve.sem_inc(X["pad"], 1)
            for k in range(KT):
                lo(0, k, "mix0")
            dve.wait_ge(r_ready, 1)
            with dve.Fori(0, 5) as i:
                for j in range(4):
                    dst = Z[:, bass.ds(4 * i + j, 1), :].rearrange("p a (h t) -> p (a h) t", h=2)
                    scaled(j, L, dst, R[0], extra=4 * i)
            scaled(20, L, tok(KR[:, :], L), R[0], m=ROPE)

            def hgrn(h, more):
                def w(name, per, c, h=h):
                    dve.wait_ge(X[name], count(X, name, h * per + c))

                def z(a, h=h):
                    return Z[:, bass.ds(a + h, 1), :].rearrange("p a t -> p (a t)")
                w("A", 8, 1)
                am3 = am[:, :].rearrange("p (c t) -> p c t", c=NCH)
                dve.tensor_tensor(am3, flat[:, 0:LP].rearrange("p (c t) -> p c t", c=NCH),
                                  ident.rearrange("p (a t) -> p a t", a=1).to_broadcast([P, NCH, P]), ALU.mult
                                  ).then_inc(X["am"], 1)

                def weigh(l):
                    m = CH >> l
                    w("E", LEVELS, l)
                    for a, b in zip(halves(XE[l % 2], m), (halves(kp, m)[0], halves(qp, m)[1])):
                        last = dve.tensor_tensor(a, a, b, ALU.mult)
                    last.then_inc(X["EQ"], 1)

                def keep(l):
                    dve.drain()
                    w("A", 8, l + 1)
                    dve.sem_inc(passed, 1)
                    o = 1024 * (l % 2)
                    msk = level[:, l - 1, :].rearrange("p (a t) -> p a t", a=1).to_broadcast([P, NCH, P]).bitcast(U32)
                    dve.copy_predicated(am3, msk, flat[:, o:o + LP].rearrange("p (c t) -> p c t", c=NCH)
                                        ).then_inc(X["am"], 1)
                w("qp", 1, 1)
                for l in range(1, LEVELS + 1):
                    weigh(l)
                    if l >= 2:
                        keep(l - 1)
                keep(LEVELS)
                w("st", 1, 1)
                dve.tensor_copy(S[:, 0, :], ps[:, 5, 0:P])
                for c in range(1, 4):
                    dve.drain()
                    last = dve.scalar_tensor_tensor(S[:, c, :], S[:, c - 1, :], GL[:, c:c + 1],
                                                    ps[:, 5, c * P:(c + 1) * P], ALU.mult, ALU.add)
                last.then_inc(X["S"], 1)
                if more:
                    hgrn_decays(h + 1)
                w("or", 1, 1)
                g = vecs[:, VEC["hg_out"]:VEC["hg_out"] + 1]
                o = flat[:, 3072 + LEAD:3072 + LP]
                dve.scalar_tensor_tensor(TB[:, :], o, g, TB[:, :], ALU.mult, ALU.mult)
                dve.drain()
                dve.tensor_tensor(TB[:, :], TB[:, :], z(16), ALU.mult).then_inc(X["og"], 1)
                w("oh", 1, 1)
                u1 = UH[:, bass.ds(h, 1), :].rearrange("p a t -> p (a t)").bitcast(F32)
                dve.tensor_tensor(UL[:, bass.ds(h, 1), :].rearrange("p a t -> p (a t)"), TB[:, :], u1,
                                  ALU.subtract).then_inc(X["end"], 1)

            dve.wait_ge(X["silu"], 2)
            def hgrn_decays(h):
                f = Z[:, bass.ds(8 + h, 1), :].rearrange("p a t -> p (a t)")
                dve.wait_ge(X["l"], h + 1)
                dve.scalar_tensor_tensor(lf[:, LEAD:LP], f, 0.0, XD[0][:, 0:L], ALU.min, ALU.subtract)
                dve.drain()
                dve.tensor_tensor(XD[1][:, 0:L], lf[:, LEAD:LP], f, ALU.subtract).then_inc(X["d"], 1)
                for c in range(NCH):
                    last = dve.tensor_tensor_scan(bb[:, c * P:(c + 1) * P], ones, lf[:, c * P:(c + 1) * P], 0.0,
                                                  ALU.mult, ALU.add)
                last.then_inc(X["b"], 1)
                dve.drain()
                b3 = bb[:, 0:4 * P].rearrange("p (c t) -> p c t", c=4)
                d3 = kd[:, 0:4 * P].rearrange("p (c t) -> p c t", c=4)
                dve.tensor_tensor(d3, b3[:, :, P - 1:P].to_broadcast([P, 4, P]), b3, ALU.subtract
                                  ).then_inc(X["dk"], 1)

            hgrn_decays(0)
            with dve.Fori(0, HEADS - 1) as h:
                hgrn(h, True)
            hgrn(HEADS - 1, False)
            def gain(n):
                return vecs[:, VEC[n]:VEC[n] + 1]
            for x in range(4):
                g = VEC["cq"] + x
                dve.wait_ge(M["chi"], x + 1)
                dve.scalar_tensor_tensor(CLO[:, x, :], Z[:, x, :], vecs[:, g:g + 1], CHI[:, x, :].bitcast(F32),
                                         ALU.mult, ALU.subtract).then_inc(M["c"], 1)
            t = TILE0["qup"]
            dve.wait_ge(M["r"], 1)
            for h in range(HEADS):
                scaled(t, L, tok(QN[:, h, :], L), R2)
                scaled(t + 1, L, tok(QR[:, h, :], L), R2, m=ROPE)
                t += 2
            dve.wait_ge(M["r"], 2)
            dve.wait_ge(rope_in, 16)
            dve.tensor_scalar(KRP[:, :], KR[:, :], gain("kr")[0:ROPE], None, ALU.mult).then_inc(M["kx"], 1)

            def rotated(x, b, other):
                dve.tensor_tensor(tok(SN[:, :], L), ps[0:ROPE, b:b + 2, 0:HALF], tok(TAB[:, 1, :], L), ALU.mult
                                  ).then_inc(other, 1)
                dve.tensor_tensor(x, x, TAB[:, 0, :], ALU.mult)
                dve.drain()
                return dve.tensor_tensor(x, x, SN[:, :], ALU.add)

            def rotated_query(h):
                dve.wait_ge(M["turn"], h + 1)
                dve.drain()
                rotated(QR[:, h, :], 4 + 2 * (h % 2), M["s"]).then_inc(M["rope"], 1)
            for h in range(HEADS):
                scaled(t, L, tok(KN[:, h, :], L), R[1])
                scaled(t + 1, L, tok(V[:, h, :], L), R[1])
                t += 2
                if h == 0:
                    dve.wait_ge(M["kturn"], 1)
                    rotated(KRP[:, :], 6, M["ks"])
                a = RB[h % 2]
                dve.wait_ge(M["rr"], h + 1)
                dve.scalar_tensor_tensor(QN[:, h, :], QN[:, h, :], gain("qn"), a[:, :], ALU.mult, ALU.mult)
                dve.scalar_tensor_tensor(QR[:, h, :], QR[:, h, :], gain("qr")[0:ROPE], a[0:ROPE, :], ALU.mult, ALU.mult
                                         ).then_inc(M["x"], 1)
                if h:
                    rotated_query(h - 1)
            rotated_query(HEADS - 1)
            for h in range(HEADS):
                a = RB[h % 2]
                dve.wait_ge(M["rr"], HEADS + h + 1)
                dve.scalar_tensor_tensor(KN[:, h, :], KN[:, h, :], gain("kn"), a[:, :], ALU.mult, ALU.mult)
                dve.tensor_tensor(KRS[:, h, :], KRP[:, :], a[0:ROPE, :], ALU.mult).then_inc(M["x"], 1)

            def top(x):
                j = x % NCH
                n, nk = (META, META) if j == 0 else (P, META + j * P)
                dve.wait_ge(M["sc"], x + 1)
                o = 1024 * (x % 2)
                dve.tensor_reduce(stat[0:n, j:j + 1], flat[0:n, o:o + nk], AXX, ALU.max)
                dve.drain()
                dve.tensor_scalar(stat[0:n, j:j + 1], stat[0:n, j:j + 1], -QK ** -0.5, None, ALU.mult
                                  ).then_inc(M["max"], 1)

            def share(x):
                j = x % NCH
                n, nk = (META, META) if j == 0 else (P, META + j * P)
                dve.wait_ge(M["exp"], x + 1)
                dve.reciprocal(stat[0:n, 8 + j:9 + j], stat[0:n, 8 + j:9 + j])
                dve.drain()
                dve.tensor_scalar(PP[x % 2][0:n, 0:nk], PP[x % 2][0:n, 0:nk], stat[0:n, 8 + j:9 + j], None,
                                  ALU.mult).then_inc(M["p"], 1)

            def rest(h):
                dve.wait_ge(M["oh"], h + 1)
                uh, ul = UH[:, 4 + h, :].bitcast(F32), UL[:, 4 + h, :]
                dve.tensor_tensor(ul[:, 0:META], flat[:, 3584:3584 + META], uh[:, 0:META], ALU.subtract)
                dve.tensor_tensor(ul[:, META:L], flat[:, 3072:3584], uh[:, META:L], ALU.subtract).then_inc(M["end"], 1)
            top(0)
            for x in range(HEADS * NCH):
                share(x)
                if x + 1 < HEADS * NCH:
                    top(x + 1)
                if x and x % NCH == 0:
                    rest(x // NCH - 1)
            rest(HEADS - 1)
            for e in range(KT):
                t = TILE0["wout"] + e
                dve.wait_ge(tile_done, t + 1)
                dve.tensor_tensor(tok(H[:, e, :], L), psum(t, L), tok(H[:, e, :], L), ALU.add).then_inc(evac[t % 2], 1)
            for e in range(KT):
                lo(1, e, "mlp0")

            def mlp(layer, n, m, split):
                r = R[(m - 1) % 2][:, :]
                dve.wait_ge(r_ready, m)
                dve.tensor_tensor(tok(R2[:, :], n), tok(r, n), tok(r, n), ALU.mult)
                dve.drain()

                def quarter(q, base, last):
                    def square(j):
                        dve.drain()
                        dve.wait_ge(evac[(b + j) % 2], 8 * (q - FQ * layer) + (b + j) // 2 + 1 + FREE)
                        a = tok(RL[j % 2][:, :], n)
                        dve.tensor_tensor(tok(SB[j % 2][:, :], n), a, a, ALU.mult).then_inc(relu2_done, 1)

                    def part(j):
                        dve.wait_ge(hh_done, 8 * q + j + 1)
                        dve.tensor_tensor(tok(HL[:, j, :], n), tok(SB[j % 2][:, :], n), tok(HH[:, j, :], n).bitcast(F32),
                                          ALU.subtract).then_inc(hid_done, 1)
                    square(0)
                    for j in range(8):
                        if j + 1 < 8:
                            square(j + 1)
                        part(j)
                    for e in range(8):
                        dve.wait_ge(tile_done, base + 8 + e + 1)
                        a, he = tok(TD[e % 2][:, :], n), tok(H[:, e, :], n)
                        dve.tensor_tensor(a, psum(b + e, n), tok(R2[:, :], n), ALU.mult
                                          ).then_inc(evac[(b + e) % 2], 1)
                        dve.drain()
                        x = dve.tensor_tensor(he, he, a, ALU.add)
                        if last:
                            x.then_inc(h_final, 1)
                            if split and e:
                                lo(*split(e - 1))
                b = TILE0["mlp%d" % layer]
                with dve.Fori(0, FQ - 1) as i:
                    quarter(i + FQ * layer, i * 16 + b, False)
                quarter(FQ * layer + FQ - 1, b + 16 * (FQ - 1), True)
                if split:
                    lo(*split(7))
            mlp(0, L, 2, None)
            for k in range(KT):
                g = VEC["mem"] + k
                dve.wait_ge(N["mem_hi"], k + 1)
                dve.scalar_tensor_tensor(ML[:, k, :], MEM[:, k, :], vecs[:, g:g + 1], MH[:, k, :].bitcast(F32), ALU.mult,
                                         ALU.subtract).then_inc(N["mem_lo"], 1)
            dve.wait_ge(r_ready, 3)
            for k in range(KT):
                g = VEC["mix1"] + k
                dve.scalar_tensor_tensor(UX[:, k, :], H[:, k, :], vecs[:, g:g + 1], R[0][:, :], ALU.mult, ALU.mult)
            dve.wait_ge(N["mem_r"], 1)

            def pool_lo(g):
                for c in range(2):
                    k = 2 * g + c
                    dve.wait_ge(uh_done, 16 + k + 1)
                    dve.tensor_tensor(UL[:, k, META:L], DD[g % 2][:, c, META:L], UH[:, k, META:L].bitcast(F32),
                                      ALU.subtract).then_inc(u_done, 1)
            for g in range(4):
                cur, a, s_ = UX[:, 2 * g:2 * g + 2, :], 0, 1
                for x in range(g + 1):
                    nxt = (W0, W1)[x % 2]
                    a += s_
                    dve.drain()
                    dve.tensor_tensor(nxt[:, :, a:L], cur[:, :, a:L], cur[:, :, a - s_:L - s_], ALU.add)
                    cur, s_ = nxt, 2 * s_
                dve.drain()
                dve.scalar_tensor_tensor(DD[g % 2][:, :, META:L], cur[:, :, META:L], 1.0 / s_,
                                         UX[:, 2 * g:2 * g + 2, META:L], ALU.mult, ALU.subtract).then_inc(N["dd"], 1)
                for x in (2 * g, 2 * g + 1):
                    t = TILE0["memkv"] + x
                    d = KM[:, x, :] if x < HEADS else VM[:, x - HEADS, :]
                    dve.wait_ge(tile_done, t + 1)
                    dve.tensor_tensor(d, psum(t, NMEM), RM[:, :], ALU.mult).then_inc(evac[t % 2], 1)
                if g:
                    pool_lo(g - 1)
            pool_lo(3)
            for e in range(KT):
                t, g = TILE0["pool"] + e, VEC["pool"] + e
                dve.wait_ge(tile_done, t + 1)
                he = tok(H[:, e, :], SEQ)
                dve.scalar_tensor_tensor(he, psum(t, SEQ), vecs[:, g:g + 1], he, ALU.mult, ALU.add
                                         ).then_inc(evac[t % 2], 1)
                if e % 2:
                    for x in (e - 1, e):
                        lo(3, x, "mlp1")
            mlp(1, SEQ, 4, lambda e: (4, e, "pre_mix"))
            for x in range(2):
                dve.memset(XP[x][:, 0:CONV - 1], 0.0)
            dve.wait_ge(r_ready, 5)
            dve.drain()
            dve.wait_ge(N["ab"], 1)
            dve.tensor_tensor(R2[0:16, META:L], ps[0:16, 7, :], R[0][0:16, META:L], ALU.mult).then_inc(N["ab_row"], 1)
            dve.wait_ge(N["ab_turn"], 1)
            dve.tensor_copy(AB[:, 1:3, :].rearrange("p a (c h) -> p a c h", c=4),
                            ps[:, 6, 0:64].rearrange("p (c a h) -> p a c h", c=4, a=2))
            dve.drain()

            def by_chunk(ap):
                return ap.rearrange("p (c h) -> p c h", c=4)

            def each_chunk(ap):
                return ap.rearrange("p (c h) -> p c h", c=1).to_broadcast([P, 4, 8])
            dve.tensor_tensor(by_chunk(AB[:, 1, :]), by_chunk(AB[:, 1, :]),
                              each_chunk(vecs[:, VEC["dtb"]:VEC["dtb"] + 8]), ALU.add).then_inc(N["ab_x"], 1)
            dve.wait_ge(N["ab_ln"], 1)
            dve.drain()
            dve.scalar_tensor_tensor(AB[:, 3, :], AB[:, 1, :], 0.0, AB[:, 3, :], ALU.max, ALU.add)
            dve.scalar_tensor_tensor(SCAL[:, 1, :], AB[:, 2, :], 0.0, AB[:, 4, :], ALU.min, ALU.subtract)
            dve.drain()
            dve.scalar_tensor_tensor(by_chunk(AB[:, 0, :]), by_chunk(AB[:, 3, :]), -1.0, each_chunk(AB[:, 5, 0:8]),
                                     ALU.mult, ALU.mult).then_inc(N["ab_g"], 1)
            with dve.Fori(0, 6) as i:
                for j in range(4):
                    t = TILE0["gin"] + j
                    dve.wait_ge(tile_done, 4 * i + t + 1)
                    xp, ca = XP[j % 2], CA[j % 2]
                    dve.tensor_tensor(xp[:, 3:3 + SEQ], psum(t, SEQ), R[0][:, META:L], ALU.mult).then_inc(evac[t % 2], 1)
                    dve.drain()
                    if j >= 2:
                        dve.wait_ge(N["conv_silu"], 4 * i + j - 1 + FREE)
                    else:
                        dve.wait_ge(N["conv_silu"], 4 * i + FREE)
                    for n in range(CONV - 1, -1, -1):
                        tap = vecs[:, bass.ds(VEC["conv"] + CONV * (4 * i + j) + n, 1)]
                        if n < CONV - 1:
                            dve.drain()
                        if n == CONV - 1:
                            dve.tensor_scalar(ca[:, :], xp[:, n:n + SEQ], tap, None, ALU.mult)
                        else:
                            last = dve.scalar_tensor_tensor(ca[:, :], xp[:, n:n + SEQ], tap, ca[:, :], ALU.mult, ALU.add)
                    last.then_inc(N["conv"], 1)
            for x in range(12):
                t = TILE0["gin"] + 24 + x
                dve.wait_ge(tile_done, t + 1)
                dve.tensor_tensor(ZQ[:, x, :], psum(t, SEQ), R[0][:, META:L], ALU.mult).then_inc(evac[t % 2], 1)
                for y in (2 * x, 2 * x + 1):
                    if y < 16:
                        dve.wait_ge(N["l2_r"], y + 1)
                        dve.scalar_tensor_tensor(QKV[:, y, :], QKV[:, y, :], P ** -0.5 if y < 8 else 1.0,
                                                 L2R[y % 2][:, META:L], ALU.mult, ALU.mult).then_inc(N["l2_done"], 1)
            dve.tensor_copy(SCAL[:, 0, :], AB[:, 0, :])
            dve.wait_ge(N["ab_exp"], 1)
            dve.tensor_scalar(SCAL[:, 2, :], SCAL[:, 2, :], -1.0, None, ALU.mult)
            dve.tensor_copy(SCAL[:, 3, :], ps[:, 7, 128:160])
            dve.drain()
            dve.tensor_tensor(SCAL[:, 4, :], ps[:, 7, 160:192], SCAL[:, 3, :], ALU.subtract).then_inc(N["ab_x"], 1)

            def top(h):
                dve.wait_ge(N["ma_s"], h + 1)
                dve.tensor_reduce(am_s[h % 2][:, 8:12],
                                  ps[:, 2 * (h % 2):2 * (h % 2) + 2, :].rearrange("p b (c k) -> p (b c) k", c=2), AXX,
                                  ALU.max)
                dve.drain()
                dve.tensor_scalar(am_s[h % 2][:, 0:4], am_s[h % 2][:, 8:12], -P ** -0.5, None, ALU.mult
                                  ).then_inc(N["ma_max"], 1)
            top(0)
            for h in range(HEADS):
                if h + 1 < HEADS:
                    top(h + 1)
                a, b = am_p[h % 2], am_s[h % 2]
                dve.wait_ge(N["ma_exp"], h + 1)
                dve.reciprocal(b[:, 12:16], b[:, 4:8])
                dve.drain()
                dve.tensor_tensor(a[:, :, :], a[:, :, :],
                                  b[:, 12:16].rearrange("p (c k) -> p c k", k=1).to_broadcast([P, 4, NMEM]), ALU.mult
                                  ).then_inc(N["ma_p"], 1)
            dve.wait_ge(N["ab_all"], 1)
            dve.wait_ge(N["ma_end"], HEADS)
            dve.wait_ge(N["mem_vtc"], 1)
            dve.memset(ST8[:, :, :], 0.0)

            def chunk(c):
                def w(name, k, per=1):
                    dve.wait_ge(G[name], count(G, name, c * 2 * per + k))

                def bank(g, b):
                    return ps[:, 4 * g + b, :].rearrange("p (x t) -> p x t", x=4)

                def four(m):
                    return m.rearrange("p (a t) -> p a t", a=1).to_broadcast([P, 4, P])

                def sc(row, g, x):
                    return SC[:, row, 4 * g + x:4 * g + x + 1]
                cols = bass.ds(c * P, P)
                dve.drain()
                dve.tensor_copy(SC[:, :, :], SCAL[:, :, bass.ds(8 * c, 8)])
                dve.drain()
                for g in range(2):
                    w("eg", g + 1)
                    for x in range(4):
                        last = dve.tensor_scalar(G2["T"][g][:, x, :], ps[:, 4 * g + 2, x * P:(x + 1) * P], sc(3, g, x), 0.0,
                                                 ALU.subtract, ALU.min)
                    last.then_inc(G["d"], 1)
                for g in range(2):
                    w("dec", g + 1)
                    w("kk", g + 1)
                    for x in range(4):
                        dve.scalar_tensor_tensor(G2["LT"][g][:, x, :], ps[:, 4 * g, x * P:(x + 1) * P], sc(1, g, x),
                                                 G2["T"][g][:, x, :], ALU.mult, ALU.mult)
                    dve.drain()
                    dve.tensor_tensor(G2["LM"][g][:, :, :], G2["LT"][g][:, :, :], four(level[:, LEVELS - 1, :]), ALU.mult
                                      ).then_inc(G["lm"], 1)
                for g in range(2):
                    w("tr", g + 1)
                    dve.tensor_tensor(G2["PT"][g][:, :, :], bank(g, 1), G2["T"][g][:, :, :], ALU.mult
                                      ).then_inc(G["pq"], 1)
                    dve.drain()
                    w("a", g + 1, LEVELS)
                    dve.tensor_tensor(G2["T"][g][:, :, :], four(ident), bank(g, 0), ALU.subtract).then_inc(G["u"], 1)
                    w("un", g + 1)
                    dve.tensor_tensor(G2["LM"][g][:, :, :], G2["LT"][g][:, :, :], four(level[:, LEVELS - 2, :]), ALU.mult
                                      ).then_inc(G["lm"], 1)
                for l in range(1, LEVELS):
                    dve.drain()
                    if l < LEVELS - 1:
                        for g in range(2):
                            w("a", 2 * l + g + 1, LEVELS)
                            dve.tensor_tensor(G2["LM"][g][:, :, :], G2["LT"][g][:, :, :],
                                              four(level[:, LEVELS - 2 - l, :]), ALU.mult).then_inc(G["lm"], 1)
                    for g in range(2):
                        w("p", 2 * (l - 1) + g + 1, LEVELS - 1)
                        if l < LEVELS - 1:
                            dve.tensor_tensor(G2["T"][g][:, :, :], G2["T"][g][:, :, :], bank(g, 1), ALU.subtract
                                              ).then_inc(G["u"], 1)
                        dve.tensor_tensor(G2["U"][g][:, :, :], G2["U"][g][:, :, :], bank(g, 2), ALU.subtract
                                          ).then_inc(G["ui"], 1)
                for g in range(2):
                    dve.drain()
                    w("ks", g + 1)
                    for x in range(4):
                        last = dve.scalar_tensor_tensor(G2["LM"][g][:, x, :], ps[:, 4 * g, x * P:(x + 1) * P], sc(2, g, x),
                                                        G2["vt"][g][:, x, :], ALU.mult, ALU.add)
                    last.then_inc(G["r"], 1)
                for g in range(2):
                    dve.drain()
                    w("o", g + 1)
                    for x in range(4):
                        last = dve.scalar_tensor_tensor(ST8[:, 4 * g + x, :], ST8[:, 4 * g + x, :], sc(5, g, x),
                                                        ps[:, 4 * g + 3, x * P:(x + 1) * P], ALU.mult, ALU.add)
                    last.then_inc(G["s"], 1)
            with dve.Fori(0, 4) as c:
                chunk(c)
            def head_lo(h):
                dve.wait_ge(uh_done, 40 + h + 1)
                dve.tensor_tensor(UL[:, h, META:L], GT[h % 2][:, META:L], UH[:, h, META:L].bitcast(F32), ALU.subtract
                                  ).then_inc(u_done, 1)
            for h in range(GH):
                dve.wait_ge(N["g_r"], h + 1)
                dve.drain()
                a = GT[h % 2][:, META:L]
                dve.scalar_tensor_tensor(a, QKV[:, h, :], vecs[:, VEC["gdn_out"]:VEC["gdn_out"] + 1],
                                         GR[h % 2][:, META:L], ALU.mult, ALU.mult)
                dve.drain()
                dve.tensor_tensor(a, a, ZQ[:, h, :], ALU.mult).then_inc(N["g_t"], 1)
                if h:
                    head_lo(h - 1)
            head_lo(GH - 1)
            dve.wait_ge(r_ready, 6)
            for e in range(KT):
                g = VEC["post_mix"] + e
                if e >= 2:
                    dve.wait_ge(h_final, 16 + e - 1)
                dve.scalar_tensor_tensor(GT[e % 2][:, META:L], Y[:, e, META:L], vecs[:, g:g + 1], R[1][:, META:L],
                                         ALU.mult, ALU.mult).then_inc(N["y_t"], 1)
                if e >= 2:
                    lo(6, e - 2, "pre_ffn")
            lo(6, 6, "pre_ffn")
            lo(6, 7, "pre_ffn")
            dve.wait_ge(r_ready, 7)

            def f_lo(a, j):
                dve.wait_ge(N["f_hh"], 11 * a + j + 1)
                dve.tensor_tensor(FL[:, j, META:L], GC[j % 2][:, META:L], FH[:, j, META:L].bitcast(F32), ALU.subtract
                                  ).then_inc(N["f_hid"], 1)
            for a in range(2):
                b = TILE0["ffn"] + 30 * a
                for j in range(11):
                    if j >= 2:
                        dve.wait_ge(N["f_silu"], 11 * a + j - 1)
                    dve.wait_ge(tile_done, b + 2 * j + 1)
                    dve.tensor_tensor(GA[j % 2][:, META:L], psum(b, SEQ), R[0][:, META:L], ALU.mult
                                      ).then_inc(evac[b % 2], 1)
                    if j:
                        f_lo(a, j - 1)
                    dve.wait_ge(tile_done, b + 2 * j + 2)
                    dve.wait_ge(N["f_silu"], 11 * a + j + 1)
                    dve.drain()
                    dve.tensor_tensor(GC[j % 2][:, META:L], psum(b + 1, SEQ), GS[j % 2][:, META:L], ALU.mult
                                      ).then_inc(evac[(b + 1) % 2], 1)
                f_lo(a, 10)
                for e in range(KT):
                    t = b + 22 + e
                    dve.wait_ge(tile_done, t + 1)
                    if a == 0:
                        dve.tensor_tensor(FO[:, e, META:L], psum(t, SEQ), R[0][:, META:L], ALU.mult
                                          ).then_inc(evac[t % 2], 1)
                    else:
                        x = GA[e % 2][:, META:L]
                        dve.drain()
                        dve.tensor_tensor(x, psum(t, SEQ), R[0][:, META:L], ALU.mult).then_inc(evac[t % 2], 1)
                        dve.drain()
                        dve.tensor_tensor(FO[:, e, META:L], FO[:, e, META:L], x, ALU.add).then_inc(h_final, 1)
            dve.wait_ge(r_ready, 8)
            for e in range(KT):
                g = VEC["post_ffn"] + e
                x, he = GA[e % 2][:, META:L], H[:, e, META:L]
                dve.drain()
                dve.scalar_tensor_tensor(x, FO[:, e, META:L], vecs[:, g:g + 1], R[1][:, META:L], ALU.mult, ALU.mult)
                dve.drain()
                dve.tensor_tensor(he, he, x, ALU.add).then_inc(N["y_out"], 1)


def constants():
    s = np.arange(P)[:, None]
    t = np.arange(P)[None, :]
    masks = []
    for l in range(1, LEVELS + 1):
        m = CH >> l
        masks.append((s // (2 * m) == t // (2 * m)) & (s % (2 * m) < m) & (t % (2 * m) >= m))
    half = ROPE // 2
    turn = np.where(t == s - half, -1.0, 0.0) * (s < ROPE) + np.where(t == s + half, 1.0, 0.0) * (t < ROPE)
    early = np.where(t < 64, BIG, 0.0)
    masks += [s == t, s <= t, s >= 0, turn, early]
    return np.ascontiguousarray(np.stack([np.broadcast_to(x, (P, P)) for x in masks], 1).astype(np.float32))


def rope_table():
    half = ROPE // 2
    inv = (np.float32(10000.0) ** (-np.arange(half, dtype=np.float32) / np.float32(half))).astype(np.float32)
    ang = np.arange(L, dtype=np.float32)[None, :] * inv[:, None]
    c, s = np.cos(ang), np.sin(ang)
    return np.ascontiguousarray(np.stack([np.concatenate([c, c]), np.concatenate([s, s])], 1).astype(np.float32))


def pack(i):
    blocks = []

    def put(w, cols, kt=None):
        w = np.asarray(w)
        for c in cols:
            for k in range(w.shape[0] // P) if kt is None else kt:
                b = np.zeros((P, P), np.float32)
                part = w[k * P:(k + 1) * P, c:c + P]
                b[:, 0:part.shape[1]] = part
                blocks.append(b)

    def halves(w, c, width):
        w = np.asarray(w)
        n = P // width
        for k in range(0, w.shape[0] // P, n):
            b = np.zeros((P, P), np.float32)
            for j in range(min(n, w.shape[0] // P - k)):
                b[:, j * width:(j + 1) * width] = w[(k + j) * P:(k + j + 1) * P, c:c + width]
            blocks.append(b)

    win = i["w_in"][0]
    put(win, [2048 + P * j for j in range(4)] + [P * j for j in range(16)])
    halves(win, 2560, ROPE)
    for h in range(HEADS):
        put(i["w_q_up"][0], [h * QK])
        halves(i["w_q_up"][0], h * QK + NOPE, ROPE)
    put(i["w_kv_up"][0], [P * j for j in range(8)])
    put(i["w_out"][0], [P * j for j in range(8)])

    def mlp(layer):
        for q in range(FQ):
            put(i["w_mlp_up"][layer], [P * (8 * q + j) for j in range(8)])
            put(i["w_mlp_down"][layer], [P * e for e in range(8)], range(8 * q, 8 * q + 8))
    mlp(0)
    put(i["w_mem_kv_2"][0], [P * j for j in range(8)])
    for g in range(4):
        put(i["pool_w"][0][g], [0, P])
    mlp(1)
    gin = i["gdn_w_in_2"][0]
    put(gin, [P * j for j in range(32)] + [4112 + P * j for j in range(4)])
    put(i["w_out_2"][0], [P * j for j in range(8)])
    for a in range(2):
        for j in range(11):
            put(i["w_ffn_in_2"][0], [P * (11 * a + j), P * (FF2 + 11 * a + j)])
        put(i["w_ffn_out_2"][0], [P * e for e in range(8)], range(11 * a, 11 * a + 11))
    assert len(blocks) == NBLOCKS, (len(blocks), NBLOCKS)
    w = np.stack(blocks).reshape(NSLOTS, SLOT, P, P).transpose(0, 2, 1, 3)
    return np.ascontiguousarray(w)


def gate_weights(i):
    w = np.asarray(i["gdn_w_in_2"][0])[:, 4096:4112]
    return np.ascontiguousarray(w.reshape(KT, P, 16).transpose(1, 0, 2))


def vectors(i):
    v = np.zeros((P, NVEC), np.float32)

    def put(name, a):
        a = np.asarray(a)
        a = a.reshape(-1, P).T
        v[:, VEC[name]:VEC[name] + a.shape[1]] = a
    put("mix0", i["mix_norm"][0]); put("mix1", i["mix_norm"][1])
    put("mlp0", i["mlp_norm"][0]); put("mlp1", i["mlp_norm"][1])
    put("hg_out", i["hgrn_out_norm"][0]); put("cq", i["mla_q_a_norm"][0]); put("ckv", i["mla_kv_a_norm"][0])
    put("qn", i["q_norm"][0][:NOPE]); put("kn", i["k_norm"][0][:NOPE])
    v[:ROPE, VEC["qr"]] = i["q_norm"][0][NOPE:]
    v[:ROPE, VEC["kr"]] = i["k_norm"][0][NOPE:]
    put("pool", i["pool_scale"][0]); put("mem", i["mem_norm_2"]); put("pre_mix", i["norm_pre_mix_2"][0])
    put("post_mix", i["norm_post_mix_2"][0]); put("pre_ffn", i["norm_pre_ffn_2"][0])
    put("post_ffn", i["norm_post_ffn_2"][0]); put("gdn_out", i["gdn_out_norm_2"][0])
    v[:, VEC["alog"]:VEC["alog"] + 8] = i["gdn_a_log_2"][0][None]
    v[:, VEC["dtb"]:VEC["dtb"] + 8] = i["gdn_dt_bias_2"][0][None]
    c = np.asarray(i["gdn_conv_2"][0]).reshape(CONV, 24, P).transpose(2, 1, 0)
    v[:, VEC["conv"]:VEC["conv"] + 24 * CONV] = c.reshape(P, -1)
    return v


def kernel(**inputs):
    import concourse.bacc as bacc
    import concourse.bass_utils as bass_utils

    i = {n: np.asarray(a) for n, a in inputs.items()}
    x = np.concatenate([i["meta_tokens"], i["x"][0]], 0)
    arrays = {
        "xT": np.ascontiguousarray(x.T.reshape(KT, P, L).transpose(1, 0, 2)),
        "memT": np.ascontiguousarray(i["mem_2"][0].T.reshape(KT, P, NMEM).transpose(1, 0, 2)),
        "W": pack(i), "vecs": vectors(i), "masks": constants(), "rope": rope_table(), "gates": gate_weights(i),
    }
    nc = bacc.Bacc("TRN2", target_bir_lowering=False, num_devices=1)
    args = [nc.dram_tensor(n, a.shape, F32, kind="ExternalInput").ap() for n, a in arrays.items()]
    out = nc.dram_tensor("out", (P, KT, SEQ), F32, kind="ExternalOutput").ap()
    build(nc, *args, out)
    r = bass_utils.run_bass_kernel_spmd(nc, [arrays], core_ids=[0])
    y = np.asarray(r.results[0]["out"])
    return np.ascontiguousarray(y.transpose(1, 0, 2).reshape(D, SEQ).T)[None]
```
